# Optimizing a Trainium2 kernel written in Bass

```python
import jax, jax.numpy as jnp
from jax import lax
import numpy as np
import math

D_MODEL = 1024
BATCH = 1
SEQ = 512
DEPTH = 1

CTX_LEN = 256
GRID_W = 64
EPS = 1e-6

POOL_WINDOWS = (2, 4, 8, 16)
POOL_WIDTH = D_MODEL // 2
POOL_GROUP = POOL_WIDTH // len(POOL_WINDOWS)

RET_HEADS = 4
RET_DK = 128
RET_DV = 256
RET_CHUNK = 128
ROPE_BASE = 10000.0
QK_WIDTH = RET_HEADS * RET_DK
V_WIDTH = RET_HEADS * RET_DV

OFF_POOL = 0
OFF_Q = OFF_POOL + POOL_WIDTH
OFF_K = OFF_Q + QK_WIDTH
OFF_V = OFF_K + QK_WIDTH
OFF_G = OFF_V + V_WIDTH
OFF_MERGE = OFF_G + V_WIDTH
IN_WIDTH = OFF_MERGE + 2 * D_MODEL

PEER_HEADS = 8
PEER_NKEYS = 128
PEER_EXPERTS = PEER_NKEYS * PEER_NKEYS
PEER_TOPK = 16
PEER_DQ = 256
PEER_BLOCK = 128


def rmsnorm(x, g):
    xf = x.astype(jnp.float32)
    y = xf * lax.rsqrt(jnp.mean(xf * xf, axis=-1, keepdims=True) + EPS)
    return (y * g.astype(jnp.float32)).astype(x.dtype)

def modulate(h, shift, scale):
    return h * (1.0 + scale) + shift

def heads(a, d):
    b, l, _ = a.shape
    return a.reshape(b, l, -1, d).transpose(0, 2, 1, 3)

def axial_rope(a, row, col):
    quarter = a.shape[-1] // 4
    inv = ROPE_BASE ** (-jnp.arange(quarter, dtype=jnp.float32) / quarter)
    ang = jnp.concatenate([row[:, None] * inv, col[:, None] * inv], axis=-1)
    cos, sin = jnp.cos(ang), jnp.sin(ang)
    a1, a2 = jnp.split(a, 2, axis=-1)
    return jnp.concatenate([a1 * cos - a2 * sin, a1 * sin + a2 * cos], axis=-1).astype(a.dtype)

def multiscale_pool(p, pool_w, pool_scale):
    L = p.shape[1]
    pf = p.astype(jnp.float32)
    cs = jnp.pad(jnp.cumsum(pf, axis=1), ((0, 0), (1, 0), (0, 0)))
    t = jnp.arange(L)
    groups = []
    for gi, w in enumerate(POOL_WINDOWS):
        lo = jnp.clip(t - w // 2, 0, L)
        hi = jnp.clip(t + w - w // 2, 0, L)
        sl = slice(gi * POOL_GROUP, (gi + 1) * POOL_GROUP)
        win_sum = cs[:, hi, sl] - cs[:, lo, sl]
        cnt = (hi - lo).astype(jnp.float32)[None, :, None]
        groups.append(win_sum / cnt - pf[:, :, sl])
    d = jnp.stack(groups, axis=2).astype(p.dtype)
    mixed = jnp.einsum('blgc,gcd->blgd', d, pool_w).reshape(p.shape)
    return mixed * pool_scale

def retention_scan(q, k, v, log_gamma, s0, strict):
    b, h, L, _ = q.shape
    dv = v.shape[-1]
    C = RET_CHUNK
    n = L // C

    def chunks(a):
        return a.reshape(b, h, n, C, a.shape[-1]).transpose(2, 0, 1, 3, 4)

    idx = jnp.arange(C, dtype=jnp.float32)
    rel = idx[:, None] - idx[None, :]
    mask = (rel > 0) if strict else (rel >= 0)
    lg = log_gamma[:, None, None]
    intra = jnp.where(mask, jnp.exp(lg * jnp.where(mask, rel, 0.0)), 0.0)
    q_dec = jnp.exp(log_gamma[:, None] * (idx + 1.0))[..., None]
    k_dec = jnp.exp(log_gamma[:, None] * (C - 1.0 - idx))[..., None]
    blk_dec = jnp.exp(log_gamma * C)[:, None, None]

    def step(s, qkv):
        qi, ki, vi = qkv
        scores = jnp.einsum('bhnd,bhmd->bhnm', qi, ki) * intra
        y = (jnp.einsum('bhnm,bhme->bhne', scores, vi)
             + jnp.einsum('bhnd,bhde->bhne', qi * q_dec, s))
        s = s * blk_dec + jnp.einsum('bhmd,bhme->bhde', ki * k_dec, vi)
        return s, y

    _, ys = lax.scan(step, s0, (chunks(q), chunks(k), chunks(v)))
    return ys.transpose(1, 2, 0, 3, 4).reshape(b, h, L, dv)

def context_states(kc, vc, lg):
    Lc = kc.shape[2]
    m = jnp.arange(Lc, dtype=jnp.float32)
    w_f = jnp.exp(lg[0][:, None] * (Lc - 1.0 - m))
    w_b = jnp.exp(lg[1][:, None] * m)
    kf = kc.astype(jnp.float32)
    vf = vc.astype(jnp.float32)
    s_f = jnp.einsum('hm,bhmd,bhme->bhde', w_f, kf, vf)
    s_b = jnp.einsum('hm,bhmd,bhme->bhde', w_b, kf, vf)
    return s_f, s_b

def bidir_retention(q, k, v, lg, s_f, s_b):
    y_f = retention_scan(q, k, v, lg[0], s_f, False)
    y_b = retention_scan(jnp.flip(q, 2), jnp.flip(k, 2), jnp.flip(v, 2), lg[1], s_b, True)
    return y_f + jnp.flip(y_b, 2)

def retention_out(y, gate, norm_g, w_o):
    b, h, L, dv = y.shape
    yf = y.astype(jnp.float32)
    mu = jnp.mean(yf, axis=-1, keepdims=True)
    var = jnp.mean(jnp.square(yf - mu), axis=-1, keepdims=True)
    yn = ((yf - mu) * lax.rsqrt(var + EPS)).transpose(0, 2, 1, 3).reshape(b, L, h * dv)
    yn = (yn * norm_g.astype(jnp.float32)).astype(gate.dtype)
    return (yn * jax.nn.silu(gate)) @ w_o

def mix_tokens(proj, y_ret, lp):
    pool = multiscale_pool(proj[..., OFF_POOL:OFF_Q], lp['pool_w'], lp['pool_scale']) @ lp['pool_out']
    ret = retention_out(y_ret, proj[..., OFF_G:OFF_MERGE], lp['ret_norm_g'], lp['ret_out'])
    g_pool, g_ret = jnp.split(proj[..., OFF_MERGE:], 2, axis=-1)
    merged = jax.nn.sigmoid(g_pool) * pool + jax.nn.sigmoid(g_ret) * ret
    return merged @ lp['w_out']

def peer_ffn(h, wq, keys, u, v):
    b, L, d = h.shape
    blocks = h.reshape(-1, PEER_BLOCK, d)

    def one_block(hb):
        t = hb.shape[0]
        q = (hb @ wq).reshape(t, PEER_HEADS, 2, PEER_DQ // 2)
        s = jnp.einsum('thpd,hpkd->thpk', q, keys).astype(jnp.float32)
        s1, i1 = lax.top_k(s[:, :, 0], PEER_TOPK)
        s2, i2 = lax.top_k(s[:, :, 1], PEER_TOPK)
        cand = (s1[..., :, None] + s2[..., None, :]).reshape(t, PEER_HEADS, PEER_TOPK * PEER_TOPK)
        cidx = (i1[..., :, None] * PEER_NKEYS + i2[..., None, :]).reshape(t, PEER_HEADS, PEER_TOPK * PEER_TOPK)
        best, pos = lax.top_k(cand, PEER_TOPK)
        eidx = jnp.take_along_axis(cidx, pos, axis=-1)
        g = jax.nn.softmax(best, axis=-1)
        act = jax.nn.gelu(jnp.einsum('thkd,td->thk', u[eidx], hb).astype(jnp.float32), approximate=False)
        return jnp.einsum('thk,thkd->td', (g * act).astype(hb.dtype), v[eidx])

    return lax.map(one_block, blocks).reshape(b, L, d)

def trunk_layer(x, ctx, c, c_ctx, lp, update_ctx):
    b, L, d = x.shape
    mod = jax.nn.silu(c) @ lp['ada_w'] + lp['ada_b']
    mod_c = jax.nn.silu(c_ctx) @ lp['ada_w'] + lp['ada_b']
    sh1, sc1, g1, sh2, sc2, g2 = jnp.split(mod[:, None, :], 6, axis=-1)
    csh1, csc1, cg1, csh2, csc2, cg2 = jnp.split(mod_c, 6, axis=-1)
    lg = jax.nn.log_sigmoid(lp['ret_decay'].astype(jnp.float32))
    k_scale = RET_DK ** -0.5

    rows = L // GRID_W
    row = jnp.repeat(jnp.arange(rows, dtype=jnp.float32), GRID_W)
    col = jnp.tile(jnp.arange(GRID_W, dtype=jnp.float32), rows)

    hc = modulate(rmsnorm(ctx, lp['norm_mix_g']), csh1, csc1)
    if update_ctx:
        projc = hc @ lp['w_in']
        kv_c = projc[..., OFF_K:OFF_G]
    else:
        kv_c = hc @ lp['w_in'][:, OFF_K:OFF_G]
    kc = heads(kv_c[..., :QK_WIDTH], RET_DK) * k_scale
    vc = heads(kv_c[..., QK_WIDTH:], RET_DV)
    s_f, s_b = context_states(kc, vc, lg)

    h = modulate(rmsnorm(x, lp['norm_mix_g']), sh1, sc1)
    proj = h @ lp['w_in']
    q = axial_rope(heads(proj[..., OFF_Q:OFF_K], RET_DK), row, col)
    k = axial_rope(heads(proj[..., OFF_K:OFF_V], RET_DK), row, col) * k_scale
    v = heads(proj[..., OFF_V:OFF_G], RET_DV)
    y = bidir_retention(q, k, v, lg, s_f, s_b)
    x = x + g1 * mix_tokens(proj, y, lp)

    hf = modulate(rmsnorm(x, lp['norm_ffn_g']), sh2, sc2)
    x = x + g2 * peer_ffn(hf, lp['peer_wq'], lp['peer_keys'], lp['peer_u'], lp['peer_v'])

    if update_ctx:
        qc = heads(projc[..., OFF_Q:OFF_K], RET_DK)
        zero = jnp.zeros_like(s_f)
        yc = bidir_retention(qc, kc, vc, lg, zero, zero)
        ctx = ctx + cg1 * mix_tokens(projc, yc, lp)
        hcf = modulate(rmsnorm(ctx, lp['norm_ffn_g']), csh2, csc2)
        ctx = ctx + cg2 * peer_ffn(hcf, lp['peer_wq'], lp['peer_keys'], lp['peer_u'], lp['peer_v'])
    return x, ctx

def first_inputs(seed: int = 0) -> dict:
    key = jax.random.key(seed)
    ks = jax.random.split(key, 24)
    f32 = jnp.float32
    D = D_MODEL

    def nrm(k, shape, s):
        return jax.random.normal(k, shape, f32) * s

    base_logit = jnp.log(2.0 ** (5.0 + jnp.arange(RET_HEADS, dtype=f32)) - 1.0)
    return {
        'x': nrm(ks[0], (BATCH, SEQ, D), 1.0),
        'c': nrm(ks[1], (BATCH, D), 1.0),
        'ctx': nrm(ks[2], (BATCH, CTX_LEN, D), 1.0),
        'c_ctx': nrm(ks[3], (D,), 1.0),
        'ada_w': nrm(ks[4], (DEPTH, D, 6 * D), 0.5 * D ** -0.5),
        'ada_b': nrm(ks[5], (DEPTH, 6 * D), 0.02),
        'norm_mix_g': 1.0 + nrm(ks[6], (DEPTH, D), 0.02),
        'norm_ffn_g': 1.0 + nrm(ks[7], (DEPTH, D), 0.02),
        'w_in': nrm(ks[8], (DEPTH, D, IN_WIDTH), D ** -0.5),
        'pool_w': nrm(ks[9], (DEPTH, len(POOL_WINDOWS), POOL_GROUP, POOL_GROUP), POOL_GROUP ** -0.5),
        'pool_scale': 1.0 + nrm(ks[10], (DEPTH, POOL_WIDTH), 0.1),
        'pool_out': nrm(ks[11], (DEPTH, POOL_WIDTH, D), POOL_WIDTH ** -0.5),
        'ret_decay': base_logit[None, None, :] + nrm(ks[12], (DEPTH, 2, RET_HEADS), 0.1),
        'ret_norm_g': 1.0 + nrm(ks[13], (DEPTH, V_WIDTH), 0.02),
        'ret_out': nrm(ks[14], (DEPTH, V_WIDTH, D), V_WIDTH ** -0.5),
        'w_out': nrm(ks[15], (DEPTH, D, D), D ** -0.5),
        'peer_wq': nrm(ks[16], (DEPTH, D, PEER_HEADS * PEER_DQ), D ** -0.5),
        'peer_keys': nrm(ks[17], (DEPTH, PEER_HEADS, 2, PEER_NKEYS, PEER_DQ // 2), (PEER_DQ // 2) ** -0.5),
        'peer_u': nrm(ks[18], (DEPTH, PEER_EXPERTS, D), D ** -0.5),
        'peer_v': nrm(ks[19], (DEPTH, PEER_EXPERTS, D), 0.5),
        'final_g': 1.0 + nrm(ks[20], (D,), 0.02),
    }

def first_block(x, c, ctx, c_ctx, ada_w, ada_b, norm_mix_g, norm_ffn_g, w_in, pool_w,
              pool_scale, pool_out, ret_decay, ret_norm_g, ret_out, w_out, peer_wq,
              peer_keys, peer_u, peer_v, final_g):
    for layer in range(DEPTH):
        lp = {
            'ada_w': ada_w[layer], 'ada_b': ada_b[layer],
            'norm_mix_g': norm_mix_g[layer], 'norm_ffn_g': norm_ffn_g[layer],
            'w_in': w_in[layer], 'pool_w': pool_w[layer], 'pool_scale': pool_scale[layer],
            'pool_out': pool_out[layer], 'ret_decay': ret_decay[layer],
            'ret_norm_g': ret_norm_g[layer], 'ret_out': ret_out[layer], 'w_out': w_out[layer],
            'peer_wq': peer_wq[layer], 'peer_keys': peer_keys[layer],
            'peer_u': peer_u[layer], 'peer_v': peer_v[layer],
        }
        x, ctx = trunk_layer(x, ctx, c, c_ctx, lp, layer + 1 < DEPTH)
    return rmsnorm(x, final_g)


MIX_WIDTH = D_MODEL
HG_WIDTH = MIX_WIDTH // 2
HG_HEADS = 4
HG_DK = HG_WIDTH // HG_HEADS
HG_CHUNK = 64
S5_WIDTH = MIX_WIDTH - HG_WIDTH
S5_GROUP = 16
S5_GROUPS = S5_WIDTH // S5_GROUP
S5_STATE = 64
IN_WIDTH_2 = 4 * HG_WIDTH + S5_WIDTH
PEER_EXPERTS_2 = PEER_NKEYS * PEER_NKEYS
PEER_QDIM = 256
PEER_HALF = PEER_QDIM // 2
PEER_TOKEN_BLOCK = 128


def _rmsnorm(x, w):
    xf = x.astype(jnp.float32)
    y = xf * lax.rsqrt(jnp.mean(xf * xf, axis=-1, keepdims=True) + EPS)
    return (y * w.astype(jnp.float32)).astype(x.dtype)

def _hgrn2(q, f_logit, i, g, lb, gn_w):
    bsz, seq, _ = q.shape
    f32 = jnp.float32
    f = lb + (1.0 - lb) * jax.nn.sigmoid(f_logit.astype(f32))
    log_f = jnp.log(f)
    k = 1.0 - f
    qs = jax.nn.silu(q.astype(f32)) * (HG_DK ** -0.5)
    v = i.astype(f32)
    n_chunks = seq // HG_CHUNK

    def to_chunks(t):
        return t.reshape(bsz, n_chunks, HG_CHUNK, HG_HEADS, HG_DK).transpose(1, 0, 3, 2, 4)

    causal = jnp.tril(jnp.ones((HG_CHUNK, HG_CHUNK), dtype=bool))[:, :, None]

    def step(state, inp):
        qc, kc, vc, lc = inp
        bcum = jnp.cumsum(lc, axis=2)
        o_inter = jnp.einsum('bhtk,bhkv->bhtv', qc * jnp.exp(bcum), state)
        diff = bcum[:, :, :, None, :] - bcum[:, :, None, :, :]
        decay = jnp.exp(jnp.where(causal, diff, -jnp.inf))
        scores = jnp.einsum('bhtk,bhsk,bhtsk->bhts', qc, kc, decay)
        o_intra = jnp.einsum('bhts,bhsv->bhtv', scores, vc)
        b_last = bcum[:, :, -1:, :]
        new_state = (jnp.exp(b_last[:, :, 0, :])[..., None] * state
                     + jnp.einsum('bhsk,bhsv->bhkv', kc * jnp.exp(b_last - bcum), vc))
        return new_state, o_inter + o_intra

    s0 = jnp.zeros((bsz, HG_HEADS, HG_DK, HG_DK), f32)
    _, o = lax.scan(step, s0, (to_chunks(qs), to_chunks(k), to_chunks(v), to_chunks(log_f)))
    o = o.transpose(1, 0, 3, 2, 4).reshape(bsz, seq, HG_HEADS, HG_DK)
    gate = jax.nn.silu(g.astype(f32)).reshape(bsz, seq, HG_HEADS, HG_DK)
    o = _rmsnorm(o, gn_w) * gate
    return o.reshape(bsz, seq, HG_WIDTH)

def _s5(u, a_re, a_im, log_dt, b_re, b_im, c_re, c_im, d_skip, w_glu, b_glu):
    bsz, seq, _ = u.shape
    f32 = jnp.float32
    uf = u.astype(f32).reshape(bsz, seq, S5_GROUPS, S5_GROUP)
    ar = a_re.astype(f32)
    ai = a_im.astype(f32)
    dt = jnp.exp(log_dt.astype(f32))[:, None]
    mag = jnp.exp(ar * dt)
    abar_re = mag * jnp.cos(ai * dt)
    abar_im = mag * jnp.sin(ai * dt)
    den = ar * ar + ai * ai
    nr = abar_re - 1.0
    ni = abar_im
    coef_re = ((nr * ar + ni * ai) / den)[..., None]
    coef_im = ((ni * ar - nr * ai) / den)[..., None]
    br = b_re.astype(f32)
    bi = b_im.astype(f32)
    bb_re = coef_re * br - coef_im * bi
    bb_im = coef_re * bi + coef_im * br
    bu_re = jnp.einsum('bsgh,gph->bsgp', uf, bb_re)
    bu_im = jnp.einsum('bsgh,gph->bsgp', uf, bb_im)
    a_re_t = jnp.broadcast_to(abar_re, bu_re.shape)
    a_im_t = jnp.broadcast_to(abar_im, bu_im.shape)

    def combine(e1, e2):
        a1r, a1i, x1r, x1i = e1
        a2r, a2i, x2r, x2i = e2
        return (a2r * a1r - a2i * a1i,
                a2r * a1i + a2i * a1r,
                a2r * x1r - a2i * x1i + x2r,
                a2r * x1i + a2i * x1r + x2i)

    _, _, xr, xi = lax.associative_scan(combine, (a_re_t, a_im_t, bu_re, bu_im), axis=1)
    y = (jnp.einsum('bsgp,ghp->bsgh', xr, c_re.astype(f32))
         - jnp.einsum('bsgp,ghp->bsgh', xi, c_im.astype(f32)))
    y = y.reshape(bsz, seq, S5_WIDTH) + d_skip.astype(f32) * uf.reshape(bsz, seq, S5_WIDTH)
    y = jax.nn.gelu(y, approximate=False)
    y = y * jax.nn.sigmoid(y @ w_glu.astype(f32) + b_glu.astype(f32))
    return y.astype(u.dtype)

def _peer(h, w_q, keys1, keys2, u_tab, v_tab):
    bsz, seq, d = h.shape
    tb = PEER_TOKEN_BLOCK
    blocks = h.reshape(-1, tb, d)
    kk = PEER_TOPK * PEER_TOPK

    def block(hb):
        qh = (hb @ w_q).reshape(tb, PEER_HEADS, 2, PEER_HALF)
        s1 = jnp.einsum('thd,nd->thn', qh[:, :, 0], keys1)
        s2 = jnp.einsum('thd,nd->thn', qh[:, :, 1], keys2)
        v1, i1 = lax.top_k(s1, PEER_TOPK)
        v2, i2 = lax.top_k(s2, PEER_TOPK)
        cand = (v1[..., :, None] + v2[..., None, :]).reshape(tb, PEER_HEADS, kk)
        cidx = (i1[..., :, None] * PEER_NKEYS + i2[..., None, :]).reshape(tb, PEER_HEADS, kk)
        best, pos = lax.top_k(cand, PEER_TOPK)
        eidx = jnp.take_along_axis(cidx, pos, axis=-1)
        gates = jax.nn.softmax(best.astype(jnp.float32), axis=-1).astype(hb.dtype)
        act = jax.nn.gelu(jnp.einsum('td,thkd->thk', hb, u_tab[eidx]), approximate=False)
        return jnp.einsum('thk,thkd->td', gates * act, v_tab[eidx])

    return lax.map(block, blocks).reshape(bsz, seq, d)

def second_inputs(seed: int = 0) -> dict:
    key = jax.random.key(seed)
    ks = jax.random.split(key, 26)
    f32 = jnp.float32

    def nrm(k, shape, std):
        return std * jax.random.normal(k, shape, f32)

    L = DEPTH
    D = D_MODEL
    G = S5_GROUPS
    P = S5_STATE
    return {
        'x': nrm(ks[0], (BATCH, SEQ, D), 1.0),
        'c': nrm(ks[1], (BATCH, D), 1.0),
        'ada_w': nrm(ks[2], (L, D, 6 * D), 0.5 * D ** -0.5),
        'ada_b': nrm(ks[3], (L, 6 * D), 0.01),
        'norm_mix_w': 1.0 + nrm(ks[4], (L, D), 0.02),
        'norm_ffn_w': 1.0 + nrm(ks[5], (L, D), 0.02),
        'w_in': nrm(ks[6], (L, D, IN_WIDTH_2), D ** -0.5),
        'w_out': nrm(ks[7], (L, MIX_WIDTH, D), MIX_WIDTH ** -0.5),
        'hg_lower_bounds': nrm(ks[8], (L + 1, HG_WIDTH), 0.1),
        'hg_gnorm_w': 1.0 + nrm(ks[9], (L, HG_DK), 0.02),
        's5_a_re': -0.5 + nrm(ks[10], (L, G, P), 0.01),
        's5_a_im': math.pi * jnp.arange(P, dtype=f32) + nrm(ks[11], (L, G, P), 0.01),
        's5_log_dt': jax.random.uniform(ks[12], (L, G), f32, math.log(1e-3), math.log(1e-1)),
        's5_b_re': nrm(ks[13], (L, G, P, S5_GROUP), (2 * S5_GROUP) ** -0.5),
        's5_b_im': nrm(ks[14], (L, G, P, S5_GROUP), (2 * S5_GROUP) ** -0.5),
        's5_c_re': nrm(ks[15], (L, G, S5_GROUP, P), 0.25),
        's5_c_im': nrm(ks[16], (L, G, S5_GROUP, P), 0.25),
        's5_d': nrm(ks[17], (L, S5_WIDTH), 0.5),
        's5_glu_w': nrm(ks[18], (L, S5_WIDTH, S5_WIDTH), S5_WIDTH ** -0.5),
        's5_glu_b': nrm(ks[19], (L, S5_WIDTH), 0.01),
        'peer_wq': nrm(ks[20], (L, D, PEER_HEADS * PEER_QDIM), D ** -0.5),
        'peer_keys1': nrm(ks[21], (L, PEER_NKEYS, PEER_HALF), PEER_HALF ** -0.5),
        'peer_keys2': nrm(ks[22], (L, PEER_NKEYS, PEER_HALF), PEER_HALF ** -0.5),
        'peer_u': nrm(ks[23], (L, PEER_EXPERTS_2, D), D ** -0.5),
        'peer_v': nrm(ks[24], (L, PEER_EXPERTS_2, D), PEER_HEADS ** -0.5),
        'final_norm_w': 1.0 + nrm(ks[25], (D,), 0.02),
    }

def second_block(x, c, ada_w, ada_b, norm_mix_w, norm_ffn_w, w_in, w_out, hg_lower_bounds,
              hg_gnorm_w, s5_a_re, s5_a_im, s5_log_dt, s5_b_re, s5_b_im, s5_c_re, s5_c_im,
              s5_d, s5_glu_w, s5_glu_b, peer_wq, peer_keys1, peer_keys2, peer_u, peer_v,
              final_norm_w):
    cond = jax.nn.silu(c)
    lb_all = jnp.cumsum(jax.nn.softmax(hg_lower_bounds.astype(jnp.float32), axis=0), axis=0)
    for l in range(DEPTH):
        mod = (cond @ ada_w[l] + ada_b[l])[:, None, :]
        sh1, sc1, gt1, sh2, sc2, gt2 = jnp.split(mod, 6, axis=-1)
        h = _rmsnorm(x, norm_mix_w[l]) * (1.0 + sc1) + sh1
        proj = h @ w_in[l]
        q, f_logit, i, g, u = jnp.split(
            proj, [HG_WIDTH, 2 * HG_WIDTH, 3 * HG_WIDTH, 4 * HG_WIDTH], axis=-1)
        o_hg = _hgrn2(q, f_logit, i, g, lb_all[l], hg_gnorm_w[l]).astype(x.dtype)
        o_s5 = _s5(u, s5_a_re[l], s5_a_im[l], s5_log_dt[l], s5_b_re[l], s5_b_im[l],
                   s5_c_re[l], s5_c_im[l], s5_d[l], s5_glu_w[l], s5_glu_b[l])
        mixed = jnp.concatenate([o_hg, o_s5], axis=-1) @ w_out[l]
        x = x + gt1 * mixed
        h2 = _rmsnorm(x, norm_ffn_w[l]) * (1.0 + sc2) + sh2
        x = x + gt2 * _peer(h2, peer_wq[l], peer_keys1[l], peer_keys2[l], peer_u[l], peer_v[l])
    return _rmsnorm(x, final_norm_w)


def setup_inputs(seed=0):
    out = dict(first_inputs(seed))
    for name, value in second_inputs(seed + 1).items():
        if name != "x":
            out[name + "_2"] = value
    return out


def reference(
    x, c, ctx, c_ctx, ada_w, ada_b, norm_mix_g, norm_ffn_g, w_in, pool_w, pool_scale, pool_out,
    ret_decay, ret_norm_g, ret_out, w_out, peer_wq, peer_keys, peer_u, peer_v, final_g, c_2,
    ada_w_2, ada_b_2, norm_mix_w_2, norm_ffn_w_2, w_in_2, w_out_2, hg_lower_bounds_2,
    hg_gnorm_w_2, s5_a_re_2, s5_a_im_2, s5_log_dt_2, s5_b_re_2, s5_b_im_2, s5_c_re_2, s5_c_im_2,
    s5_d_2, s5_glu_w_2, s5_glu_b_2, peer_wq_2, peer_keys1_2, peer_keys2_2, peer_u_2, peer_v_2,
    final_norm_w_2,
):
    x = first_block(
        x, c, ctx, c_ctx, ada_w, ada_b, norm_mix_g, norm_ffn_g, w_in, pool_w, pool_scale,
        pool_out, ret_decay, ret_norm_g, ret_out, w_out, peer_wq, peer_keys, peer_u, peer_v,
        final_g,
    )
    return second_block(
        x, c_2, ada_w_2, ada_b_2, norm_mix_w_2, norm_ffn_w_2, w_in_2, w_out_2,
        hg_lower_bounds_2, hg_gnorm_w_2, s5_a_re_2, s5_a_im_2, s5_log_dt_2, s5_b_re_2,
        s5_b_im_2, s5_c_re_2, s5_c_im_2, s5_d_2, s5_glu_w_2, s5_glu_b_2, peer_wq_2,
        peer_keys1_2, peer_keys2_2, peer_u_2, peer_v_2, final_norm_w_2,
    )


_drawn_inputs = setup_inputs


def setup_inputs(seed=0):
    import zlib

    import numpy as np

    out = dict(_drawn_inputs(seed))
    spreads = {}
    factors = {'norm_mix_g': 5.314,
     'norm_ffn_g': 23.94,
     'pool_scale': 2.686,
     'ret_norm_g': 8.0,
     'final_g': 2.681,
     'ada_b_2': 5.757,
     'norm_mix_w_2': 8.0,
     'norm_ffn_w_2': 51.897,
     'hg_lower_bounds_2': 8.0,
     'hg_gnorm_w_2': 25.804,
     's5_a_re_2': 64.0,
     's5_a_im_2': 26.208,
     's5_log_dt_2': 31.576,
     's5_b_re_2': 36.232,
     's5_b_im_2': 34.616,
     's5_c_re_2': 38.048,
     's5_c_im_2': 31.96,
     's5_glu_w_2': 6.154,
     's5_glu_b_2': 64.0,
     'final_norm_w_2': 8.417}
    for name, (base, spread) in spreads.items():
        noise = np.random.default_rng([zlib.crc32(name.encode()), seed]).standard_normal(out[name].shape)
        drawn = base * np.exp(spread * noise) if base else spread * noise
        out[name] = __import__('jax').numpy.asarray(drawn.astype(out[name].dtype))
    for name, factor in factors.items():
        out[name] = (out[name] * factor).astype(out[name].dtype)
    return out
```

```python
from contextlib import ExitStack

import numpy as np
import concourse.bass as bass
from concourse import mybir

F32 = mybir.dt.float32
F32R = mybir.dt.float32r
BF16 = mybir.dt.bfloat16
U32 = mybir.dt.uint32
ALU = mybir.AluOpType
ACT = mybir.ActivationFunctionType
AX = mybir.AxisListType

P = 128
D = 1024
DC = D // P
L = 512
LC = 256
EPS = 1e-6


class Core:

    def __init__(self, nc, dram, ctx):
        self.nc, self.dram, self.ctx = nc, dram, ctx
        self.used = []

    def sb(self, name, shape, dt=F32, ctx=None):
        return (ctx or self.ctx).enter_context(self.nc.sbuf_tensor(name, shape, dt))

    def ps(self, name, shape, ctx, dt=F32):
        return ctx.enter_context(self.nc.psum_tensor(name, shape, dt))

    def sem(self, name):
        self.used.append(self.nc.alloc_semaphore(name=name))
        return self.used[-1]

    def recycle(self):
        self.nc.clear_and_free_semaphores(self.used)
        self.nc.all_engine_barrier()
        self.used = []


def f32(ap):
    return ap.bitcast(F32)




class WeightRing:

    def __init__(self, k, name, weights, n0, kc, ctx):
        self.weights, self.n0 = weights, n0
        self.raw = [k.sb(f"{name}_raw{j}", [P, kc, P], F32, ctx) for j in range(2)]
        self.k, self.name, self.landed = k, name, None

    def load(self, sp, i, j):
        sp.dma_start(self.raw[j][:], self.weights[self.n0 + 2 * i + j]).then_inc(self.landed[j], 16)

    def start(self, sp):
        self.landed = [self.k.sem(f"{self.name}_landed{j}") for j in range(2)]
        for j in range(2):
            self.load(sp, 0, j)


class Section:

    def __init__(self, first, last, act_out=None, dve_out=None, modulate=None):
        self.first, self.last = first, last
        self.act_out, self.dve_out, self.modulate = act_out, dve_out, modulate


def gemm(k, name, ring, sections, kc, rhs_hi, rhs_lo, width, at_end=None):
    nc = k.nc
    n0 = sections[0].first
    assert all((s.last - s.first) % 2 == 0 for s in sections)
    with ExitStack() as ctx:
        raw, landed = ring.raw, ring.landed
        hi = [k.sb(f"{name}_hi{j}", [P, kc, P], F32R, ctx) for j in range(2)]
        lo = [k.sb(f"{name}_lo{j}", [P, kc, P], F32R, ctx) for j in range(2)]
        acc = [k.ps(f"{name}_acc{j}", [P, 512], ctx) for j in range(2)]
        hi_ready, lo_ready = k.sem(f"{name}_hi_ready"), k.sem(f"{name}_lo_ready")
        product, taken = k.sem(f"{name}_product"), k.sem(f"{name}_taken")
        if any(s.modulate for s in sections):
            rows = [k.sb(f"{name}_rows{j}", [P, D], F32, ctx) for j in range(2)]
            rows_landed = [k.sem(f"{name}_rows_landed{j}") for j in range(2)]
            modulated = k.sem(f"{name}_modulated")
        block = ctx.enter_context(nc.Block(no_gpsimd_drain=True))

        def each(eng, pair, skip_first=False):
            before, at, m0 = None, 0, 0
            for s in sections:
                pairs = (s.last - s.first) // 2
                if not (skip_first and before is None):
                    pair(at, s, before, 0, m0)
                if pairs > 1:
                    with eng.Fori(1, pairs) as m:
                        pair(at + m, s, s, m, m0)
                before, at = s, at + pairs
                if s.modulate:
                    m0 += pairs

        @block.sync
        def _(sp):
            def pair(i, s, before, m, m0):
                for j in range(2):
                    if before is not None:
                        sp.wait_ge(lo_ready, 2 * i + j - 1)
                        ring.load(sp, i, j)
                    if s.modulate:
                        if not isinstance(m, int) or m or m0:
                            sp.wait_ge(modulated, 2 * (m0 + m) + j - 1)
                        sp.dma_start(rows[j][:], s.modulate[0][2 * m + j]).then_inc(rows_landed[j], 16)

            each(sp, pair)

        @block.tensor
        def _(pe):
            def pair(i, s, before, m, m0):
                for j in range(2):
                    pe.wait_ge(lo_ready, 2 * i + j + 1)
                    if before is not None:
                        pe.wait_ge(taken, 2 * i + j - 1)
                    for c in range(kc):
                        for n, (a, b) in enumerate(((hi, rhs_hi), (hi, rhs_lo), (lo, rhs_hi))):
                            mm = nc.tensor.matmul(acc[j][:, 0:width], a[j][:, c, :], b[:, c, :],
                                                  start=(c == 0 and n == 0), stop=(c == kc - 1 and n == 2))
                    mm.then_inc(product, 1)

            each(pe, pair)

        def take_out(eng, emit, i, j, tile):
            if emit is None:
                return
            eng.wait_ge(product, 2 * i + j + 1)
            emit(eng, tile, acc[j][:, 0:width]).then_inc(taken, 1)

        def last_tile(before, s, m):
            return 2 * m - 1 if before is s else before.last - before.first - 1

        @block.scalar
        def _(act):
            def split_hi(i, j, before):
                act.wait_ge(landed[j], 16 * (i + 1))
                if before is not None:
                    act.wait_ge(product, 2 * i + j - 1)
                nc.scalar.copy(hi[j][:], raw[j][:]).then_inc(hi_ready, 1)

            def pair(i, s, before, m, m0):
                split_hi(i, 0, before)
                if before is not None:
                    take_out(act, before.act_out, i - 1, 1, last_tile(before, s, m))
                split_hi(i, 1, before)
                take_out(act, s.act_out, i, 0, 2 * m)

            each(act, pair)
            s = sections[-1]
            take_out(act, s.act_out, (s.last - n0) // 2 - 1, 1, s.last - s.first - 1)

        @block.vector
        def _(dve):
            def split_lo(i, j):
                dve.wait_ge(hi_ready, 2 * i + j + 1)
                nc.vector.tensor_tensor(lo[j][:], raw[j][:], f32(hi[j][:]), ALU.subtract).then_inc(lo_ready, 1)

            def modulate(s, j, m, m0):
                if s.modulate:
                    _, cond, out = s.modulate
                    dve.wait_ge(rows_landed[j], 16 * (m0 + m + 1))
                    nc.vector.scalar_tensor_tensor(rows[j][:], rows[j][:], 1.0, cond, ALU.mult, ALU.mult,
                                                   accum_out=out(2 * m + j)).then_inc(modulated, 1)

            def pair(i, s, before, m, m0):
                split_lo(i, 0)
                if before is not None:
                    take_out(dve, before.dve_out, i - 1, 1, last_tile(before, s, m))
                modulate(s, 0, m, m0)
                split_lo(i, 1)
                take_out(dve, s.dve_out, i, 0, 2 * m)
                modulate(s, 1, m, m0)

            each(dve, pair)
            s = sections[-1]
            take_out(dve, s.dve_out, (s.last - n0) // 2 - 1, 1, s.last - s.first - 1)
            if at_end:
                dve.wait_ge(modulated, sum(s.last - s.first for s in sections if s.modulate))
                at_end()




def load_all(k, name, pairs):
    nc = k.nc
    loaded = k.sem(f"{name}_loaded")
    with nc.Block(no_gpsimd_drain=True) as block:

        @block.sync
        def _(sp):
            for dst, src in pairs:
                sp.dma_start(dst[:], src).then_inc(loaded, 16)
            sp.wait_ge(loaded, 16 * len(pairs))


def fill_constants(k, pairs):
    nc = k.nc
    with nc.Block(no_gpsimd_drain=True) as block:

        @block.vector
        def _(dve):
            for dst, value in pairs:
                nc.vector.memset(dst[:], value)


def start(k, loads, conds, weights, bias, out, tiles):
    nc = k.nc
    NR = 4
    with ExitStack() as ctx:
        rows = [k.sb(f"ada_rows{j}", [P, D], F32, ctx) for j in range(NR)]
        loaded, cond_loaded, silu_done = k.sem("ada_loaded"), k.sem("ada_cond_loaded"), k.sem("ada_silu")
        landed = [k.sem(f"ada_landed{j}") for j in range(NR)]
        modulated = k.sem("ada_modulated")
        block = ctx.enter_context(nc.Block(no_gpsimd_drain=True))

        @block.sync
        def _(sp):
            for dst, src in conds:
                sp.dma_start(dst[:], src).then_inc(cond_loaded, 16)
            for j in range(NR):
                sp.dma_start(rows[j][:], weights[j]).then_inc(landed[j], 16)
            for dst, src in loads:
                sp.dma_start(dst[:], src).then_inc(loaded, 16)
            with sp.Fori(1, tiles // NR) as i:
                for j in range(NR):
                    sp.wait_ge(modulated, NR * i + j - NR + 1)
                    sp.dma_start(rows[j][:], weights[NR * i + j]).then_inc(landed[j], 16)
            sp.wait_ge(loaded, 16 * len(loads))

        @block.scalar
        def _(act):
            act.wait_ge(cond_loaded, 16 * len(conds))
            for dst, _ in conds:
                nc.scalar.activation(dst[:], dst[:], ACT.Silu).then_inc(silu_done, 1)

        @block.vector
        def _(dve):
            nc.vector.memset(k.ones_model[:], 1.0 / D)
            dve.wait_ge(silu_done, len(conds))
            with dve.Fori(0, tiles // NR) as i:
                for j in range(NR):
                    dve.wait_ge(landed[j], 16 * (i + 1))
                    nc.vector.scalar_tensor_tensor(rows[j][:], rows[j][:], 1.0, conds[0][0][:], ALU.mult, ALU.mult,
                                                   accum_out=out[:, bass.ds(NR * i + j, 1), 0]).then_inc(modulated, 1)
            dve.wait_ge(modulated, tiles)
            dve.wait_ge(loaded, 16 * len(loads))
            nc.vector.tensor_tensor(out[:, 0:tiles, 0], out[:, 0:tiles, 0], bias[:, 0:tiles], ALU.add)


def norm_modulate(k, name, x, width, gain, shift, out_hi, out_lo, scale=None, plain=None, ring=None):
    nc = k.nc
    with ExitStack() as ctx:
        gain_in = gain
        gain = k.sb(f"{name}_gain", [P, DC], F32, ctx)
        gain_loaded = k.sem(f"{name}_gain_loaded")
        sq = k.sb(f"{name}_sq", [P, DC, width], F32, ctx)
        h = sq
        root = k.sb(f"{name}_root", [P, width], F32, ctx)
        rstd = k.sb(f"{name}_rstd", [P, width], F32, ctx)
        coef = k.sb(f"{name}_coef", [P, DC], F32, ctx)
        mean = k.ps(f"{name}_mean", [P, width], ctx)
        squared, summed = k.sem(f"{name}_squared"), k.sem(f"{name}_summed")
        guarded, rooted = k.sem(f"{name}_guarded"), k.sem(f"{name}_rooted")
        inverted, coef_ready = k.sem(f"{name}_inverted"), k.sem(f"{name}_coef_ready")
        scaled, hi_ready = k.sem(f"{name}_scaled"), k.sem(f"{name}_hi_ready")
        block = ctx.enter_context(nc.Block(no_gpsimd_drain=True))

        @block.sync
        def _(sp):
            sp.dma_start(gain[:], gain_in).then_inc(gain_loaded, 16)
            if ring is not None:
                ring.start(sp)

        @block.scalar
        def _(act):
            for c in range(DC):
                nc.scalar.activation(sq[:, c, :], x[:, c, :], ACT.Square).then_inc(squared, 1)
            act.wait_ge(guarded, 1)
            nc.scalar.activation(root[:], rstd[:], ACT.Sqrt).then_inc(rooted, 1)
            if plain is None:
                for c in range(DC):
                    act.wait_ge(scaled, c + 1)
                    nc.scalar.activation(out_hi[:, c, :], h[:, c, :], ACT.Identity,
                                         bias=shift[:, c:c + 1]).then_inc(hi_ready, 1)

        @block.tensor
        def _(pe):
            for c in range(DC):
                pe.wait_ge(squared, c + 1)
                mm = nc.tensor.matmul(mean[:], k.ones_model[:], sq[:, c, :], start=(c == 0), stop=(c == DC - 1))
            mm.then_inc(summed, 1)

        @block.vector
        def _(dve):
            dve.wait_ge(gain_loaded, 16)
            if scale is not None:
                nc.vector.scalar_tensor_tensor(coef[:], scale, 1.0, gain[:], ALU.add, ALU.mult).then_inc(coef_ready, 1)
            else:
                nc.vector.tensor_copy(coef[:], gain[:]).then_inc(coef_ready, 1)
            dve.wait_ge(summed, 1)
            nc.vector.tensor_scalar(rstd[:], mean[:], EPS, None, ALU.add).then_inc(guarded, 1)
            dve.wait_ge(rooted, 1)
            nc.vector.reciprocal(rstd[:], root[:]).then_inc(inverted, 1)
            dve.wait_ge(coef_ready, 1)
            dve.wait_ge(inverted, 1)
            for c in range(DC):
                nc.vector.scalar_tensor_tensor((h if plain is None else plain)[:, c, :], x[:, c, :], coef[:, c:c + 1],
                                               rstd[:], ALU.mult, ALU.mult).then_inc(scaled, 1)
            if plain is None:
                for c in range(DC):
                    dve.wait_ge(hi_ready, c + 1)
                    nc.vector.scalar_tensor_tensor(out_lo[:, c, :], h[:, c, :], shift[:, c:c + 1], f32(out_hi[:, c, :]),
                                                   ALU.add, ALU.subtract)


def activate(nc, dst, func):
    return lambda act, n, psum: nc.scalar.activation(dst[:, bass.ds(n, 1), :], psum, func)


def split(k, name, src, hi, lo, chunks, ring, small=None):
    nc = k.nc
    hi_ready, loaded = k.sem(f"{name}_hi_ready"), k.sem(f"{name}_loaded")
    with nc.Block(no_gpsimd_drain=True) as block:

        @block.sync
        def _(sp):
            ring.start(sp)
            if small:
                sp.dma_start(small[0][:], small[1]).then_inc(loaded, 16)
                sp.wait_ge(loaded, 16)

        @block.scalar
        def _(act):
            for c in range(chunks):
                nc.scalar.copy(hi[:, c, :], src[:, c, :]).then_inc(hi_ready, 1)

        @block.vector
        def _(dve):
            for c in range(chunks):
                dve.wait_ge(hi_ready, c + 1)
                nc.vector.tensor_tensor(lo[:, c, :], src[:, c, :], f32(hi[:, c, :]), ALU.subtract)


def to_rows(k, name, src, dst, tiles, blocks):
    nc = k.nc
    with ExitStack() as ctx:
        turn = [k.ps(f"{name}_turn{j}", [P, blocks, P], ctx) for j in range(2)]
        turned, copied = k.sem(f"{name}_turned"), k.sem(f"{name}_copied")
        block = ctx.enter_context(nc.Block(no_gpsimd_drain=True))

        @block.tensor
        def _(pe):
            for f in range(tiles):
                if f >= 2:
                    pe.wait_ge(copied, f - 1)
                for b in range(blocks):
                    mm = nc.tensor.transpose(turn[f % 2][:, b, :], src[:, f, b * P:(b + 1) * P], k.ident[:])
                mm.then_inc(turned, 1)

        @block.scalar
        def _(act):
            for f in range(tiles):
                act.wait_ge(turned, f + 1)
                nc.scalar.copy(dst[:, :, f * P:(f + 1) * P], turn[f % 2][:]).then_inc(copied, 1)


def head_norm(k, name, y, heads, per, ones, center, gain, gate, hi, lo, first, ring=None, free=None):
    nc = k.nc
    n = heads * per
    with ExitStack() as ctx:
        sq = free if free is not None else k.sb(f"{name}_sq", [P, n, L], F32, ctx)
        rstd = k.sb(f"{name}_rstd", [P, heads, L], F32, ctx)
        stat = [k.ps(f"{name}_stat{j}", [P, L], ctx) for j in range(2 * heads)]
        mean_done, centered = k.sem(f"{name}_mean_done"), k.sem(f"{name}_centered")
        squared, summed = k.sem(f"{name}_squared"), k.sem(f"{name}_summed")
        guarded, rooted = k.sem(f"{name}_guarded"), k.sem(f"{name}_rooted")
        inverted, scaled = k.sem(f"{name}_inverted"), k.sem(f"{name}_scaled")
        gated, hi_ready = k.sem(f"{name}_gated"), k.sem(f"{name}_hi_ready")
        block = ctx.enter_context(nc.Block(no_gpsimd_drain=True))

        @block.sync
        def _(sp):
            if ring is not None:
                ring.start(sp)

        @block.tensor
        def _(pe):
            if center:
                for h in range(heads):
                    for c in range(per):
                        mm = nc.tensor.matmul(stat[h][:], ones[:], y[:, h * per + c, :],
                                              start=(c == 0), stop=(c == per - 1))
                    mm.then_inc(mean_done, 1)
            for h in range(heads):
                pe.wait_ge(squared, h + 1)
                for c in range(per):
                    mm = nc.tensor.matmul(stat[heads + h][:], ones[:], sq[:, h * per + c, :],
                                          start=(c == 0), stop=(c == per - 1))
                mm.then_inc(summed, 1)

        @block.scalar
        def _(act):
            for h in range(heads):
                if center:
                    act.wait_ge(centered, per * (h + 1))
                nc.scalar.activation(sq[:, h * per:(h + 1) * per, :], y[:, h * per:(h + 1) * per, :],
                                     ACT.Square).then_inc(squared, 1)
            for h in range(heads):
                act.wait_ge(guarded, h + 1)
                nc.scalar.activation(rstd[:, h, :], rstd[:, h, :], ACT.Sqrt).then_inc(rooted, 1)
            for c in range(n):
                act.wait_ge(gated, c + 1)
                nc.scalar.copy(hi[:, first + c, :], y[:, c, :]).then_inc(hi_ready, 1)

        @block.vector
        def _(dve):
            if center:
                for h in range(heads):
                    dve.wait_ge(mean_done, h + 1)
                    for c in range(h * per, (h + 1) * per):
                        nc.vector.tensor_tensor(y[:, c, :], y[:, c, :], stat[h][:], ALU.subtract).then_inc(centered, 1)
            for h in range(heads):
                dve.wait_ge(summed, h + 1)
                nc.vector.tensor_scalar(rstd[:, h, :], stat[heads + h][:], EPS, None, ALU.add).then_inc(guarded, 1)
            for h in range(heads):
                dve.wait_ge(rooted, h + 1)
                nc.vector.reciprocal(rstd[:, h, :], rstd[:, h, :]).then_inc(inverted, 1)
            for h in range(heads):
                dve.wait_ge(inverted, h + 1)
                for c in range(h * per, (h + 1) * per):
                    nc.vector.tensor_tensor(sq[:, c, :], y[:, c, :], rstd[:, h, :], ALU.mult).then_inc(scaled, 1)
            for c in range(n):
                dve.wait_ge(scaled, c + 1)
                nc.vector.scalar_tensor_tensor(y[:, c, :], sq[:, c, :], gain(c), gate[:, c, :],
                                               ALU.mult, ALU.mult).then_inc(gated, 1)
            for c in range(n):
                dve.wait_ge(hi_ready, c + 1)
                nc.vector.tensor_tensor(lo[:, first + c, :], y[:, c, :], f32(hi[:, first + c, :]), ALU.subtract)



POOL_WINDOWS = (2, 4, 8, 16)
RET_HEADS = 4
RET_DK = 128
K_SCALE = RET_DK ** -0.5
STRIP = 3 * P + L
CSTRIP = P + L


def rope(k, name, x, cos, sin, heads):
    nc = k.nc
    with ExitStack() as ctx:
        a = [k.sb(f"{name}_a{j}", [P, L], F32, ctx) for j in range(2)]
        b = [k.sb(f"{name}_b{j}", [P, L], F32, ctx) for j in range(2)]
        swapped = [k.ps(f"{name}_swapped{j}", [P, L], ctx) for j in range(2)]
        swap_done, parts, rotated = k.sem(f"{name}_swap"), k.sem(f"{name}_parts"), k.sem(f"{name}_rotated")
        block = ctx.enter_context(nc.Block(no_gpsimd_drain=True))

        @block.tensor
        def _(pe):
            for h in range(heads):
                if h >= 2:
                    pe.wait_ge(parts, 2 * (h - 1))
                nc.tensor.matmul(swapped[h % 2][:], k.swap[:], x[:, h, :], start=True, stop=True).then_inc(swap_done, 1)

        @block.vector
        def _(dve):
            for h in range(heads):
                dve.wait_ge(swap_done, h + 1)
                if h >= 2:
                    dve.wait_ge(rotated, h - 1)
                nc.vector.tensor_tensor(a[h % 2][:], x[:, h, :], cos, ALU.mult).then_inc(parts, 1)
                nc.vector.tensor_tensor(b[h % 2][:], swapped[h % 2][:], sin, ALU.mult).then_inc(parts, 1)
                dve.wait_ge(parts, 2 * h + 2)
                nc.vector.tensor_tensor(x[:, h, :], a[h % 2][:], b[h % 2][:], ALU.add).then_inc(rotated, 1)


def decay_tables(k, decay, rel, crel, strip, cstrip):
    nc = k.nc
    n = 2 * RET_HEADS
    with ExitStack() as ctx:
        t = k.sb("decay_t", [P, 8, n], F32, ctx)
        ahead = k.sb("decay_ahead", [P, STRIP], F32, ctx)
        behind = k.sb("decay_behind", [P, STRIP], F32, ctx)
        to_end = k.sb("decay_to_end", [P, CSTRIP], F32, ctx)
        expo = k.sb("decay_expo", [P, STRIP], F32, ctx)
        cexp = [k.sb(f"decay_cexp{j}", [P, CSTRIP], F32, ctx) for j in range(2)]
        step, exp_done = k.sem("decay_step"), k.sem("decay_exp")
        ready, taken = k.sem("decay_ready"), k.sem("decay_taken")
        block = ctx.enter_context(nc.Block(no_gpsimd_drain=True))
        mag, z, w, w2, total, lg, den, term = (t[:, j, :] for j in range(8))

        @block.scalar
        def _(act):
            act.wait_ge(step, 1)
            nc.scalar.activation(z, mag, ACT.Exp, scale=-1.0).then_inc(exp_done, 1)
            for h in range(RET_HEADS):
                act.wait_ge(ready, 3 * h + 1)
                nc.scalar.activation(strip[:, h, :], expo[:], ACT.Exp).then_inc(taken, 1)
                act.wait_ge(ready, 3 * h + 3)
                for j in range(2):
                    nc.scalar.activation(cexp[j][:], cexp[j][:], ACT.Exp).then_inc(taken, 1)

        @block.vector
        def _(dve):
            n_steps = 0

            def after(ins):
                nonlocal n_steps
                n_steps += 1
                ins.then_inc(step, 1)
                dve.wait_ge(step, n_steps)

            after(nc.vector.scalar_tensor_tensor(mag, decay[:], -1.0, decay[:], ALU.mult, ALU.max))
            dve.wait_ge(exp_done, 1)
            after(nc.vector.tensor_scalar(den, z, 2.0, None, ALU.add))
            after(nc.vector.reciprocal(den, den))
            after(nc.vector.tensor_tensor(w, z, den, ALU.mult))
            after(nc.vector.tensor_tensor(w2, w, w, ALU.mult))
            after(nc.vector.tensor_scalar(total, w2, 1.0 / 17, 1.0 / 15, ALU.mult, ALU.add))
            for odd in (13, 11, 9, 7, 5, 3, 1):
                after(nc.vector.tensor_tensor(total, total, w2, ALU.mult))
                after(nc.vector.tensor_scalar(total, total, 1.0 / odd, None, ALU.add))
            after(nc.vector.tensor_tensor(total, total, w, ALU.mult))
            after(nc.vector.tensor_scalar(lg, decay[:], 0.0, None, ALU.min))
            after(nc.vector.scalar_tensor_tensor(lg, total, -2.0, lg, ALU.mult, ALU.add))
            after(nc.vector.tensor_scalar(ahead[:], rel[:], 0.0, None, ALU.max))
            after(nc.vector.tensor_scalar(behind[:], rel[:], 0.0, -1.0, ALU.min, ALU.mult))
            after(nc.vector.tensor_scalar(to_end[:], crel[:], -1.0, float(L + LC), ALU.mult, ALU.add))
            for h in range(RET_HEADS):
                f, b = lg[:, h:h + 1], lg[:, RET_HEADS + h:RET_HEADS + h + 1]
                if h >= 1:
                    dve.wait_ge(taken, 3 * h)
                after(nc.vector.tensor_scalar(expo[:], ahead[:], f, None, ALU.mult))
                nc.vector.scalar_tensor_tensor(expo[:], behind[:], b, expo[:], ALU.mult, ALU.add).then_inc(ready, 1)
                nc.vector.tensor_scalar(cexp[0][:], crel[:], f, None, ALU.mult).then_inc(ready, 1)
                nc.vector.tensor_scalar(cexp[1][:], to_end[:], b, None, ALU.mult).then_inc(ready, 1)
                dve.wait_ge(taken, 3 * h + 3)
                after(nc.vector.tensor_tensor(cstrip[:, h, :], cexp[0][:], cexp[1][:], ALU.add))


def retention(k, q, kk, kc, v, vc, strip, cstrip, y):
    nc = k.nc
    NS, NC = L // P, LC // P
    n = NS + NC
    with ExitStack() as ctx:
        w = k.sb("ret_w", [P, 4, L], F32, ctx)
        score = [k.ps(f"ret_score{j}", [P, L], ctx) for j in range(4)]
        out = [k.ps(f"ret_out{j}", [P, L], ctx) for j in range(4)]
        scored, weighted = k.sem("ret_scored"), k.sem("ret_weighted")
        used, summed, taken = k.sem("ret_used"), k.sem("ret_summed"), k.sem("ret_taken")
        block = ctx.enter_context(nc.Block(no_gpsimd_drain=True))
        units = [(h, s) for h in range(RET_HEADS) for s in range(n)]

        @block.tensor
        def _(pe):
            def weigh(u):
                h, s = units[u]
                pe.wait_ge(weighted, u + 1)
                if s == 0 and h >= 2:
                    pe.wait_ge(taken, 2 * (h - 1))
                for e in range(2):
                    val = v[:, s, (2 * h + e) * P:(2 * h + e + 1) * P] if s < NS else \
                        vc[:, s - NS, (2 * h + e) * P:(2 * h + e + 1) * P]
                    mm = nc.tensor.matmul(out[2 * (h % 2) + e][:], val, w[:, u % 4, :], start=(s == 0),
                                          stop=(s == n - 1), skip_group_check=True)
                mm.then_inc(used, 1)

            for u, (h, s) in enumerate(units):
                if u >= 4:
                    pe.wait_ge(weighted, u - 3)
                key = kk[:, h, s * P:(s + 1) * P] if s < NS else kc[:, h, (s - NS) * P:(s - NS + 1) * P]
                nc.tensor.matmul(score[u % 4][:], key, q[:, h, :], start=True, stop=True).then_inc(scored, 1)
                if u >= 2:
                    weigh(u - 2)
            weigh(len(units) - 2)
            weigh(len(units) - 1)

        @block.vector
        def _(dve):
            for u, (h, s) in enumerate(units):
                dve.wait_ge(scored, u + 1)
                if u >= 4:
                    dve.wait_ge(used, u - 3)
                at = (NS - 1 - s) * P if s < NS else (NC - 1 - (s - NS)) * P
                table = strip[:, h, at:at + L] if s < NS else cstrip[:, h, at:at + L]
                nc.vector.tensor_tensor(w[:, u % 4, :], score[u % 4][:], table, ALU.mult).then_inc(weighted, 1)

        @block.scalar
        def _(act):
            for h in range(RET_HEADS):
                act.wait_ge(used, n * (h + 1))
                for e in range(2):
                    nc.scalar.copy(y[:, 2 * h + e, :], out[2 * (h % 2) + e][:]).then_inc(taken, 1)


def pooling(k, p, inv_count, weights, gain, hi, lo, ring):
    nc = k.nc
    G = len(POOL_WINDOWS)
    PAD = max(POOL_WINDOWS)
    W = L + 2 * PAD
    with ExitStack() as ctx:
        s = [k.sb(f"pool_s{j}", [P, G, W], F32, ctx) for j in range(2)]
        d = k.sb("pool_d", [P, G, L], F32, ctx)
        mixed = k.sb("pool_mixed", [P, G, L], F32, ctx)
        prod = [k.ps(f"pool_prod{j}", [P, L], ctx) for j in range(G)]
        step, d_ready = k.sem("pool_step"), k.sem("pool_d_ready")
        product, mix_done, hi_ready = k.sem("pool_product"), k.sem("pool_mix"), k.sem("pool_hi")
        block = ctx.enter_context(nc.Block(no_gpsimd_drain=True))

        @block.sync
        def _(sp):
            ring.start(sp)

        @block.vector
        def _(dve):
            steps = 0

            def after(ins):
                nonlocal steps
                steps += 1
                ins.then_inc(step, 1)
                dve.wait_ge(step, steps)

            nc.vector.memset(s[0][:], 0.0).then_inc(step, 1)
            nc.vector.memset(s[1][:], 0.0).then_inc(step, 1)
            steps = 2
            dve.wait_ge(step, steps)
            after(nc.vector.tensor_copy(s[0][:, :, PAD:PAD + L], p[:]))
            for j in range(G):
                a, b, lag = s[j % 2], s[(j + 1) % 2], 2 ** j
                after(nc.vector.tensor_tensor(b[:, j:G, lag:W], a[:, j:G, lag:W], a[:, j:G, 0:W - lag], ALU.add))
                w = 2 ** (j + 1)
                at = PAD + w - w // 2 - 1
                after(nc.vector.tensor_tensor(d[:, j, :], b[:, j, at:at + L], inv_count[:, j, :], ALU.mult))
                nc.vector.tensor_tensor(d[:, j, :], d[:, j, :], p[:, j, :], ALU.subtract).then_inc(d_ready, 1)
            for g in range(G):
                dve.wait_ge(product, g + 1)
                nc.vector.tensor_scalar(mixed[:, g, :], prod[g][:], gain[:, g:g + 1], None, ALU.mult).then_inc(mix_done, 1)
            for g in range(G):
                dve.wait_ge(hi_ready, g + 1)
                nc.vector.tensor_tensor(lo[:, g, :], mixed[:, g, :], f32(hi[:, g, :]), ALU.subtract)

        @block.tensor
        def _(pe):
            for g in range(G):
                pe.wait_ge(d_ready, g + 1)
                nc.tensor.matmul(prod[g][:], weights[:, g, :], d[:, g, :], start=True, stop=True).then_inc(product, 1)

        @block.scalar
        def _(act):
            for g in range(G):
                act.wait_ge(mix_done, g + 1)
                nc.scalar.copy(hi[:, g, :], mixed[:, g, :]).then_inc(hi_ready, 1)



HEADS = 8
NKEYS = 128
TOPK = 16
PAIRS = HEADS * TOPK
LOWEST = -3.4028234663852886e38
TB = L // P
HALF = P // 2
PIECE = NKEYS // 16


class Chooser:

    SCORES, PAIRED, BEST, PLACED = 1 + 2 + 4, 2 + 2 + 1 + 1, 1 + 2 + 1 + 1, 2 + 2 + 2 + 2 + 2

    def __init__(self, k, name, ctx):
        sb = lambda n, shape, dt=F32: k.sb(f"{name}_{n}", shape, dt, ctx)
        self.k, self.nc = k, k.nc
        self.step = k.sem(f"{name}_step")
        self.s, self.rest = sb("s", [P, 2, NKEYS]), sb("rest", [P, 2, NKEYS])
        self.top, self.index = sb("top", [P, 2, TOPK]), sb("index", [P, 2, TOPK], U32)
        self.index_f = sb("index_f", [P, 2, TOPK])
        self.cand, self.crest = sb("cand", [P, TOPK, TOPK]), sb("crest", [P, TOPK, TOPK])
        self.best, self.pos = sb("best", [P, TOPK]), sb("pos", [P, TOPK], U32)
        self.place, self.place_f = sb("place", [P, 2, TOPK], U32), sb("place_f", [P, 2, TOPK])
        self.pick = [sb(f"pick{j}", [P, TOPK, TOPK]) for j in range(2)]
        self.n = 0

    def after(self, *inss):
        for ins in inss:
            ins.then_inc(self.step, 1)
        self.n += len(inss)
        self.nc.vector.wait_ge(self.step, self.n)

    def scores(self, s_all, tb, h):
        V, s, top, index = self.nc.vector, self.s, self.top, self.index
        self.n = 0
        self.after(V.tensor_copy(s[:], s_all[:, bass.ds(tb * (2 * HEADS) + h * 2, 2), :]))
        self.after(*[V.max(top[:, r, 0:8], s[:, r, :]) for r in range(2)])
        self.after(*[V.max_index(index[:, r, 0:8], top[:, r, 0:8], s[:, r, :]) for r in range(2)],
                   *[V.match_replace(self.rest[:, r, :], top[:, r, 0:8], s[:, r, :], LOWEST) for r in range(2)])
        assert self.n == self.SCORES

    def paired(self):
        V, rest, top, index = self.nc.vector, self.rest, self.top, self.index
        grid = [P, TOPK, TOPK]
        self.after(*[V.max(top[:, r, 8:16], rest[:, r, :]) for r in range(2)])
        self.after(*[V.max_index(index[:, r, 8:16], top[:, r, 8:16], rest[:, r, :]) for r in range(2)],
                   V.tensor_tensor(self.cand[:], top[:, 0, :].unsqueeze(2).broadcast_to(grid),
                                   top[:, 1, :].unsqueeze(1).broadcast_to(grid), ALU.add))
        self.after(V.tensor_copy(self.index_f[:], index[:]))

    def sixteen(self):
        V = self.nc.vector
        cand, crest = (m[:].rearrange("p a b -> p (a b)") for m in (self.cand, self.crest))
        best, pos = self.best, self.pos
        self.after(V.max(best[:, 0:8], cand))
        self.after(V.max_index(pos[:, 0:8], best[:, 0:8], cand), V.match_replace(crest, best[:, 0:8], cand, LOWEST))
        self.after(V.max(best[:, 8:16], crest))
        self.after(V.max_index(pos[:, 8:16], best[:, 8:16], crest))

    def placed(self, h, iota, found, shifted):
        V = self.nc.vector
        grid = [P, TOPK, TOPK]
        self.after(V.tensor_scalar(self.place[:, 0, :], self.pos[:], 4, None, ALU.logical_shift_right),
                   V.tensor_scalar(self.place[:, 1, :], self.pos[:], 15, None, ALU.bitwise_and))
        self.after(V.tensor_copy(self.place_f[:], self.place[:]),
                   V.tensor_scalar(shifted[:, bass.ds(h, 1), :], self.best[:].unsqueeze(1), self.best[:, 0:1], None, ALU.subtract))
        self.after(*[V.tensor_tensor(self.pick[r][:], self.place_f[:, r, :].unsqueeze(2).broadcast_to(grid),
                                     iota[:, 0:TOPK].unsqueeze(1).broadcast_to(grid), ALU.is_equal) for r in range(2)])
        self.after(*[V.tensor_tensor(self.pick[r][:], self.pick[r][:],
                                     self.index_f[:, r, :].unsqueeze(1).broadcast_to(grid), ALU.mult) for r in range(2)])
        self.after(*[V.tensor_reduce(found[:, r, bass.ds(h * TOPK, TOPK)], self.pick[r][:], AX.X, ALU.add) for r in range(2)])
        V.sem_clear(self.step)


def queries(k, name, wq, h_hi, h_lo, keys, iota, s_all, found, shifted):
    nc = k.nc
    with ExitStack() as ctx:
        raw = [k.sb(f"{name}_raw{j}", [P, DC, P], F32, ctx) for j in range(2)]
        hi = [k.sb(f"{name}_hi{j}", [P, DC, P], F32R, ctx) for j in range(2)]
        lo = [k.sb(f"{name}_lo{j}", [P, DC, P], F32R, ctx) for j in range(2)]
        q = [k.sb(f"{name}_q{j}", [P, L], F32, ctx) for j in range(2)]
        acc = [k.ps(f"{name}_acc{j}", [P, L], ctx) for j in range(2)]
        score = [k.ps(f"{name}_score{j}", [P, TB, NKEYS], ctx) for j in range(2)]
        sem = lambda n: k.sem(f"{name}_{n}")
        landed = [sem("landed0"), sem("landed1")]
        hi_ready, lo_ready, product = sem("hi_ready"), sem("lo_ready"), sem("product")
        q_ready, scored, s_ready = sem("q_ready"), sem("scored"), sem("s_ready")
        chooser = Chooser(k, f"{name}_choose", ctx)
        FREE = 2
        block = ctx.enter_context(nc.Block(no_gpsimd_drain=True))

        @block.sync
        def _(sp):
            with sp.Fori(0, HEADS) as i:
                for j in range(2):
                    sp.wait_ge(lo_ready, 2 * i + j + 1)
                    sp.dma_start(raw[j][:], wq[2 * i + j]).then_inc(landed[j], 16)

        @block.tensor
        def _(pe):
            pe.sem_inc(product, FREE)

            def products(i, j):
                pe.wait_ge(lo_ready, FREE + 2 * i + j + 1)
                pe.wait_ge(q_ready, 2 * i + j + 1)
                for c in range(DC):
                    for m, (a, b) in enumerate(((hi, h_hi), (hi, h_lo), (lo, h_hi))):
                        mm = nc.tensor.matmul(acc[j][:], a[j][:, c, :], b[:, c, :],
                                              start=(c == 0 and m == 0), stop=(c == DC - 1 and m == 2))
                mm.then_inc(product, 1)

            def scores(h):
                pe.wait_ge(q_ready, FREE + 2 * h + 2)
                pe.wait_ge(s_ready, 2 * h + 2)
                for r in range(2):
                    for tb in range(TB):
                        mm = nc.tensor.matmul(score[r][:, tb, :], q[r][:, tb * P:(tb + 1) * P],
                                              keys[:, bass.ds(2 * h + r, 1), :].rearrange("p o k -> p (o k)"),
                                              start=True, stop=True)
                mm.then_inc(scored, 1)

            products(0, 0)
            products(0, 1)
            with pe.Fori(1, HEADS) as i:
                products(i, 0)
                scores(i - 1)
                products(i, 1)
            scores(HEADS - 1)

        @block.scalar
        def _(act):
            act.sem_inc(q_ready, FREE)
            act.sem_inc(s_ready, 2)

            def split_hi(i, j):
                act.wait_ge(landed[j], 16 * (i + 1))
                act.wait_ge(product, 2 * i + j + 1)
                nc.scalar.copy(hi[j][:], raw[j][:]).then_inc(hi_ready, 1)

            def query(i, j):
                act.wait_ge(product, FREE + 2 * i + j + 1)
                nc.scalar.copy(q[j][:], acc[j][:]).then_inc(q_ready, 1)

            def take_scores(h):
                act.wait_ge(scored, h + 1)
                for r in range(2):
                    nc.scalar.copy(s_all[:].rearrange("p (tb hp) k -> p tb hp k", tb=TB)[:, :, bass.ds(2 * h + r, 1), :],
                                   score[r][:].unsqueeze(2)).then_inc(s_ready, 1)

            split_hi(0, 0)
            split_hi(0, 1)
            query(0, 0)
            with act.Fori(1, HEADS) as i:
                split_hi(i, 0)
                query(i - 1, 1)
                split_hi(i, 1)
                take_scores(i - 1)
                query(i, 0)
            query(HEADS - 1, 1)
            take_scores(HEADS - 1)

        @block.vector
        def _(dve):
            dve.sem_inc(lo_ready, FREE)

            def split_lo(i, j):
                dve.wait_ge(hi_ready, 2 * i + j + 1)
                nc.vector.tensor_tensor(lo[j][:], raw[j][:], f32(hi[j][:]), ALU.subtract).then_inc(lo_ready, 1)

            for i in range(2):
                split_lo(i, 0)
                split_lo(i, 1)
            with dve.Fori(2, HEADS) as i:
                dve.wait_ge(s_ready, 2 * i)
                split_lo(i, 0)
                chooser.scores(s_all, 0, i - 2)
                chooser.paired()
                split_lo(i, 1)
                chooser.sixteen()
                chooser.placed(i - 2, iota, found, shifted)
            for h in (HEADS - 2, HEADS - 1):
                dve.wait_ge(s_ready, 2 * h + 4)
                chooser.scores(s_all, 0, h)
                chooser.paired()
                chooser.sixteen()
                chooser.placed(h, iota, found, shifted)


def expert_inputs(k, name, u, h_hi, h_lo, iota, s_all, found, shifted, acts, table, held):
    nc = k.nc
    with ExitStack() as ctx:
        sb = lambda n, shape, dt=F32: k.sb(f"{name}_{n}", shape, dt, ctx)
        raw = [sb(f"raw{j}", [P, DC, P]) for j in range(4)]
        hi = [sb(f"hi{j}", [P, DC, P], F32R) for j in range(2)]
        lo = [sb(f"lo{j}", [P, DC, P], F32R) for j in range(2)]
        out = [sb(f"out{j}", [P, L]) for j in range(2)]
        one2 = [sb(f"one2_{j}", [P, 4, P]) for j in range(2)]
        one1 = [sb(f"one1_{j}", [P, 4, P]) for j in range(2)]
        warm = sb("warm", [P, 1])
        e, den, inv = sb("e", [P, HEADS, TOPK]), sb("den", [P, HEADS]), sb("inv", [P, HEADS])
        pairs = sb("pairs", [P, 3, P])
        acc = [k.ps(f"{name}_acc{j}", [P, L], ctx) for j in range(2)]
        bank = [k.ps(f"{name}_bank{j}", [P, 4, P], ctx) for j in range(2)]
        turn = k.ps(f"{name}_turn", [P, 3, P], ctx)
        sem = lambda n: k.sem(f"{name}_{n}")
        landed = [sem(f"landed{j}") for j in range(4)]
        stored = [sem("stored0"), sem("stored1")]
        sent = [sem("sent0"), sem("sent1")]
        hi_ready, lo_ready, product, taken = sem("hi_ready"), sem("lo_ready"), sem("product"), sem("taken")
        exp_done, summed, gate_ready, turned, pairs_ready = (sem(n) for n in ("exp_done", "summed", "gate_ready",
                                                                             "turned", "pairs_ready"))
        equal, hot, spread, emptied = sem("equal"), sem("hot"), sem("spread"), sem("emptied")
        chosen = sem("chosen")
        chooser = Chooser(k, f"{name}_choose", ctx)
        FREE = 2
        block = ctx.enter_context(nc.Block(no_gpsimd_drain=True))

        def all_slabs(eng, start_block, slab, half_done):
            class State:
                pass

            def a_block(p, first, more):
                s = State()
                s.p, s.more = p, more
                start_block(p)
                for s.half in range(2):
                    s.before = not first or s.half == 1
                    peel = not more and s.half == 1
                    def four(i, last):
                        for j in range(4):
                            s.last = last and j == 3
                            t = 16 * s.half + 4 * i + j
                            slab(32 * p + t, t, j, 2 * i + j // 2, s)
                    with eng.Fori(0, 3 if peel else 4) as i:
                        four(i, False)
                    if peel:
                        four(3, True)
                    half_done(s)

            a_block(0, True, True)
            with eng.Fori(1, TB - 1) as p:
                a_block(p, False, True)
            a_block(TB - 1, False, False)

        def nothing(s):
            pass

        @block.sync
        def _(sp):
            for j in range(4):
                sp.dma_start(raw[j][:], u[j]).then_inc(landed[j], 16)
            with sp.Fori(1, NKEYS // 4) as i:
                for j in range(4):
                    sp.wait_ge(lo_ready, FREE + 4 * i + j - 3)
                    sp.dma_start(raw[j][:], u[4 * i + j]).then_inc(landed[j], 16)

        @block.tensor
        def _(pe):
            pe.sem_inc(product, FREE)
            pe.sem_inc(spread, FREE)

            def start_block(p):
                pe.wait_ge(gate_ready, p + 1)
                for j in range(3):
                    mm = nc.tensor.transpose(turn[:, j, :], found[:, j, :], k.ident[:])
                mm.then_inc(turned, 1)

            def slab(n, t, j, h, s):
                pe.wait_ge(lo_ready, FREE + n + 1)
                pe.wait_ge(taken, n + 1)
                for c in range(DC):
                    for m, (a, b) in enumerate(((hi, h_hi), (hi, h_lo), (lo, h_hi))):
                        mm = nc.tensor.matmul(acc[j % 2][:], a[j % 2][:, c, :], b[:, c, :],
                                              start=(c == 0 and m == 0), stop=(c == DC - 1 and m == 2))
                mm.then_inc(product, 1)
                pe.wait_ge(hot, 1 + n + 1)
                pe.wait_ge(emptied, n + 1)
                for m in range(4):
                    mm = nc.tensor.matmul(bank[j % 2][:, m, :], one2[j % 2][:, m, :], one1[j % 2][:, m, :],
                                          start=True, stop=True)
                mm.then_inc(spread, 1)

            all_slabs(pe, start_block, slab, nothing)

        @block.scalar
        def _(act):
            act.sem_inc(taken, FREE)
            act.sem_inc(emptied, FREE)
            for j in range(2):
                act.sem_inc(stored[j], 16)
                act.sem_inc(sent[j], 16)

            def exp_scores(p):
                act.wait_ge(chosen, p + 1)
                nc.scalar.activation(e[:], shifted[:], ACT.Exp).then_inc(exp_done, 1)
                act.wait_ge(exp_done, 2 * p + 1)
                nc.scalar.activation(warm[:], e[:, 0, 0:1], ACT.Gelu).then_inc(exp_done, 1)

            def start_block(p):
                act.wait_ge(turned, p + 1)
                act.wait_ge(hot, 32 * p + 1)
                nc.scalar.copy(pairs[:], turn[:]).then_inc(pairs_ready, 1)

            def split_hi(n, slot):
                act.wait_ge(landed[slot], 4 * (n - slot) + 16)
                act.wait_ge(product, n + 1)
                nc.scalar.copy(hi[slot % 2][:], raw[slot][:]).then_inc(hi_ready, 1)

            def slab(n, t, j, h, s):
                if not s.last:
                    split_hi(n + 1, (j + 1) % 4)
                act.wait_ge(product, FREE + n + 1)
                act.wait_ge(stored[j % 2], 8 * (n - j % 2) + 16)
                nc.scalar.activation(out[j % 2][:], acc[j % 2][:], ACT.Gelu).then_inc(taken, 1)
                act.wait_ge(taken, FREE + n + 1)
                act.dma_start(acts[bass.ds(n, 1)].rearrange("o p t -> p (o t)"), out[j % 2][:]).then_inc(stored[j % 2], 16)
                at = t - 16 * s.half
                if s.before:
                    act.wait_ge(emptied, FREE + 32 * s.p + 16 * s.half)
                    act.wait_ge(sent[j % 2], 8 * (n - j % 2 - 16) + 16)
                    act.dma_start(table[bass.ds(at * PIECE, PIECE), :, bass.ds(s.p * P - HALF + s.half * HALF, HALF)]
                                  .rearrange("i j t -> j i t"),
                                  held[1 - s.half][:, bass.ds(at * PIECE, PIECE), :]).then_inc(sent[j % 2], 16)
                if s.before and j == 0:
                    for r in range(2):
                        act.wait_ge(sent[r], 128 * (2 * s.p + s.half - 1) + 16)
                act.wait_ge(spread, FREE + n + 1)
                nc.scalar.copy(held[s.half][:, :, bass.ds(at * 4, 4)].rearrange("p i t -> p t i"),
                               bank[j % 2][:]).then_inc(emptied, 1)

            def half_done(s):
                if s.half == 0 and s.more:
                    exp_scores(s.p + 1)

            exp_scores(0)
            act.wait_ge(landed[0], 16)
            nc.scalar.copy(hi[0][:], raw[0][:]).then_inc(hi_ready, 1)
            all_slabs(act, start_block, slab, half_done)
            for j in range(2):
                act.wait_ge(stored[j], 16 * (NKEYS // 2 + 1))
                act.wait_ge(sent[j], 128 * (2 * TB - 1) + 16)

        @block.vector
        def _(dve):
            dve.sem_inc(chosen, 1)

            def start_block(p):
                dve.wait_ge(exp_done, 2 * p + 2)
                nc.vector.tensor_reduce(den[:], e[:], AX.X, ALU.add).then_inc(summed, 1)
                dve.wait_ge(summed, 2 * p + 1)
                nc.vector.reciprocal(inv[:], den[:]).then_inc(summed, 1)
                dve.wait_ge(summed, 2 * p + 2)
                nc.vector.tensor_tensor(found[:, 2, :].rearrange("p (h c) -> p h c", h=HEADS), e[:],
                                        inv[:].unsqueeze(2).broadcast_to([P, HEADS, TOPK]), ALU.mult).then_inc(gate_ready, 1)

            def slab(n, t, j, h, s):
                dve.wait_ge(spread, n + 1)
                if j == 0:
                    dve.wait_ge(pairs_ready, s.p + 1)
                grid = [P, 4, P]
                row = iota[:].unsqueeze(1).broadcast_to(grid)
                cols = lambda what: pairs[:, what, bass.ds(4 * t, 4)].unsqueeze(2).broadcast_to(grid)
                nc.vector.tensor_tensor(one2[j % 2][:], row, cols(1), ALU.is_equal)
                nc.vector.tensor_tensor(one1[j % 2][:], row, cols(0), ALU.is_equal).then_inc(equal, 1)
                if s.more and s.half == 0:
                    if j % 2 == 0:
                        chooser.scores(s_all, s.p + 1, h)
                        chooser.paired()
                    else:
                        chooser.sixteen()
                        chooser.placed(h, iota, found, shifted)

            def half_done(s):
                if s.half == 0 and s.more:
                    dve.sem_inc(chosen, 1)

            all_slabs(dve, start_block, slab, half_done)

        @block.gpsimd
        def _(pool):
            pool.sem_inc(lo_ready, FREE)
            pool.sem_inc(hot, 1)

            def slab(n, t, j, h, s):
                pool.wait_ge(hi_ready, n + 1)
                nc.gpsimd.tensor_tensor(lo[j % 2][:], raw[j][:], f32(hi[j % 2][:]), ALU.subtract).then_inc(lo_ready, 1)
                pool.wait_ge(equal, n + 1)
                nc.gpsimd.tensor_tensor(one1[j % 2][:], one1[j % 2][:],
                                        pairs[:, 2, bass.ds(4 * t, 4)].unsqueeze(2).broadcast_to([P, 4, P]),
                                        ALU.mult).then_inc(hot, 1)

            all_slabs(pool, nothing, slab, nothing)


def expert_outputs(k, name, v, acts, table, held, x, gate, beside=None):
    nc = k.nc
    NT = NKEYS
    with ExitStack() as ctx:
        raw = [k.sb(f"{name}_raw{j}", [P, D], F32, ctx) for j in range(2)]
        hi = [k.sb(f"{name}_hi{j}", [P, D], F32R, ctx) for j in range(2)]
        lo = [k.sb(f"{name}_lo{j}", [P, D], F32R, ctx) for j in range(2)]
        a = [k.sb(f"{name}_a{j}", [P, L], F32, ctx) for j in range(2)]
        g = [k.sb(f"{name}_g{j}", [P, L], F32, ctx) for j in range(2)]
        w = [k.sb(f"{name}_w{j}", [P, L], F32, ctx) for j in range(2)]
        w_hi = [k.sb(f"{name}_w_hi{j}", [P, L], F32R, ctx) for j in range(2)]
        w_lo = [k.sb(f"{name}_w_lo{j}", [P, L], F32R, ctx) for j in range(2)]
        acc = [k.ps(f"{name}_acc{c}", [P, L], ctx) for c in range(DC)]
        sem = lambda n: k.sem(f"{name}_{n}")
        landed = [sem("landed0"), sem("landed1")]
        sent = sem("sent")
        w_ready, hi_ready, lo_ready, product = sem("w_ready"), sem("hi_ready"), sem("lo_ready"), sem("product")
        FREE = 2
        block = ctx.enter_context(nc.Block(no_gpsimd_drain=True))

        @block.sync
        def _(sp):
            def send(piece):
                sp.dma_start(table[bass.ds(piece * PIECE, PIECE), :, L - HALF:L].rearrange("i j t -> j i t"),
                             held[:, bass.ds(piece * PIECE, PIECE), :]).then_inc(sent, 16)

            def load_piece(piece):
                sp.wait_ge(sent, 16 * piece + 16)
                if not isinstance(piece, int) or piece + 1 < NT // PIECE:
                    send(piece + 1)
                for s in range(PIECE):
                    j, n = s % 2, piece * PIECE + s
                    sp.wait_ge(lo_ready, n + 1)
                    sp.dma_start(a[j][:], acts[bass.ds(n, 1)].rearrange("o p t -> p (o t)")).then_inc(landed[j], 16)
                    sp.dma_start(g[j][:], table[bass.ds(n, 1)].rearrange("o p t -> p (o t)")).then_inc(landed[j], 16)
                    sp.dma_start(raw[j][:], v[bass.ds(n, 1)].rearrange("o p t -> p (o t)")).then_inc(landed[j], 16)
                    if beside:
                        beside.load(sp, piece, s)

            send(0)
            with sp.Fori(0, NT // PIECE - 1) as piece:
                load_piece(piece)
            load_piece(NT // PIECE - 1)

        @block.tensor
        def _(pe):
            pe.sem_inc(product, FREE)

            def products(i, j, first=False, last=False):
                pe.wait_ge(lo_ready, FREE + 2 * i + j + 1)
                for c in range(DC):
                    for m, (p, q) in enumerate(((hi, w_hi), (hi, w_lo), (lo, w_hi))):
                        mm = nc.tensor.matmul(acc[c][:], p[j][:, c * P:(c + 1) * P], q[j][:],
                                              start=(first and m == 0), stop=(last and m == 2), skip_group_check=True)
                mm.then_inc(product, 1)

            products(0, 0, first=True)
            products(0, 1)
            with pe.Fori(1, NT // 2 - 1) as i:
                products(i, 0)
                products(i, 1)
            products(NT // 2 - 1, 0)
            products(NT // 2 - 1, 1, last=True)

        @block.scalar
        def _(act):
            def split_piece(piece):
                for s in range(PIECE):
                    j, n = s % 2, piece * PIECE + s
                    act.wait_ge(product, n + 1)
                    act.wait_ge(landed[j], 24 * (n - j) + 48)
                    nc.scalar.copy(hi[j][:], raw[j][:])
                    act.wait_ge(w_ready, n + 1)
                    nc.scalar.copy(w_hi[j][:], w[j][:]).then_inc(hi_ready, 1)
                    if beside:
                        beside.scalar(act, piece, s)

            if beside:
                beside.begin(act)
            split_piece(0)
            with act.Fori(1, NT // PIECE) as piece:
                split_piece(piece)
            if beside:
                beside.scalar_end(act)

        @block.vector
        def _(dve):
            dve.sem_inc(lo_ready, FREE)
            if beside:
                beside.vector_begin(dve)
            with dve.Fori(0, NT // PIECE) as piece:
                for s in range(PIECE):
                    j, n = s % 2, piece * PIECE + s
                    dve.wait_ge(landed[j], 24 * (n - j) + 48)
                    nc.vector.tensor_tensor(w[j][:], a[j][:], g[j][:], ALU.mult).then_inc(w_ready, 1)
                    dve.wait_ge(hi_ready, n + 1)
                    nc.vector.tensor_tensor(lo[j][:], raw[j][:], f32(hi[j][:]), ALU.subtract)
                    nc.vector.tensor_tensor(w_lo[j][:], w[j][:], f32(w_hi[j][:]), ALU.subtract).then_inc(lo_ready, 1)
                    if beside:
                        beside.vector(dve, piece, s)
            if beside:
                beside.vector_end(dve)
            dve.wait_ge(product, FREE + NT)
            for c in range(DC):
                nc.vector.scalar_tensor_tensor(x[:, c, :], acc[c][:], gate[:, c:c + 1], x[:, c, :], ALU.mult, ALU.add)


def peer(k, name, x, gain, shift, scale, gate, wq, keys_in, u, v, beside=None):
    nc = k.nc
    k.recycle()
    with ExitStack() as whole:
        held = [k.sb(f"{name}_held{j}", [P, NKEYS, HALF], F32, whole) for j in range(2)]
        with ExitStack() as outer:
            h_hi = k.sb(f"{name}_h_hi", [P, DC, L], F32R, outer)
            h_lo = k.sb(f"{name}_h_lo", [P, DC, L], F32R, outer)
            norm_modulate(k, f"{name}_norm", x, L, gain, shift, h_hi, h_lo, scale=scale)
            s_all = k.sb(f"{name}_s_all", [P, TB * 2 * HEADS, NKEYS], F32, outer)
            found = k.sb(f"{name}_found", [P, 3, PAIRS], F32, outer)
            shifted = k.sb(f"{name}_shifted", [P, HEADS, TOPK], F32, outer)
            with ExitStack() as ctx:
                keys = k.sb(f"{name}_keys", [P, 2 * HEADS, NKEYS], F32, ctx)
                load_all(k, f"{name}_keys", [(keys, keys_in)])
                queries(k, f"{name}_q", wq, h_hi, h_lo, keys, k.iota, s_all, found, shifted)
            expert_inputs(k, f"{name}_u", u, h_hi, h_lo, k.iota, s_all, found, shifted, k.acts, k.table, held)
            k.recycle()
        expert_outputs(k, f"{name}_v", v, k.acts, k.table, held[1], x, gate,
                       beside(k, whole) if beside else None)



HG_HEADS = 4
HG_SCALE = 128 ** -0.5
TINY = 2.0 ** -60
S5_TILES = 16
TWO_PI = 6.283185307179586
MAGIC = 12582912.0


def lower_bound(k, logits, lb, one_minus):
    nc = k.nc
    with ExitStack() as ctx:
        t = k.sb("lb_t", [P, 4, HG_HEADS], F32, ctx)
        step, exp_done = k.sem("lb_step"), k.sem("lb_exp")
        block = ctx.enter_context(nc.Block(no_gpsimd_drain=True))

        @block.vector
        def _(dve):
            nc.vector.tensor_tensor(t[:, 0, :], logits[:, 0, :], logits[:, 1, :], ALU.max).then_inc(step, 1)
            dve.wait_ge(step, 1)
            for r in range(2):
                nc.vector.tensor_tensor(t[:, 1 + r, :], logits[:, r, :], t[:, 0, :], ALU.subtract).then_inc(step, 1)
            dve.wait_ge(exp_done, 1)
            nc.vector.tensor_tensor(t[:, 3, :], t[:, 1, :], t[:, 2, :], ALU.add).then_inc(step, 1)
            dve.wait_ge(step, 4)
            nc.vector.reciprocal(t[:, 0, :], t[:, 3, :]).then_inc(step, 1)
            dve.wait_ge(step, 5)
            nc.vector.tensor_tensor(lb[:], t[:, 1, :], t[:, 0, :], ALU.mult)
            nc.vector.tensor_tensor(one_minus[:], t[:, 2, :], t[:, 0, :], ALU.mult)

        @block.scalar
        def _(act):
            act.wait_ge(step, 3)
            nc.scalar.activation(t[:, 1:3, :], t[:, 1:3, :], ACT.Exp).then_inc(exp_done, 1)


def forget_gates(k, q, sig, lb, one_minus, resets, b, key):
    nc = k.nc
    H = HG_HEADS
    with ExitStack() as ctx:
        f = k.sb("fg_f", [P, H, L], F32, ctx)
        t = [k.sb(f"fg_t{j}", [P, H, L], F32, ctx) for j in range(2)]
        ready, logged, log_f, f_ready = k.sem("fg_ready"), k.sem("fg_logged"), k.sem("fg_log_f"), k.sem("fg_f_ready")
        block = ctx.enter_context(nc.Block(no_gpsimd_drain=True))

        @block.vector
        def _(dve):
            for h in range(H):
                nc.vector.tensor_scalar(f[:, h, :], sig[:, h, :], one_minus[:, h:h + 1], lb[:, h:h + 1],
                                        ALU.mult, ALU.add).then_inc(f_ready, 1)
            nc.vector.tensor_scalar(q[:], q[:], HG_SCALE, None, ALU.mult)
            dve.wait_ge(f_ready, H)
            nc.vector.tensor_scalar(t[0][:], f[:], TINY, None, ALU.max).then_inc(ready, 1)
            nc.vector.tensor_scalar(t[1][:], f[:], 1.0 / TINY, 1.0, ALU.mult, ALU.min).then_inc(ready, 1)
            nc.vector.tensor_scalar(key[:], f[:], -1.0, 1.0, ALU.mult, ALU.add).then_inc(ready, 1)
            dve.wait_ge(logged, 2)
            dve.wait_ge(ready, 3)
            nc.vector.tensor_tensor(f[:], t[0][:], t[1][:], ALU.add).then_inc(log_f, 1)
            dve.wait_ge(log_f, 1)
            for h in range(H):
                nc.vector.tensor_tensor_scan(b[:, h, :], resets[:], f[:, h, :], 0.0, ALU.mult, ALU.add)

        @block.scalar
        def _(act):
            for j in range(2):
                act.wait_ge(ready, j + 1)
                nc.scalar.activation(t[j][:], t[j][:], ACT.Ln).then_inc(logged, 1)


def chunk_scores(k, q, key, b, masks, scores):
    nc = k.nc
    U = HG_HEADS * L // P
    W = U * P
    halves = [64, 32, 16, 8, 4, 2, 1]
    with ExitStack() as ctx:
        ql = [k.sb(f"cs_q{j}", [P, W], F32, ctx) for j in range(2)]
        kl = [k.sb(f"cs_k{j}", [P, W], F32, ctx) for j in range(2)]
        e = [k.sb(f"cs_e{j}", [P, W], F32, ctx) for j in range(2)]
        out = [k.ps(f"cs_out{j}", [P, 4, P], ctx) for j in range(8)]
        cleared, diff, exp_done = k.sem("cs_cleared"), k.sem("cs_diff"), k.sem("cs_exp")
        factors, product, merged = k.sem("cs_factors"), k.sem("cs_product"), k.sem("cs_merged")
        block = ctx.enter_context(nc.Block(no_gpsimd_drain=True))
        flat = lambda t: t[:].rearrange("p h t -> p (h t)")
        levels = len(halves) + 1

        def parts(ap, m):
            v = ap.rearrange("p (n two m) -> p n two m", two=2, m=m)
            return v[:, :, 0, :], v[:, :, 1, :]

        @block.tensor
        def _(pe):
            for i in range(levels):
                if i < len(halves):
                    pe.wait_ge(factors, 2 * (i + 1))
                for g in range(U // 4):
                    if i >= 2:
                        pe.wait_ge(merged, (i - 2) * (U // 4) + g + 1)
                    for j in range(4):
                        u = slice((4 * g + j) * P, (4 * g + j + 1) * P)
                        a, c = (kl[i % 2][:, u], ql[i % 2][:, u]) if i < len(halves) else (flat(key)[:, u], flat(q)[:, u])
                        mm = nc.tensor.matmul(out[4 * (i % 2) + g][:, j, :], a, c, start=True, stop=True)
                    mm.then_inc(product, 1)

        @block.scalar
        def _(act):
            for i in range(len(halves)):
                act.wait_ge(diff, 2 * (i + 1))
                nc.scalar.activation(e[i % 2][:], e[i % 2][:], ACT.Exp).then_inc(exp_done, 1)

        @block.vector
        def _(dve):
            for j in range(2):
                nc.vector.memset(ql[j][:], 0.0).then_inc(cleared, 1)
                nc.vector.memset(kl[j][:], 0.0).then_inc(cleared, 1)
            nc.vector.memset(scores[:], 0.0).then_inc(cleared, 1)
            dve.wait_ge(cleared, 5)

            def exponents(i):
                m = halves[i]
                first, second = parts(flat(b), m)
                mid = first[:, :, m - 1:m].broadcast_to([P, W // (2 * m), m])
                if i >= 2:
                    dve.wait_ge(factors, 2 * (i - 1))
                e1, e2 = parts(e[i % 2][:], m)
                nc.vector.tensor_tensor(e1, mid, first, ALU.subtract).then_inc(diff, 1)
                nc.vector.tensor_tensor(e2, second, mid, ALU.subtract).then_inc(diff, 1)

            def level(i):
                m = halves[i]
                dve.wait_ge(exp_done, i + 1)
                if i >= 2:
                    dve.wait_ge(product, (i - 1) * (U // 4))
                e1, e2 = parts(e[i % 2][:], m)
                k1, _ = parts(flat(key), m)
                _, q2 = parts(flat(q), m)
                nc.vector.tensor_tensor(parts(kl[i % 2][:], m)[0], k1, e1, ALU.mult).then_inc(factors, 1)
                nc.vector.tensor_tensor(parts(ql[i % 2][:], m)[1], q2, e2, ALU.mult).then_inc(factors, 1)

            def merge(i):
                for g in range(U // 4):
                    dve.wait_ge(product, i * (U // 4) + g + 1)
                    if i >= 1:
                        dve.wait_ge(merged, (i - 1) * (U // 4) + g + 1)
                    nc.vector.copy_predicated(scores[:, 4 * g:4 * g + 4, :],
                                              masks[:, i, :].unsqueeze(1).broadcast_to([P, 4, P]),
                                              out[4 * (i % 2) + g][:]).then_inc(merged, 1)

            exponents(0)
            for i in range(len(halves)):
                if i + 1 < len(halves):
                    exponents(i + 1)
                level(i)
                if i >= 1:
                    merge(i - 1)
            merge(levels - 2)
            merge(levels - 1)


def chunk_outputs(k, q, key, b, v, scores, y):
    nc = k.nc
    H, C = HG_HEADS, L // P
    U = H * C
    with ExitStack() as ctx:
        e = k.sb("co_e", [P, H, L], F32, ctx)
        qe = k.sb("co_qe", [P, H, L], F32, ctx)
        ke = k.sb("co_ke", [P, H, L], F32, ctx)
        kt = k.sb("co_kt", [P, U, P], F32, ctx)
        last = k.sb("co_last", [P, U], F32, ctx)
        state = k.sb("co_state", [P, U, P], F32, ctx)
        turn = [k.ps(f"co_turn{j}", [P, 4, P], ctx) for j in range(2)]
        out = [k.ps(f"co_out{j}", [P, L], ctx) for j in range(H)]
        add = [k.ps(f"co_add{j}", [P, 4, P], ctx) for j in range(2)]
        diff, exp_done, mult_done = k.sem("co_diff"), k.sem("co_exp"), k.sem("co_mult")
        turned, rows_ready, added, new_state = k.sem("co_turned"), k.sem("co_rows"), k.sem("co_added"), k.sem("co_state")
        out_done = k.sem("co_out_done")
        block = ctx.enter_context(nc.Block(no_gpsimd_drain=True))
        ends = b[:].rearrange("p h (c t) -> p (h c) t", t=P)[:, :, P - 1:P]

        @block.vector
        def _(dve):
            bu = b[:].rearrange("p h (c t) -> p (h c) t", t=P)
            nc.vector.tensor_tensor(ke[:].rearrange("p h (c t) -> p (h c) t", t=P),
                                    ends.broadcast_to([P, U, P]), bu, ALU.subtract).then_inc(diff, 1)
            dve.wait_ge(exp_done, 3)
            nc.vector.tensor_tensor(ke[:], ke[:], key[:], ALU.mult).then_inc(mult_done, 1)
            nc.vector.tensor_tensor(qe[:], q[:], e[:], ALU.mult).then_inc(mult_done, 1)
            for c in range(C - 1):
                dve.wait_ge(added, c + 1)
                if c >= 1:
                    dve.wait_ge(new_state, H * c)
                for h in range(H):
                    u = h * C + c
                    if c == 0:
                        ins = nc.vector.tensor_copy(state[:, u + 1, :], add[c % 2][:, h, :])
                    else:
                        ins = nc.vector.scalar_tensor_tensor(state[:, u + 1, :], state[:, u, :], last[:, u:u + 1],
                                                             add[c % 2][:, h, :], ALU.mult, ALU.add)
                    ins.then_inc(new_state, 1)

        @block.scalar
        def _(act):
            nc.scalar.activation(e[:], b[:], ACT.Exp).then_inc(exp_done, 1)
            nc.scalar.activation(last[:].unsqueeze(2), ends, ACT.Exp).then_inc(exp_done, 1)
            act.wait_ge(diff, 1)
            nc.scalar.activation(ke[:], ke[:], ACT.Exp).then_inc(exp_done, 1)
            for h in range(H):
                act.wait_ge(turned, h + 1)
                nc.scalar.copy(kt[:, 4 * h:4 * h + 4, :], turn[h % 2][:]).then_inc(rows_ready, 1)
            for h in range(H):
                act.wait_ge(out_done, H)
                nc.scalar.copy(y[:, h, :], out[h][:])

        @block.tensor
        def _(pe):
            pe.wait_ge(mult_done, 1)
            for h in range(H):
                if h >= 2:
                    pe.wait_ge(rows_ready, h - 1)
                for c in range(C):
                    mm = nc.tensor.transpose(turn[h % 2][:, c, :], ke[:, h, c * P:(c + 1) * P], k.ident[:])
                mm.then_inc(turned, 1)
            pe.wait_ge(rows_ready, H)
            for c in range(C - 1):
                if c >= 2:
                    pe.wait_ge(new_state, H * (c - 1))
                for h in range(H):
                    mm = nc.tensor.matmul(add[c % 2][:, h, :], kt[:, h * C + c, :], v[:, c, h * P:(h + 1) * P],
                                          start=True, stop=True)
                mm.then_inc(added, 1)
            pe.wait_ge(mult_done, 2)
            for c in range(C):
                if c >= 1:
                    pe.wait_ge(new_state, H * c)
                for h in range(H):
                    u, at = h * C + c, slice(c * P, (c + 1) * P)
                    mm = nc.tensor.matmul(out[h][:, at], v[:, c, h * P:(h + 1) * P], scores[:, u, :],
                                          start=True, stop=(c == 0))
                    if c >= 1:
                        mm = nc.tensor.matmul(out[h][:, at], state[:, u, :], qe[:, h, at], start=False, stop=True)
                    if c == C - 1:
                        mm.then_inc(out_done, 1)


def s5_parameters(k, a_re, a_im, log_dt, mag, turn_hi, turn_lo, coef_re, coef_im):
    nc = k.nc
    T = S5_TILES
    with ExitStack() as ctx:
        t = k.sb("s5p", [P, 20, T], F32, ctx)
        r12 = k.sb("s5p_r12", [P, T], F32R, ctx)
        step, act_done = k.sem("s5p_step"), k.sem("s5p_act")
        block = ctx.enter_context(nc.Block(no_gpsimd_drain=True))
        (dt, ard, th, n, r, r2, sin, cos, are, aim, den, inv, nr, p1, p2, cr, ci, ab, q1, q2) = (t[:, j, :] for j in range(20))

        @block.scalar
        def _(act):
            nc.scalar.activation(dt, log_dt[:], ACT.Exp).then_inc(act_done, 1)
            act.wait_ge(step, 2)
            nc.scalar.activation(mag[:], ard, ACT.Exp).then_inc(act_done, 1)
            act.wait_ge(step, 9)
            nc.scalar.activation(sin, r2, ACT.Sin, scale=6.28318500).then_inc(act_done, 1)
            nc.scalar.activation(cos, ab, ACT.Sin, scale=6.28318500).then_inc(act_done, 1)

        @block.vector
        def _(dve):
            steps = 0

            def after(ins):
                nonlocal steps
                steps += 1
                ins.then_inc(step, 1)
                dve.wait_ge(step, steps)

            V = nc.vector
            dve.wait_ge(act_done, 1)
            after(V.tensor_tensor(th, a_im[:], dt, ALU.mult))
            after(V.tensor_tensor(ard, a_re[:], dt, ALU.mult))
            after(V.tensor_scalar(n, th, 1.0 / TWO_PI, MAGIC, ALU.mult, ALU.add))
            after(V.tensor_scalar(n, n, MAGIC, None, ALU.subtract))
            after(V.scalar_tensor_tensor(r, n, -6.28125, th, ALU.mult, ALU.add))
            after(V.scalar_tensor_tensor(r, n, -(TWO_PI - 6.28125), r, ALU.mult, ALU.add))
            after(V.tensor_scalar(r2, r, 1.0 / TWO_PI, None, ALU.mult))
            after(V.scalar_tensor_tensor(ab, r2, -1.0, r2, ALU.mult, ALU.max))
            after(V.tensor_scalar(ab, ab, -1.0, 0.25, ALU.mult, ALU.add))
            after(V.tensor_copy(r12[:], r2))
            after(V.tensor_copy(turn_hi[:], f32(r12[:])))
            after(V.tensor_tensor(turn_lo[:], r2, turn_hi[:], ALU.subtract))
            dve.wait_ge(act_done, 4)
            after(V.tensor_tensor(are, mag[:], cos, ALU.mult))
            after(V.tensor_tensor(aim, mag[:], sin, ALU.mult))
            after(V.tensor_scalar(nr, are, 1.0, None, ALU.subtract))
            after(V.tensor_tensor(p1, a_re[:], a_re[:], ALU.mult))
            after(V.tensor_tensor(p2, a_im[:], a_im[:], ALU.mult))
            after(V.tensor_tensor(den, p1, p2, ALU.add))
            after(V.reciprocal(inv, den))
            for x1, y1, x2, y2, op, dst in ((nr, a_re[:], aim, a_im[:], ALU.add, coef_re[:]), (aim, a_re[:], nr, a_im[:], ALU.subtract, coef_im[:])):
                after(V.tensor_tensor(p1, x1, y1, ALU.mult))
                after(V.tensor_tensor(p2, x2, y2, ALU.mult))
                after(V.tensor_tensor(p1, p1, p2, op))
                after(V.tensor_tensor(dst, p1, inv, ALU.mult))

def s5_outputs(k, c_re, c_im, coef_re, coef_im, cc_re, cc_im):
    nc = k.nc
    with ExitStack() as ctx:
        big = [k.sb(f"s5c_big{j}", [P, S5_TILES, P], F32, ctx) for j in range(4)]
        part, part2 = k.sem("s5c_part"), k.sem("s5c_part2")
        block = ctx.enter_context(nc.Block(no_gpsimd_drain=True))
        wide = [P, S5_TILES, P]
        crb, cib = coef_re[:].unsqueeze(2).broadcast_to(wide), coef_im[:].unsqueeze(2).broadcast_to(wide)
        flat = lambda t: t[:].rearrange("p a b -> p (a b)")

        @block.gpsimd
        def _(pool):
            nc.gpsimd.tensor_tensor(big[3][:], c_im[:], crb, ALU.mult).then_inc(part2, 1)

        @block.vector
        def _(dve):
            nc.vector.tensor_tensor(big[0][:], c_re[:], crb, ALU.mult).then_inc(part, 1)
            nc.vector.tensor_tensor(big[1][:], c_im[:], cib, ALU.mult).then_inc(part, 1)
            nc.vector.tensor_tensor(big[2][:], c_re[:], cib, ALU.mult).then_inc(part, 1)
            dve.wait_ge(part, 3)
            nc.vector.tensor_tensor(cc_re[:], big[0][:], big[1][:], ALU.subtract)
            dve.wait_ge(part2, 1)
            nc.vector.scalar_tensor_tensor(flat(cc_im), flat(big[2]), -1.0, flat(big[3]), ALU.mult, ALU.subtract)


class BesideOutputs:

    def __init__(self, k, ctx):
        self.k, self.nc = k, k.nc
        self.rows = [k.sb(f"beside_rows{j}", [P, D], F32, ctx) for j in range(3)]
        self.turns, self.whole = k.sb("beside_turns", [P, L], F32, ctx), k.sb("beside_whole", [P, L], F32, ctx)
        self.arg = k.sb("beside_arg", [P, 2, L], F32, ctx)
        self.table = k.sb("beside_table", [P, 2, L], F32, ctx)
        self.time = k.sb("beside_time", [P, L], F32, ctx)
        self.bias = k.sb("beside_bias", [P, 6 * DC], F32, ctx)
        sem = lambda n: k.sem(f"beside_{n}")
        self.rows_landed = [sem(f"rows_landed{j}") for j in range(3)]
        self.modulated, self.loaded = sem("modulated"), sem("loaded")
        self.step, self.arg_ready = sem("step"), sem("arg_ready")
        self.table_ready, self.table_sent = sem("table_ready"), sem("table_sent")

    def load(self, sp, piece, s):
        if s in (0, 2, 4):
            m = s // 2
            if s == 0:
                sp.wait_ge(self.modulated, 3 * piece + 1)
            else:
                sp.wait_ge(self.modulated, 3 * piece + m + 1)
            sp.dma_start(self.rows[m][:], self.k.dram["ada_w_2"][3 * piece + m]).then_inc(self.rows_landed[m], 16)

    def begin(self, act):
        act.dma_start(self.time[:], self.k.dram["time"]).then_inc(self.loaded, 16)
        act.dma_start(self.bias[:], self.k.dram["ada_b_2"]).then_inc(self.loaded, 16)

    def scalar(self, act, piece, s):
        if isinstance(piece, int) and piece == 0:
            return
        self.tables(act, piece - 1, s)

    def tables(self, act, tile, s):
        if s in (0, 1):
            if s == 0:
                act.wait_ge(self.arg_ready, tile + 1)
                act.wait_ge(self.table_sent, 16 * tile + 16)
            self.nc.scalar.activation(self.table[:, s, :], self.arg[:, s, :], ACT.Sin,
                                      scale=6.28318500).then_inc(self.table_ready, 1)
        if s == 1:
            act.wait_ge(self.table_ready, 2 * tile + 4)
            act.dma_start(self.k.s5_table[bass.ds(tile, 1)].rearrange("o p r t -> p (o r) t"),
                          self.table[:]).then_inc(self.table_sent, 16)

    def scalar_end(self, act):
        for s in (0, 1):
            self.tables(act, S5_TILES - 1, s)
        act.wait_ge(self.table_sent, 16 * (S5_TILES + 1))

    def vector_begin(self, dve):
        dve.sem_inc(self.modulated, 3)
        dve.sem_inc(self.step, 1)
        dve.sem_inc(self.table_ready, 2)
        dve.sem_inc(self.table_sent, 16)
        dve.wait_ge(self.loaded, 32)

    def vector(self, dve, piece, s):
        V, k = self.nc.vector, self.k
        turns, whole, arg_sin, arg_cos = self.turns[:], self.whole[:], self.arg[:, 0, :], self.arg[:, 1, :]
        theta_hi, theta_lo = (t[:, bass.ds(piece, 1)] for t in (k.turn_hi, k.turn_lo))
        if s == 5:
            dve.wait_ge(self.table_ready, 2 * piece + 2)
        dve.wait_ge(self.step, 8 * piece + s + 1)
        if s == 0:
            ins = V.tensor_scalar(turns, self.time[:], theta_hi, None, ALU.mult)
        elif s in (1, 4):
            ins = V.tensor_scalar(whole, turns, MAGIC, MAGIC, ALU.add, ALU.subtract)
        elif s == 2:
            ins = V.tensor_tensor(turns, turns, whole, ALU.subtract)
        elif s == 3:
            ins = V.scalar_tensor_tensor(turns, self.time[:], theta_lo, turns, ALU.mult, ALU.add)
        elif s == 5:
            ins = V.tensor_tensor(arg_sin, turns, whole, ALU.subtract)
        elif s == 6:
            ins = V.scalar_tensor_tensor(arg_cos, arg_sin, -1.0, arg_sin, ALU.mult, ALU.max)
        else:
            ins = V.tensor_scalar(arg_cos, arg_cos, -1.0, 0.25, ALU.mult, ALU.add)
        ins.then_inc(self.step, 1)
        if s == 7:
            dve.wait_ge(self.step, 8 * piece + 9)
            dve.sem_inc(self.arg_ready, 1)
        if s in (1, 3, 5):
            m = s // 2
            dve.wait_ge(self.rows_landed[m], 16 * piece + 16)
            rows = self.rows[m][:]
            V.scalar_tensor_tensor(rows, rows, 1.0, k.cond_2[:], ALU.mult, ALU.mult,
                                   accum_out=k.mods2[:, bass.ds(3 * piece + m, 1), 0]).then_inc(self.modulated, 1)

    def vector_end(self, dve):
        dve.wait_ge(self.modulated, 3 + 6 * DC)
        mods = self.k.mods2[:, :, 0]
        self.nc.vector.tensor_tensor(mods, mods, self.bias[:], ALU.add)


def s5_scan(k, u, b_re, b_im, cc_re, cc_im, mag, skip, y):
    nc = k.nc
    T = S5_TILES
    NT = 3
    with ExitStack() as ctx:
        sb = lambda n, c: [k.sb(f"s5_{n}{j}", [P, L], F32, ctx) for j in range(c)]
        table = [k.sb(f"s5_table{j}", [P, 2, L], F32, ctx) for j in range(NT)]
        m, zin, z, parts, x = sb("m", 8), sb("zin", 4), sb("z", 4), sb("parts", 4), sb("x", 4)
        ypre = k.sb("s5_ypre", [P, 4, L], F32, ctx)
        bu = [k.ps(f"s5_bu{j}", [P, L], ctx) for j in range(4)]
        out = [k.ps(f"s5_out{j}", [P, L], ctx) for j in range(4)]
        landed = [k.sem(f"s5_landed{j}") for j in range(NT)]
        driven, turned, zin_ready, scanned = k.sem("s5_driven"), k.sem("s5_turned"), k.sem("s5_zin"), k.sem("s5_scanned")
        parts_vector, parts_pool = k.sem("s5_parts_vector"), k.sem("s5_parts_pool")
        x_vector, x_pool = k.sem("s5_x_vector"), k.sem("s5_x_pool")
        summed, y_ready = k.sem("s5_summed"), k.sem("s5_y")
        block = ctx.enter_context(nc.Block(no_gpsimd_drain=True))
        sin, cos = (lambda j: table[j % NT][:, 0, :]), (lambda j: table[j % NT][:, 1, :])


        @block.sync
        def _(sp):
            for j in range(T):
                if j >= NT:
                    sp.wait_ge(parts_vector, 2 * (j - NT + 1))
                    sp.wait_ge(parts_pool, 2 * (j - NT + 1))
                sp.dma_start(table[j % NT][:], k.s5_table[j]).then_inc(landed[j % NT], 16)

        @block.tensor
        def _(pe):
            def drive(j):
                if j >= 2:
                    pe.wait_ge(turned, 4 * (j - 1))
                for part, w in enumerate((b_re, b_im)):
                    mm = nc.tensor.matmul(bu[2 * (j % 2) + part][:], w[:, j, :], u[:, j // 4, :], start=True, stop=True)
                mm.then_inc(driven, 1)

            drive(0)
            drive(1)
            for j in range(T):
                if j + 2 < T:
                    drive(j + 2)
                pe.wait_ge(x_pool, j + 1)
                pe.wait_ge(x_vector, j + 1)
                for part, w in enumerate((cc_re, cc_im)):
                    mm = nc.tensor.matmul(out[j // 4][:], w[:, j, :], x[2 * (j % 2) + part][:],
                                          start=(j % 4 == 0 and part == 0), stop=(j % 4 == 3 and part == 1),
                                          skip_group_check=True)
                mm.then_inc(summed, 1)

        @block.scalar
        def _(act):
            for c in range(4):
                act.wait_ge(y_ready, c + 1)
                nc.scalar.activation(y[:, c, :], ypre[:, c, :], ACT.Gelu)

        @block.vector
        def _(dve):
            V = nc.vector

            def turn_back(j):
                s, c, a = sin(j), cos(j), 4 * (j % 2)
                br, bi = bu[2 * (j % 2)][:], bu[2 * (j % 2) + 1][:]
                dve.wait_ge(landed[j % NT], 16 * (j // NT + 1))
                dve.wait_ge(driven, j + 1)
                if j >= 2:
                    dve.wait_ge(zin_ready, 2 * (j - 1))
                for r, (p, q) in enumerate(((c, br), (s, bi), (c, bi), (s, br))):
                    V.tensor_tensor(m[a + r][:], p, q, ALU.mult).then_inc(turned, 1)

            def scan(j):
                a = 2 * (j % 2)
                dve.wait_ge(zin_ready, 2 * (j + 1))
                if j >= 2:
                    dve.wait_ge(parts_pool, 2 * (j - 1))
                    dve.wait_ge(parts_vector, 2 * (j - 1))
                decay = mag[:, j:j + 1].broadcast_to([P, L])
                for r in range(2):
                    V.tensor_tensor_scan(z[a + r][:], decay, zin[a + r][:], 0.0, ALU.mult, ALU.add).then_inc(scanned, 1)

            def turn_forth(j):
                dve.wait_ge(scanned, 2 * (j + 1))
                if j >= 1:
                    dve.wait_ge(x_vector, j)
                for r, p in enumerate((sin(j), cos(j))):
                    V.tensor_tensor(parts[2 + r][:], p, z[2 * (j % 2) + r][:], ALU.mult).then_inc(parts_vector, 1)
                if j >= 2:
                    dve.wait_ge(summed, j - 1)
                dve.wait_ge(parts_vector, 2 * (j + 1))
                V.tensor_tensor(x[2 * (j % 2) + 1][:], parts[2][:], parts[3][:], ALU.add).then_inc(x_vector, 1)

            turn_back(0)
            for j in range(T):
                if j + 1 < T:
                    turn_back(j + 1)
                scan(j)
                turn_forth(j)
            for c in range(4):
                dve.wait_ge(summed, 4 * (c + 1))
                V.scalar_tensor_tensor(ypre[:, c, :], u[:, c, :], skip[:, c:c + 1], out[c][:],
                                       ALU.mult, ALU.add).then_inc(y_ready, 1)

        @block.gpsimd
        def _(pool):
            G = nc.gpsimd

            def add(j):
                a = 4 * (j % 2)
                pool.wait_ge(turned, 4 * (j + 1))
                if j >= 2:
                    pool.wait_ge(scanned, 2 * (j - 1))
                for r, op in enumerate((ALU.add, ALU.subtract)):
                    G.tensor_tensor(zin[2 * (j % 2) + r][:], m[a + 2 * r][:], m[a + 2 * r + 1][:], op).then_inc(zin_ready, 1)

            def turn_forth(j):
                pool.wait_ge(landed[j % NT], 16 * (j // NT + 1))
                pool.wait_ge(scanned, 2 * (j + 1))
                if j >= 1:
                    pool.wait_ge(x_pool, j)
                for r, p in enumerate((cos(j), sin(j))):
                    G.tensor_tensor(parts[r][:], p, z[2 * (j % 2) + r][:], ALU.mult).then_inc(parts_pool, 1)
                if j >= 2:
                    pool.wait_ge(summed, j - 1)
                pool.wait_ge(parts_pool, 2 * (j + 1))
                G.tensor_tensor(x[2 * (j % 2)][:], parts[0][:], parts[1][:], ALU.subtract).then_inc(x_pool, 1)

            add(0)
            for j in range(T):
                if j + 1 < T:
                    add(j + 1)
                turn_forth(j)


def second_mixer(k, x):
    nc, d = k.nc, k.dram
    mods = k.mods2
    with ExitStack() as outer:
        out_ring = WeightRing(k, "mix2_out", d["w_out_2"], 0, DC, outer)
        both_hi = k.sb("both_hi", [P, DC, L], F32R, outer)
        both_lo = k.sb("both_lo", [P, DC, L], F32R, outer)
        with ExitStack() as top:
            u = k.sb("s5_u", [P, 4, L], F32, top)
            with ExitStack() as mid:
                q, sig, gate = (k.sb(n, [P, HG_HEADS, L], F32, mid) for n in ("hg_q", "hg_sig", "hg_gate"))
                v = k.sb("hg_v", [P, L // P, HG_HEADS * P], F32, mid)
                with ExitStack() as ctx:
                    vf = k.sb("hg_vf", [P, HG_HEADS, L], F32, ctx)
                    h_hi = k.sb("h2_hi", [P, DC, L], F32R, ctx)
                    h_lo = k.sb("h2_lo", [P, DC, L], F32R, ctx)
                    ring = WeightRing(k, "in2", d["w_in_2"], 0, DC, ctx)
                    norm_modulate(k, "mix2_norm", x, L, d["norm_mix_w_2"], mods[:, 0:DC, 0], h_hi, h_lo,
                                  scale=mods[:, DC:2 * DC, 0], ring=ring)
                    gemm(k, "in2", ring, [
                        Section(0, 4, act_out=activate(nc, q, ACT.Silu)),
                        Section(4, 8, act_out=activate(nc, sig, ACT.Sigmoid)),
                        Section(8, 12, act_out=activate(nc, vf, ACT.Copy)),
                        Section(12, 16, act_out=activate(nc, gate, ACT.Silu)),
                        Section(16, 20, act_out=activate(nc, u, ACT.Copy))], DC, h_hi, h_lo, L)
                    to_rows(k, "hg_v_rows", vf, v, HG_HEADS, L // P)
                k.recycle()
                key, b, y = (k.sb(n, [P, HG_HEADS, L], F32, mid) for n in ("hg_key", "hg_b", "hg_y"))
                scores = k.sb("hg_scores", [P, 16, P], F32, mid)
                masks = k.sb("hg_masks", [P, 8, P], U32, mid)
                logits = k.sb("hg_logits", [P, 2, HG_HEADS], F32, mid)
                lb, one_minus = (k.sb(n, [P, HG_HEADS], F32, mid) for n in ("hg_lb", "hg_1lb"))
                resets = k.sb("hg_resets", [P, L], F32, mid)
                gn = k.sb("hg_gn", [P, 1], F32, mid)
                ones = k.sb("ones_head2", [P, P], F32, mid)
                load_all(k, "hg", [(masks, d["hg_masks"]), (logits, d["hg_lower_bounds"]), (resets, d["resets"]),
                                   (gn, d["hg_gnorm_w"])])
                fill_constants(k, [(ones, 1.0 / P)])
                lower_bound(k, logits, lb, one_minus)
                forget_gates(k, q, sig, lb, one_minus, resets, b, key)
                chunk_scores(k, q, key, b, masks, scores)
                chunk_outputs(k, q, key, b, v, scores, y)
                head_norm(k, "hg_norm", y, HG_HEADS, 1, ones, False, lambda c: gn[:, 0:1], gate, both_hi, both_lo, 0)
            k.recycle()
            y = k.sb("s5_y", [P, 4, L], F32, top)
            with ExitStack() as mid:
                sb = lambda n, shape: k.sb(f"s5_{n}", shape, F32, mid)
                b_re, b_im, cc_re, cc_im = (sb(n, [P, S5_TILES, P]) for n in ("b_re", "b_im", "cc_re", "cc_im"))
                skip = sb("skip", [P, 4])
                with ExitStack() as ctx:
                    c_re, c_im = (k.sb(f"s5_{n}", [P, S5_TILES, P], F32, ctx) for n in ("c_re", "c_im"))
                    load_all(k, "s5", [(c_re, d["s5_c_re"]), (c_im, d["s5_c_im"]), (b_re, d["s5_b_re"]),
                                       (b_im, d["s5_b_im"]), (skip, d["s5_d"])])
                    s5_outputs(k, c_re, c_im, k.coef_re, k.coef_im, cc_re, cc_im)
                s5_scan(k, u, b_re, b_im, cc_re, cc_im, k.mag, skip, y)
            with ExitStack() as mid:
                y_hi = k.sb("s5_y_hi", [P, 4, L], F32R, mid)
                y_lo = k.sb("s5_y_lo", [P, 4, L], F32R, mid)
                glu = k.sb("s5_glu", [P, 4, L], F32, mid)
                bias = k.sb("s5_glu_b", [P, 4], F32, mid)
                ring = WeightRing(k, "s5_glu", d["s5_glu_w"], 0, 4, mid)
                split(k, "s5_y_split", y, y_hi, y_lo, 4, ring, (bias, d["s5_glu_b"]))
                gemm(k, "s5_glu", ring, [Section(0, 4, act_out=lambda e, n, ps: nc.scalar.activation(
                    glu[:, bass.ds(n, 1), :], ps, ACT.Sigmoid, bias=bias[:, bass.ds(n, 1)]))], 4, y_hi, y_lo, L)
                gate_and_split(k, "s5_gated", y, glu, both_hi, both_lo, 4, 4, out_ring)
        residual_gemm(k, "mix2_out", out_ring, both_hi, both_lo, x, mods[:, 2 * DC:3 * DC, 0])


def gate_and_split(k, name, y, g, hi, lo, chunks, first, ring):
    nc = k.nc
    gated, hi_ready = k.sem(f"{name}_gated"), k.sem(f"{name}_hi_ready")
    with nc.Block(no_gpsimd_drain=True) as block:

        @block.sync
        def _(sp):
            ring.start(sp)

        @block.vector
        def _(dve):
            for c in range(chunks):
                nc.vector.tensor_tensor(y[:, c, :], y[:, c, :], g[:, c, :], ALU.mult).then_inc(gated, 1)
            for c in range(chunks):
                dve.wait_ge(hi_ready, c + 1)
                nc.vector.tensor_tensor(lo[:, first + c, :], y[:, c, :], f32(hi[:, first + c, :]), ALU.subtract)

        @block.scalar
        def _(act):
            for c in range(chunks):
                act.wait_ge(gated, c + 1)
                nc.scalar.copy(hi[:, first + c, :], y[:, c, :]).then_inc(hi_ready, 1)




def first_mixer(k, x):
    nc, d = k.nc, k.dram
    mods, ada_w = k.mods1, d["ada_w"]

    def modulation_tiles(first, vector, cond):
        return ada_w[first:6 * DC], cond[:], lambda n: mods[:, bass.ds(first + n, 1), vector]

    def add_bias(first, last, vector):
        m = mods[:, first:last, vector]
        return nc.vector.tensor_tensor(m, m, k.ada_b[:, first:last], ALU.add)

    with ExitStack() as outer:
        g_pool = k.sb("g_pool", [P, DC, L], F32, outer)
        g_ret = k.sb("g_ret", [P, DC, L], F32, outer)
        with ExitStack() as mid:
            gate = k.sb("gate", [P, DC, L], F32, mid)
            pool_in = k.sb("pool_in", [P, 4, L], F32, mid)
            with ExitStack() as inner:
                q = k.sb("q", [P, RET_HEADS, L], F32, inner)
                kk = k.sb("kk", [P, RET_HEADS, L], F32, inner)
                v = k.sb("v", [P, L // P, D], F32, inner)
                with ExitStack() as ctx:
                    vf = k.sb("vf", [P, DC, L], F32, ctx)
                    with ExitStack() as act_ctx:
                        h_hi = k.sb("h_hi", [P, DC, L], F32R, act_ctx)
                        h_lo = k.sb("h_lo", [P, DC, L], F32R, act_ctx)
                        ring = WeightRing(k, "in", d["w_in"], 0, DC, act_ctx)
                        norm_modulate(k, "mix_norm", x, L, d["norm_mix_g"], mods[:, 0:DC, 0], h_hi, h_lo,
                                      scale=mods[:, DC:2 * DC, 0], ring=ring)

                        def rest(first):
                            return modulation_tiles(first, 0, k.cond)

                        def context(first):
                            return modulation_tiles(first, 1, k.cond_ctx)

                        gemm(k, "in", ring, [
                            Section(0, 4, act_out=activate(nc, pool_in, ACT.Copy), modulate=context(0)),
                            Section(4, 8, act_out=activate(nc, q, ACT.Copy), modulate=context(4)),
                            Section(8, 12, act_out=activate(nc, kk, ACT.Copy), modulate=context(8)),
                            Section(12, 16, act_out=activate(nc, vf[:, 0:4, :], ACT.Copy), modulate=context(12)),
                            Section(16, 20, act_out=activate(nc, vf[:, 4:8, :], ACT.Copy), modulate=rest(16)),
                            Section(20, 28, act_out=activate(nc, gate, ACT.Silu), modulate=rest(20)),
                            Section(28, 36, act_out=activate(nc, g_pool, ACT.Sigmoid), modulate=rest(28)),
                            Section(36, 44, act_out=activate(nc, g_ret, ACT.Sigmoid), modulate=rest(36))],
                            DC, h_hi, h_lo, L, at_end=lambda: (add_bias(0, 16, 1), add_bias(16, 44, 0)))
                    to_rows(k, "v_rows", vf, v, DC, L // P)
                k.recycle()
                kc = k.sb("kc", [P, RET_HEADS, LC], F32, inner)
                vc = k.sb("vc", [P, LC // P, D], F32, inner)
                with ExitStack() as ctx:
                    ctx_in = k.sb("ctx_in", [P, DC, LC], F32, ctx)
                    ctx_hi = k.sb("ctx_hi", [P, DC, LC], F32R, ctx)
                    ctx_lo = k.sb("ctx_lo", [P, DC, LC], F32R, ctx)
                    vcf = k.sb("vcf", [P, DC, LC], F32, ctx)
                    ring = WeightRing(k, "ctx", d["w_ctx"], 0, DC, ctx)
                    load_all(k, "ctx_in", [(ctx_in, d["ctx"])])
                    norm_modulate(k, "ctx_norm", ctx_in, LC, d["norm_mix_g"], mods[:, 0:DC, 1], ctx_hi, ctx_lo,
                                  scale=mods[:, DC:2 * DC, 1], ring=ring)
                    gemm(k, "ctx_kv", ring, [
                        Section(0, 4, act_out=lambda e, n, ps: nc.scalar.mul(kc[:, bass.ds(n, 1), :], ps, K_SCALE),
                                modulate=modulation_tiles(44, 0, k.cond)),
                        Section(4, 12, act_out=activate(nc, vcf, ACT.Copy))],
                        DC, ctx_hi, ctx_lo, LC, at_end=lambda: add_bias(44, 48, 0))
                    to_rows(k, "ctx_v_rows", vcf, vc, DC, LC // P)
                with ExitStack() as ctx:
                    table = {n: k.sb(f"rope_{n}", [P, L], F32, ctx) for n in ("cos", "sin", "kcos", "ksin")}
                    load_all(k, "rope", [(t, d[f"rope_{n}"]) for n, t in table.items()])
                    rope(k, "rope_q", q, table["cos"][:], table["sin"][:], RET_HEADS)
                    rope(k, "rope_k", kk, table["kcos"][:], table["ksin"][:], RET_HEADS)
                y = k.sb("ret_y", [P, DC, L], F32, inner)
                with ExitStack() as ctx:
                    strip = k.sb("strip", [P, RET_HEADS, STRIP], F32, ctx)
                    cstrip = k.sb("cstrip", [P, RET_HEADS, CSTRIP], F32, ctx)
                    with ExitStack() as c2:
                        decay = k.sb("decay", [P, 2 * RET_HEADS], F32, c2)
                        rel = k.sb("rel", [P, STRIP], F32, c2)
                        crel = k.sb("crel", [P, CSTRIP], F32, c2)
                        load_all(k, "decay", [(decay, d["ret_decay"]), (rel, d["rel"]), (crel, d["crel"])])
                        decay_tables(k, decay, rel, crel, strip, cstrip)
                    retention(k, q, kk, kc, v, vc, strip, cstrip, y)
                k.recycle()
                with ExitStack() as ctx:
                    ng = k.sb("ret_ng", [P, DC], F32, ctx)
                    ones = k.sb("ones_head", [P, P], F32, ctx)
                    r_hi = k.sb("r_hi", [P, DC, L], F32R, ctx)
                    r_lo = k.sb("r_lo", [P, DC, L], F32R, ctx)
                    ring = WeightRing(k, "ret_out", d["ret_out"], 0, DC, ctx)
                    fill_constants(k, [(ones, 1.0 / (2 * P))])
                    load_all(k, "ret_ng", [(ng, d["ret_norm_g"])])
                    with ExitStack() as c2:
                        head_norm(k, "ret_norm", y, RET_HEADS, 2, ones, True, lambda c: ng[:, c:c + 1], gate,
                                  r_hi, r_lo, 0, ring, v[:].rearrange("p a (b t) -> p (a b) t", t=L))
                    gemm(k, "ret_out", ring, [Section(0, DC, dve_out=lambda e, n, ps: nc.vector.tensor_tensor(
                        g_ret[:, bass.ds(n, 1), :], ps, g_ret[:, bass.ds(n, 1), :], ALU.mult))], DC, r_hi, r_lo, L)
            with ExitStack() as ctx:
                inv = k.sb("inv_count", [P, 4, L], F32, ctx)
                pw = k.sb("pool_w", [P, 4, P], F32, ctx)
                pg = k.sb("pool_gain", [P, 4], F32, ctx)
                p_hi = k.sb("p_hi", [P, 4, L], F32R, ctx)
                p_lo = k.sb("p_lo", [P, 4, L], F32R, ctx)
                ring = WeightRing(k, "pool_out", d["pool_out"], 0, 4, ctx)
                load_all(k, "pool", [(inv, d["inv_count"]), (pw, d["pool_w"]), (pg, d["pool_scale"])])
                pooling(k, pool_in, inv, pw, pg, p_hi, p_lo, ring)
                gemm(k, "pool_out", ring, [Section(0, DC, dve_out=lambda e, n, ps: nc.vector.tensor_tensor(
                    g_pool[:, bass.ds(n, 1), :], ps, g_pool[:, bass.ds(n, 1), :], ALU.mult))], 4, p_hi, p_lo, L)
        with ExitStack() as ctx:
            m_hi = k.sb("m_hi", [P, DC, L], F32R, ctx)
            m_lo = k.sb("m_lo", [P, DC, L], F32R, ctx)
            ring = WeightRing(k, "mix_out", d["w_out"], 0, DC, ctx)
            add_into(k, "merge", g_pool, g_ret, DC)
            split(k, "merged", g_pool, m_hi, m_lo, DC, ring)
            residual_gemm(k, "mix_out", ring, m_hi, m_lo, x, mods[:, 2 * DC:3 * DC, 0])


def add_into(k, name, a, b, chunks):
    nc = k.nc
    with nc.Block(no_gpsimd_drain=True) as block:

        @block.vector
        def _(dve):
            for c in range(chunks):
                nc.vector.tensor_tensor(a[:, c, :], a[:, c, :], b[:, c, :], ALU.add)


def residual_gemm(k, name, ring, hi, lo, x, gate):
    nc = k.nc
    gemm(k, name, ring, [Section(0, DC, dve_out=lambda e, n, ps: nc.vector.scalar_tensor_tensor(
        x[:, bass.ds(n, 1), :], ps, gate[:, bass.ds(n, 1)], x[:, bass.ds(n, 1), :], ALU.mult, ALU.add))], DC, hi, lo, L)


def program(nc, dram, out, stop=99):
    with ExitStack() as ctx:
        k = Core(nc, dram, ctx)
        d = dram
        x = k.sb("x", [P, DC, L])
        k.mods1 = k.sb("mods1", [P, 6 * DC, 2])
        k.mods2 = k.sb("mods2", [P, 6 * DC, 1])
        k.ident = k.sb("ident", [P, P])
        k.swap = k.sb("swap", [P, P])
        k.ones_model = k.sb("ones_model", [P, P])
        k.iota = k.sb("iota", [P, NKEYS])
        k.mag, k.turn_hi, k.turn_lo, k.coef_re, k.coef_im = (
            k.sb(f"s5_{n}", [P, S5_TILES]) for n in ("mag", "turn_hi", "turn_lo", "coef_re", "coef_im"))
        k.table = nc.dram_tensor("gate_table", [NKEYS, NKEYS, L], F32).ap()
        k.acts = nc.dram_tensor("expert_acts", [NKEYS, NKEYS, L], F32).ap()
        k.s5_table = nc.dram_tensor("s5_rotations", [S5_TILES, P, 2, L], F32).ap()

        def third(m, j):
            return m[:, j * DC:(j + 1) * DC, 0]

        with ExitStack() as first:
            k.cond_2 = k.sb("cond_2", [P, D], F32, first)
            with ExitStack() as mixer:
                k.cond, k.cond_ctx = (k.sb(n, [P, D], F32, mixer) for n in ("cond", "cond_ctx"))
                k.ada_b = k.sb("ada_b", [P, 6 * DC], F32, mixer)
                with ExitStack() as begin:
                    a_re, a_im, log_dt = (k.sb(f"s5_{n}", [P, S5_TILES], F32, begin) for n in ("a_re", "a_im", "log_dt"))
                    start(k, [(x, d["x"]), (k.ident, d["ident"]), (k.swap, d["swap"]), (k.iota, d["iota"]),
                              (k.ada_b, d["ada_b"]), (a_re, d["s5_a_re"]), (a_im, d["s5_a_im"]), (log_dt, d["s5_log_dt"])],
                          [(k.cond, d["cond"]), (k.cond_ctx, d["cond_ctx"]), (k.cond_2, d["cond_2"])],
                          d["ada_w"], k.ada_b, k.mods1, 2 * DC)
                    s5_parameters(k, a_re, a_im, log_dt, k.mag, k.turn_hi, k.turn_lo, k.coef_re, k.coef_im)
                first_mixer(k, x)
            peer(k, "peer1", x, d["norm_ffn_g"], third(k.mods1, 3), third(k.mods1, 4), third(k.mods1, 5),
                 d["peer_wq"], d["peer_keys"], d["peer_u"], d["peer_v"], BesideOutputs)
        final_norm(k, "norm1", x, d["final_g"])
        k.recycle()
        second_mixer(k, x)
        peer(k, "peer2", x, d["norm_ffn_w_2"], third(k.mods2, 3), third(k.mods2, 4), third(k.mods2, 5),
             d["peer_wq_2"], d["peer_keys_2"], d["peer_u_2"], d["peer_v_2"])
        final_norm(k, "norm2", x, d["final_norm_w_2"])
        store(k, x, out)


def final_norm(k, name, x, gain):
    norm_modulate(k, name, x, L, gain, None, None, None, None, plain=x)


def store(k, x, out):
    nc = k.nc
    stored = k.sem("stored")
    with nc.Block(no_gpsimd_drain=True) as block:

        @block.sync
        def _(sp):
            sp.dma_start(out, x[:]).then_inc(stored, 16)
            sp.wait_ge(stored, 16)




def by_feature(a):
    t, f = a.shape
    return a.reshape(t, f // P, P).transpose(2, 1, 0)


def columns(a):
    return a.reshape(-1, P).T


def slabs(w):
    kk, n = w.shape
    return w.reshape(kk // P, P, n // P, P).transpose(2, 1, 0, 3)


def rows(w):
    return w.T.reshape(w.shape[1] // P, P, w.shape[0])


def shape_constants():
    f = np.float32
    c = {"ident": np.eye(P, dtype=f)}
    swap = np.zeros((P, P), f)
    swap[(np.arange(P) + P // 2) % P, np.arange(P)] = 1
    c["swap"] = swap
    grid = 64
    quarter = RET_DK // 4
    inv = (np.float32(10000.0) ** (-np.arange(quarter, dtype=f) / f(quarter))).astype(f)
    t = np.arange(L)
    row, col = (t // grid).astype(f), (t % grid).astype(f)
    ang = np.concatenate([row[:, None] * inv, col[:, None] * inv], axis=-1).astype(f)
    cos, sin = np.cos(ang).T.astype(f), np.sin(ang).T.astype(f)
    c["rope_cos"], c["rope_sin"] = np.concatenate([cos, cos]), np.concatenate([-sin, sin])
    c["rope_kcos"], c["rope_ksin"] = c["rope_cos"] * f(K_SCALE), c["rope_sin"] * f(K_SCALE)
    s = np.arange(P)
    c["rel"] = (np.arange(STRIP)[None] - 3 * P - s[:, None]).astype(f)
    c["crel"] = (np.arange(CSTRIP)[None] + P - s[:, None]).astype(f)
    counts = [np.clip(t + w - w // 2, 0, L) - np.clip(t - w // 2, 0, L) for w in POOL_WINDOWS]
    c["inv_count"] = np.broadcast_to(np.stack([f(1) / n.astype(f) for n in counts]), (P, 4, L))
    c["resets"] = np.broadcast_to((t % P != 0).astype(f), (P, L))
    c["time"] = np.broadcast_to(t.astype(f), (P, L))
    masks = []
    for m in (64, 32, 16, 8, 4, 2, 1):
        half, blk = (s // m) % 2, s // (2 * m)
        masks.append((blk[:, None] == blk[None]) & (half[:, None] == 0) & (half[None] == 1))
    masks.append(s[:, None] == s[None])
    c["hg_masks"] = np.stack(masks).transpose(1, 0, 2).astype(np.uint32)
    c["iota"] = np.broadcast_to(np.arange(NKEYS, dtype=f), (P, NKEYS))
    return c


def layout(v):
    w_in = slabs(v["w_in"][0])
    a = {
        "x": by_feature(v["x"][0]),
        "ctx": by_feature(v["ctx"][0]),
        "cond": np.broadcast_to(v["c"][0], (P, D)), "cond_ctx": np.broadcast_to(v["c_ctx"], (P, D)),
        "ada_w": rows(v["ada_w"][0]), "ada_b": columns(v["ada_b"][0]),
        "norm_mix_g": columns(v["norm_mix_g"][0]), "norm_ffn_g": columns(v["norm_ffn_g"][0]),
        "w_in": w_in, "w_ctx": w_in[8:20],
        "pool_w": v["pool_w"][0].transpose(1, 0, 2), "pool_scale": columns(v["pool_scale"][0]),
        "pool_out": slabs(v["pool_out"][0]),
        "ret_decay": np.broadcast_to(v["ret_decay"][0].reshape(1, -1), (P, 2 * RET_HEADS)),
        "ret_norm_g": columns(v["ret_norm_g"][0]),
        "ret_out": slabs(v["ret_out"][0]), "w_out": slabs(v["w_out"][0]),
    }
    def states(a):
        return a.reshape(S5_TILES, P).T

    def s5_blocks(w):
        out = np.zeros((S5_TILES, P, P), w.dtype)
        for g in range(w.shape[0]):
            r, c = (g % 2) * 64, (g % 8) * 16
            out[g // 2, r:r + 64, c:c + 16] = w[g]
        return out

    def experts(u):
        return u.reshape(NKEYS, NKEYS, DC, P).transpose(0, 3, 2, 1)

    a.update({
        "cond_2": np.broadcast_to(v["c_2"][0], (P, D)),
        "ada_w_2": rows(v["ada_w_2"][0]), "ada_b_2": columns(v["ada_b_2"][0]),
        "norm_mix_w_2": columns(v["norm_mix_w_2"][0]), "norm_ffn_w_2": columns(v["norm_ffn_w_2"][0]),
        "w_in_2": slabs(v["w_in_2"][0]), "w_out_2": slabs(v["w_out_2"][0]),
        "hg_lower_bounds": v["hg_lower_bounds_2"].reshape(2, HG_HEADS, P).transpose(2, 0, 1),
        "hg_gnorm_w": columns(v["hg_gnorm_w_2"][0]),
        "s5_a_re": states(v["s5_a_re_2"][0]), "s5_a_im": states(v["s5_a_im_2"][0]),
        "s5_log_dt": states(np.repeat(v["s5_log_dt_2"][0][:, None], 64, axis=1)),
        "s5_b_re": s5_blocks(v["s5_b_re_2"][0]).transpose(2, 0, 1), "s5_b_im": s5_blocks(v["s5_b_im_2"][0]).transpose(2, 0, 1),
        "s5_c_re": s5_blocks(v["s5_c_re_2"][0].transpose(0, 2, 1)).transpose(1, 0, 2),
        "s5_c_im": s5_blocks(v["s5_c_im_2"][0].transpose(0, 2, 1)).transpose(1, 0, 2),
        "s5_d": columns(v["s5_d_2"][0]), "s5_glu_w": slabs(v["s5_glu_w_2"][0]), "s5_glu_b": columns(v["s5_glu_b_2"][0]),
        "peer_wq_2": slabs(v["peer_wq_2"][0]),
        "peer_keys_2": np.stack([v["peer_keys1_2"][0], v["peer_keys2_2"][0]] * HEADS).transpose(2, 0, 1),
        "peer_u_2": experts(v["peer_u_2"][0]), "peer_v_2": v["peer_v_2"][0].reshape(NKEYS, NKEYS, D),
        "final_g": columns(v["final_g"]), "final_norm_w_2": columns(v["final_norm_w_2"]),
        "peer_wq": slabs(v["peer_wq"][0]),
        "peer_keys": v["peer_keys"][0].reshape(2 * HEADS, NKEYS, P).transpose(2, 0, 1),
        "peer_u": experts(v["peer_u"][0]), "peer_v": v["peer_v"][0].reshape(NKEYS, NKEYS, D),
    })
    a.update(shape_constants())
    return a


def kernel(**inputs):
    import concourse.bacc as bacc
    from concourse.bass_utils import run_bass_kernel_spmd

    nc = bacc.Bacc("TRN2", target_bir_lowering=False, num_devices=1)
    arrays = {f"in_{n}": np.ascontiguousarray(a) for n, a in layout({n: np.asarray(a) for n, a in inputs.items()}).items()}
    dram = {n[3:]: nc.dram_tensor(n, a.shape, mybir.dt.from_np(a.dtype), kind="ExternalInput").ap()
            for n, a in arrays.items()}
    out = nc.dram_tensor("out", (P, DC, L), F32, kind="ExternalOutput").ap()
    program(nc, dram, out)
    got = run_bass_kernel_spmd(nc, [arrays], core_ids=[0]).results[0]["out"]
    return np.ascontiguousarray(np.asarray(got).transpose(2, 1, 0).reshape(1, L, D))
```

```python
from contextlib import ExitStack

import numpy as np
import concourse.bass as bass
from concourse import mybir

F32 = mybir.dt.float32
F32R = mybir.dt.float32r
BF16 = mybir.dt.bfloat16
U32 = mybir.dt.uint32
ALU = mybir.AluOpType
ACT = mybir.ActivationFunctionType
AX = mybir.AxisListType

P = 128
D = 1024
DC = D // P
L = 512
LC = 256
EPS = 1e-6


class Core:

    def __init__(self, nc, dram, ctx):
        self.nc, self.dram, self.ctx = nc, dram, ctx
        self.used = []

    def sb(self, name, shape, dt=F32, ctx=None):
        return (ctx or self.ctx).enter_context(self.nc.sbuf_tensor(name, shape, dt))

    def ps(self, name, shape, ctx, dt=F32):
        return ctx.enter_context(self.nc.psum_tensor(name, shape, dt))

    def sem(self, name):
        self.used.append(self.nc.alloc_semaphore(name=name))
        return self.used[-1]

    def recycle(self):
        self.nc.clear_and_free_semaphores(self.used)
        self.nc.all_engine_barrier()
        self.used = []


def f32(ap):
    return ap.bitcast(F32)




class WeightRing:

    def __init__(self, k, name, weights, n0, kc, ctx):
        self.weights, self.n0 = weights, n0
        self.raw = [k.sb(f"{name}_raw{j}", [P, kc, P], F32, ctx) for j in range(2)]
        self.k, self.name, self.landed = k, name, None

    def load(self, sp, i, j):
        sp.dma_start(self.raw[j][:], self.weights[self.n0 + 2 * i + j]).then_inc(self.landed[j], 16)

    def start(self, sp):
        self.landed = [self.k.sem(f"{self.name}_landed{j}") for j in range(2)]
        for j in range(2):
            self.load(sp, 0, j)


class Section:

    def __init__(self, first, last, act_out=None, dve_out=None, modulate=None):
        self.first, self.last = first, last
        self.act_out, self.dve_out, self.modulate = act_out, dve_out, modulate


def gemm(k, name, ring, sections, kc, rhs_hi, rhs_lo, width, at_end=None):
    nc = k.nc
    n0 = sections[0].first
    assert all((s.last - s.first) % 2 == 0 for s in sections)
    with ExitStack() as ctx:
        raw, landed = ring.raw, ring.landed
        hi = [k.sb(f"{name}_hi{j}", [P, kc, P], F32R, ctx) for j in range(2)]
        lo = [k.sb(f"{name}_lo{j}", [P, kc, P], F32R, ctx) for j in range(2)]
        acc = [k.ps(f"{name}_acc{j}", [P, 512], ctx) for j in range(2)]
        hi_ready, lo_ready = k.sem(f"{name}_hi_ready"), k.sem(f"{name}_lo_ready")
        product, taken = k.sem(f"{name}_product"), k.sem(f"{name}_taken")
        if any(s.modulate for s in sections):
            rows = [k.sb(f"{name}_rows{j}", [P, D], F32, ctx) for j in range(2)]
            rows_landed = [k.sem(f"{name}_rows_landed{j}") for j in range(2)]
            modulated = k.sem(f"{name}_modulated")
        block = ctx.enter_context(nc.Block(no_gpsimd_drain=True))

        def each(eng, pair, skip_first=False):
            before, at, m0 = None, 0, 0
            for s in sections:
                pairs = (s.last - s.first) // 2
                if not (skip_first and before is None):
                    pair(at, s, before, 0, m0)
                if pairs > 1:
                    with eng.Fori(1, pairs) as m:
                        pair(at + m, s, s, m, m0)
                before, at = s, at + pairs
                if s.modulate:
                    m0 += pairs

        @block.sync
        def _(sp):
            def pair(i, s, before, m, m0):
                for j in range(2):
                    if before is not None:
                        sp.wait_ge(lo_ready, 2 * i + j - 1)
                        ring.load(sp, i, j)
                    if s.modulate:
                        if not isinstance(m, int) or m or m0:
                            sp.wait_ge(modulated, 2 * (m0 + m) + j - 1)
                        sp.dma_start(rows[j][:], s.modulate[0][2 * m + j]).then_inc(rows_landed[j], 16)

            each(sp, pair)

        @block.tensor
        def _(pe):
            def pair(i, s, before, m, m0):
                for j in range(2):
                    pe.wait_ge(lo_ready, 2 * i + j + 1)
                    if before is not None:
                        pe.wait_ge(taken, 2 * i + j - 1)
                    for c in range(kc):
                        for n, (a, b) in enumerate(((hi, rhs_hi), (hi, rhs_lo), (lo, rhs_hi))):
                            mm = nc.tensor.matmul(acc[j][:, 0:width], a[j][:, c, :], b[:, c, :],
                                                  start=(c == 0 and n == 0), stop=(c == kc - 1 and n == 2))
                    mm.then_inc(product, 1)

            each(pe, pair)

        def take_out(eng, emit, i, j, tile):
            if emit is None:
                return
            eng.wait_ge(product, 2 * i + j + 1)
            emit(eng, tile, acc[j][:, 0:width]).then_inc(taken, 1)

        def last_tile(before, s, m):
            return 2 * m - 1 if before is s else before.last - before.first - 1

        @block.scalar
        def _(act):
            def split_hi(i, j, before):
                act.wait_ge(landed[j], 16 * (i + 1))
                if before is not None:
                    act.wait_ge(product, 2 * i + j - 1)
                nc.scalar.copy(hi[j][:], raw[j][:]).then_inc(hi_ready, 1)

            def pair(i, s, before, m, m0):
                split_hi(i, 0, before)
                if before is not None:
                    take_out(act, before.act_out, i - 1, 1, last_tile(before, s, m))
                split_hi(i, 1, before)
                take_out(act, s.act_out, i, 0, 2 * m)

            each(act, pair)
            s = sections[-1]
            take_out(act, s.act_out, (s.last - n0) // 2 - 1, 1, s.last - s.first - 1)

        @block.vector
        def _(dve):
            def split_lo(i, j):
                dve.wait_ge(hi_ready, 2 * i + j + 1)
                nc.vector.tensor_tensor(lo[j][:], raw[j][:], f32(hi[j][:]), ALU.subtract).then_inc(lo_ready, 1)

            def modulate(s, j, m, m0):
                if s.modulate:
                    _, cond, out = s.modulate
                    dve.wait_ge(rows_landed[j], 16 * (m0 + m + 1))
                    nc.vector.scalar_tensor_tensor(rows[j][:], rows[j][:], 1.0, cond, ALU.mult, ALU.mult,
                                                   accum_out=out(2 * m + j)).then_inc(modulated, 1)

            def pair(i, s, before, m, m0):
                split_lo(i, 0)
                if before is not None:
                    take_out(dve, before.dve_out, i - 1, 1, last_tile(before, s, m))
                modulate(s, 0, m, m0)
                split_lo(i, 1)
                take_out(dve, s.dve_out, i, 0, 2 * m)
                modulate(s, 1, m, m0)

            each(dve, pair)
            s = sections[-1]
            take_out(dve, s.dve_out, (s.last - n0) // 2 - 1, 1, s.last - s.first - 1)
            if at_end:
                dve.wait_ge(modulated, sum(s.last - s.first for s in sections if s.modulate))
                at_end()




def load_all(k, name, pairs, later=(), later_loaded=None):
    nc = k.nc
    loaded = k.sem(f"{name}_loaded")
    with nc.Block(no_gpsimd_drain=True) as block:

        @block.sync
        def _(sp):
            for dst, src in pairs:
                sp.dma_start(dst[:], src).then_inc(loaded, 16)
            for dst, src in later:
                sp.dma_start(dst[:], src).then_inc(later_loaded, 16)
            sp.wait_ge(loaded, 16 * len(pairs))


def fill_constants(k, pairs):
    nc = k.nc
    with nc.Block(no_gpsimd_drain=True) as block:

        @block.vector
        def _(dve):
            for dst, value in pairs:
                nc.vector.memset(dst[:], value)


def start(k, loads, conds, weights, bias, out, tiles):
    nc = k.nc
    NR = 4
    with ExitStack() as ctx:
        rows = [k.sb(f"ada_rows{j}", [P, D], F32, ctx) for j in range(NR)]
        loaded, cond_loaded, silu_done = k.sem("ada_loaded"), k.sem("ada_cond_loaded"), k.sem("ada_silu")
        landed = [k.sem(f"ada_landed{j}") for j in range(NR)]
        modulated = k.sem("ada_modulated")
        block = ctx.enter_context(nc.Block(no_gpsimd_drain=True))

        @block.sync
        def _(sp):
            for dst, src in conds:
                sp.dma_start(dst[:], src).then_inc(cond_loaded, 16)
            for j in range(NR):
                sp.dma_start(rows[j][:], weights[j]).then_inc(landed[j], 16)
            for dst, src in loads:
                sp.dma_start(dst[:], src).then_inc(loaded, 16)
            with sp.Fori(1, tiles // NR) as i:
                for j in range(NR):
                    sp.wait_ge(modulated, NR * i + j - NR + 1)
                    sp.dma_start(rows[j][:], weights[NR * i + j]).then_inc(landed[j], 16)
            sp.wait_ge(loaded, 16 * len(loads))

        @block.scalar
        def _(act):
            act.wait_ge(cond_loaded, 16 * len(conds))
            for dst, _ in conds:
                nc.scalar.activation(dst[:], dst[:], ACT.Silu).then_inc(silu_done, 1)

        @block.vector
        def _(dve):
            nc.vector.memset(k.ones_model[:], 1.0 / D)
            dve.wait_ge(silu_done, len(conds))
            with dve.Fori(0, tiles // NR) as i:
                for j in range(NR):
                    dve.wait_ge(landed[j], 16 * (i + 1))
                    nc.vector.scalar_tensor_tensor(rows[j][:], rows[j][:], 1.0, conds[0][0][:], ALU.mult, ALU.mult,
                                                   accum_out=out[:, bass.ds(NR * i + j, 1), 0]).then_inc(modulated, 1)
            dve.wait_ge(modulated, tiles)
            dve.wait_ge(loaded, 16 * len(loads))
            nc.vector.tensor_tensor(out[:, 0:tiles, 0], out[:, 0:tiles, 0], bias[:, 0:tiles], ALU.add)


def norm_modulate(k, name, x, width, gain, shift, out_hi, out_lo, scale=None, plain=None, ring=None,
                  later=None):
    nc = k.nc
    with ExitStack() as ctx:
        gain_in = gain
        gain = k.sb(f"{name}_gain", [P, DC], F32, ctx)
        gain_loaded = k.sem(f"{name}_gain_loaded")
        sq = k.sb(f"{name}_sq", [P, DC, width], F32, ctx)
        h = sq
        root = k.sb(f"{name}_root", [P, width], F32, ctx)
        rstd = k.sb(f"{name}_rstd", [P, width], F32, ctx)
        coef = k.sb(f"{name}_coef", [P, DC], F32, ctx)
        mean = k.ps(f"{name}_mean", [P, width], ctx)
        squared, summed = k.sem(f"{name}_squared"), k.sem(f"{name}_summed")
        paired = k.sem(f"{name}_paired")
        guarded, rooted = k.sem(f"{name}_guarded"), k.sem(f"{name}_rooted")
        inverted, coef_ready = k.sem(f"{name}_inverted"), k.sem(f"{name}_coef_ready")
        scaled, hi_ready = k.sem(f"{name}_scaled"), k.sem(f"{name}_hi_ready")
        block = ctx.enter_context(nc.Block(no_gpsimd_drain=True))

        @block.sync
        def _(sp):
            sp.dma_start(gain[:], gain_in).then_inc(gain_loaded, 16)
            if ring is not None:
                ring.start(sp)
            if later is not None:
                (dst, src), loaded = later
                sp.dma_start(dst[:], src).then_inc(loaded, 16)

        @block.scalar
        def _(act):
            for c in range(DC):
                nc.scalar.activation(sq[:, c, :], x[:, c, :], ACT.Square).then_inc(squared, 1)
            act.wait_ge(guarded, 1)
            nc.scalar.activation(root[:], rstd[:], ACT.Sqrt).then_inc(rooted, 1)
            if plain is None:
                for c in range(DC):
                    act.wait_ge(scaled, c + 1)
                    nc.scalar.activation(out_hi[:, c, :], h[:, c, :], ACT.Identity,
                                         bias=shift[:, c:c + 1]).then_inc(hi_ready, 1)

        @block.tensor
        def _(pe):
            pe.wait_ge(paired, DC - 1)
            nc.tensor.matmul(mean[:], k.ones_model[:], sq[:, DC - 1, :], start=True, stop=True).then_inc(summed, 1)

        @block.vector
        def _(dve):
            for c in range(1, DC):
                dve.wait_ge(squared, c + 1)
                if c > 1:
                    dve.wait_ge(paired, c - 1)
                nc.vector.tensor_tensor(sq[:, c, :], sq[:, c, :], sq[:, c - 1, :], ALU.add).then_inc(paired, 1)
            dve.wait_ge(gain_loaded, 16)
            if scale is not None:
                nc.vector.scalar_tensor_tensor(coef[:], scale, 1.0, gain[:], ALU.add, ALU.mult).then_inc(coef_ready, 1)
            else:
                nc.vector.tensor_copy(coef[:], gain[:]).then_inc(coef_ready, 1)
            dve.wait_ge(summed, 1)
            nc.vector.tensor_scalar(rstd[:], mean[:], EPS, None, ALU.add).then_inc(guarded, 1)
            dve.wait_ge(rooted, 1)
            nc.vector.reciprocal(rstd[:], root[:]).then_inc(inverted, 1)
            dve.wait_ge(coef_ready, 1)
            dve.wait_ge(inverted, 1)
            for c in range(DC):
                nc.vector.scalar_tensor_tensor((h if plain is None else plain)[:, c, :], x[:, c, :], coef[:, c:c + 1],
                                               rstd[:], ALU.mult, ALU.mult).then_inc(scaled, 1)
            if plain is None:
                for c in range(DC):
                    dve.wait_ge(hi_ready, c + 1)
                    nc.vector.scalar_tensor_tensor(out_lo[:, c, :], h[:, c, :], shift[:, c:c + 1], f32(out_hi[:, c, :]),
                                                   ALU.add, ALU.subtract)


def activate(nc, dst, func):
    return lambda act, n, psum: nc.scalar.activation(dst[:, bass.ds(n, 1), :], psum, func)


def split(k, name, src, hi, lo, chunks, ring, small=None):
    nc = k.nc
    hi_ready, loaded = k.sem(f"{name}_hi_ready"), k.sem(f"{name}_loaded")
    with nc.Block(no_gpsimd_drain=True) as block:

        @block.sync
        def _(sp):
            ring.start(sp)
            if small:
                sp.dma_start(small[0][:], small[1]).then_inc(loaded, 16)
                sp.wait_ge(loaded, 16)

        @block.scalar
        def _(act):
            for c in range(chunks):
                nc.scalar.copy(hi[:, c, :], src[:, c, :]).then_inc(hi_ready, 1)

        @block.vector
        def _(dve):
            for c in range(chunks):
                dve.wait_ge(hi_ready, c + 1)
                nc.vector.tensor_tensor(lo[:, c, :], src[:, c, :], f32(hi[:, c, :]), ALU.subtract)


def to_rows(k, name, src, dst, tiles, blocks):
    nc = k.nc
    with ExitStack() as ctx:
        turn = [k.ps(f"{name}_turn{j}", [P, blocks, P], ctx) for j in range(2)]
        turned, copied = k.sem(f"{name}_turned"), k.sem(f"{name}_copied")
        block = ctx.enter_context(nc.Block(no_gpsimd_drain=True))

        @block.tensor
        def _(pe):
            for f in range(tiles):
                if f >= 2:
                    pe.wait_ge(copied, f - 1)
                for b in range(blocks):
                    mm = nc.tensor.transpose(turn[f % 2][:, b, :], src[:, f, b * P:(b + 1) * P], k.ident[:])
                mm.then_inc(turned, 1)

        @block.scalar
        def _(act):
            for f in range(tiles):
                act.wait_ge(turned, f + 1)
                nc.scalar.copy(dst[:, :, f * P:(f + 1) * P], turn[f % 2][:]).then_inc(copied, 1)


def head_norm(k, name, y, heads, per, ones, center, gain, gate, hi, lo, first, ring=None, free=None):
    nc = k.nc
    n = heads * per
    with ExitStack() as ctx:
        sq = free if free is not None else k.sb(f"{name}_sq", [P, n, L], F32, ctx)
        rstd = k.sb(f"{name}_rstd", [P, heads, L], F32, ctx)
        stat = [k.ps(f"{name}_stat{j}", [P, L], ctx) for j in range(2 * heads)]
        mean_done, centered = k.sem(f"{name}_mean_done"), k.sem(f"{name}_centered")
        squared, summed = k.sem(f"{name}_squared"), k.sem(f"{name}_summed")
        guarded, rooted = k.sem(f"{name}_guarded"), k.sem(f"{name}_rooted")
        inverted, scaled = k.sem(f"{name}_inverted"), k.sem(f"{name}_scaled")
        gated, hi_ready = k.sem(f"{name}_gated"), k.sem(f"{name}_hi_ready")
        block = ctx.enter_context(nc.Block(no_gpsimd_drain=True))

        @block.sync
        def _(sp):
            if ring is not None:
                ring.start(sp)

        @block.tensor
        def _(pe):
            if center:
                for h in range(heads):
                    for c in range(per):
                        mm = nc.tensor.matmul(stat[h][:], ones[:], y[:, h * per + c, :],
                                              start=(c == 0), stop=(c == per - 1))
                    mm.then_inc(mean_done, 1)
            for h in range(heads):
                pe.wait_ge(squared, h + 1)
                for c in range(per):
                    mm = nc.tensor.matmul(stat[heads + h][:], ones[:], sq[:, h * per + c, :],
                                          start=(c == 0), stop=(c == per - 1))
                mm.then_inc(summed, 1)

        @block.scalar
        def _(act):
            for h in range(heads):
                if center:
                    act.wait_ge(centered, per * (h + 1))
                nc.scalar.activation(sq[:, h * per:(h + 1) * per, :], y[:, h * per:(h + 1) * per, :],
                                     ACT.Square).then_inc(squared, 1)
            for h in range(heads):
                act.wait_ge(guarded, h + 1)
                nc.scalar.activation(rstd[:, h, :], rstd[:, h, :], ACT.Sqrt).then_inc(rooted, 1)
            for c in range(n):
                act.wait_ge(gated, c + 1)
                nc.scalar.copy(hi[:, first + c, :], y[:, c, :]).then_inc(hi_ready, 1)

        @block.vector
        def _(dve):
            if center:
                for h in range(heads):
                    dve.wait_ge(mean_done, h + 1)
                    for c in range(h * per, (h + 1) * per):
                        nc.vector.tensor_tensor(y[:, c, :], y[:, c, :], stat[h][:], ALU.subtract).then_inc(centered, 1)
            for h in range(heads):
                dve.wait_ge(summed, h + 1)
                nc.vector.tensor_scalar(rstd[:, h, :], stat[heads + h][:], EPS, None, ALU.add).then_inc(guarded, 1)
            for h in range(heads):
                dve.wait_ge(rooted, h + 1)
                nc.vector.reciprocal(rstd[:, h, :], rstd[:, h, :]).then_inc(inverted, 1)
            for h in range(heads):
                dve.wait_ge(inverted, h + 1)
                for c in range(h * per, (h + 1) * per):
                    nc.vector.tensor_tensor(sq[:, c, :], y[:, c, :], rstd[:, h, :], ALU.mult).then_inc(scaled, 1)
            for c in range(n):
                dve.wait_ge(scaled, c + 1)
                nc.vector.scalar_tensor_tensor(y[:, c, :], sq[:, c, :], gain(c), gate[:, c, :],
                                               ALU.mult, ALU.mult).then_inc(gated, 1)
            for c in range(n):
                dve.wait_ge(hi_ready, c + 1)
                nc.vector.tensor_tensor(lo[:, first + c, :], y[:, c, :], f32(hi[:, first + c, :]), ALU.subtract)



POOL_WINDOWS = (2, 4, 8, 16)
RET_HEADS = 4
RET_DK = 128
K_SCALE = RET_DK ** -0.5
STRIP = 3 * P + L
CSTRIP = P + L


def rope(k, name, x, cos, sin, heads):
    nc = k.nc
    with ExitStack() as ctx:
        a = [k.sb(f"{name}_a{j}", [P, L], F32, ctx) for j in range(2)]
        b = [k.sb(f"{name}_b{j}", [P, L], F32, ctx) for j in range(2)]
        swapped = [k.ps(f"{name}_swapped{j}", [P, L], ctx) for j in range(2)]
        swap_done, parts, rotated = k.sem(f"{name}_swap"), k.sem(f"{name}_parts"), k.sem(f"{name}_rotated")
        block = ctx.enter_context(nc.Block(no_gpsimd_drain=True))

        @block.tensor
        def _(pe):
            for h in range(heads):
                if h >= 2:
                    pe.wait_ge(parts, 2 * (h - 1))
                nc.tensor.matmul(swapped[h % 2][:], k.swap[:], x[:, h, :], start=True, stop=True).then_inc(swap_done, 1)

        @block.vector
        def _(dve):
            for h in range(heads):
                dve.wait_ge(swap_done, h + 1)
                if h >= 2:
                    dve.wait_ge(rotated, h - 1)
                nc.vector.tensor_tensor(a[h % 2][:], x[:, h, :], cos, ALU.mult).then_inc(parts, 1)
                nc.vector.tensor_tensor(b[h % 2][:], swapped[h % 2][:], sin, ALU.mult).then_inc(parts, 1)
                dve.wait_ge(parts, 2 * h + 2)
                nc.vector.tensor_tensor(x[:, h, :], a[h % 2][:], b[h % 2][:], ALU.add).then_inc(rotated, 1)


class DecayTables:

    def __init__(self, k, decay, rel, crel, strip, cstrip, loaded, ctx):
        n = 2 * RET_HEADS
        self.k, self.nc, self.decay, self.rel, self.crel = k, k.nc, decay, rel, crel
        self.strip, self.cstrip, self.loaded = strip, cstrip, loaded
        self.t = k.sb("decay_t", [P, 8, n], F32, ctx)
        self.ahead = k.sb("decay_ahead", [P, STRIP], F32, ctx)
        self.behind = k.sb("decay_behind", [P, STRIP], F32, ctx)
        self.to_end = k.sb("decay_to_end", [P, CSTRIP], F32, ctx)
        self.expo = k.sb("decay_expo", [P, STRIP], F32, ctx)
        self.cexp = [k.sb(f"decay_cexp{j}", [P, CSTRIP], F32, ctx) for j in range(2)]
        self.step, self.exp_done = k.sem("decay_step"), k.sem("decay_exp")
        self.ready, self.taken = k.sem("decay_ready"), k.sem("decay_taken")
        self.mag, self.z, self.w, self.w2, self.total, self.lg, self.den = (self.t[:, j, :] for j in range(7))
        self.steps = 0

    def scalar_begin(self, act):
        act.wait_ge(self.step, 1)
        self.nc.scalar.activation(self.z, self.mag, ACT.Exp, scale=-1.0).then_inc(self.exp_done, 1)

    def scalar(self, act, h):
        act.wait_ge(self.ready, 3 * h + 1)
        self.nc.scalar.activation(self.strip[:, h, :], self.expo[:], ACT.Exp).then_inc(self.taken, 1)
        act.wait_ge(self.ready, 3 * h + 3)
        for j in range(2):
            self.nc.scalar.activation(self.cexp[j][:], self.cexp[j][:], ACT.Exp).then_inc(self.taken, 1)

    def after(self, ins):
        self.steps += 1
        ins.then_inc(self.step, 1)
        self.nc.vector.wait_ge(self.step, self.steps)

    def vector_begin(self, dve):
        V, after, w, w2, z, den, total = self.nc.vector, self.after, self.w, self.w2, self.z, self.den, self.total
        dve.wait_ge(self.loaded, 48)
        after(V.scalar_tensor_tensor(self.mag, self.decay[:], -1.0, self.decay[:], ALU.mult, ALU.max))
        after(V.tensor_scalar(self.ahead[:], self.rel[:], 0.0, None, ALU.max))
        after(V.tensor_scalar(self.behind[:], self.rel[:], 0.0, -1.0, ALU.min, ALU.mult))
        after(V.tensor_scalar(self.to_end[:], self.crel[:], -1.0, float(L + LC), ALU.mult, ALU.add))
        dve.wait_ge(self.exp_done, 1)
        after(V.tensor_scalar(den, z, 2.0, None, ALU.add))
        after(V.reciprocal(den, den))
        after(V.tensor_tensor(w, z, den, ALU.mult))
        after(V.tensor_tensor(w2, w, w, ALU.mult))
        after(V.tensor_scalar(total, w2, 1.0 / 17, 1.0 / 15, ALU.mult, ALU.add))
        for odd in (13, 11, 9, 7, 5, 3, 1):
            after(V.tensor_tensor(total, total, w2, ALU.mult))
            after(V.tensor_scalar(total, total, 1.0 / odd, None, ALU.add))
        after(V.tensor_tensor(total, total, w, ALU.mult))
        after(V.tensor_scalar(self.lg, self.decay[:], 0.0, None, ALU.min))
        after(V.scalar_tensor_tensor(self.lg, total, -2.0, self.lg, ALU.mult, ALU.add))

    def exponents(self, dve, h):
        V = self.nc.vector
        f, b = self.lg[:, h:h + 1], self.lg[:, RET_HEADS + h:RET_HEADS + h + 1]
        if h >= 1:
            dve.wait_ge(self.taken, 3 * h)
        self.after(V.tensor_scalar(self.expo[:], self.ahead[:], f, None, ALU.mult))
        V.scalar_tensor_tensor(self.expo[:], self.behind[:], b, self.expo[:], ALU.mult, ALU.add).then_inc(self.ready, 1)
        V.tensor_scalar(self.cexp[0][:], self.crel[:], f, None, ALU.mult).then_inc(self.ready, 1)
        V.tensor_scalar(self.cexp[1][:], self.to_end[:], b, None, ALU.mult).then_inc(self.ready, 1)

    def join(self, dve, h):
        dve.wait_ge(self.taken, 3 * h + 3)
        self.after(self.nc.vector.tensor_tensor(self.cstrip[:, h, :], self.cexp[0][:], self.cexp[1][:], ALU.add))


def retention(k, q, kk, kc, v, vc, tables, y):
    nc = k.nc
    NS, NC = L // P, LC // P
    n = NS + NC
    with ExitStack() as ctx:
        w = k.sb("ret_w", [P, 4, L], F32, ctx)
        score = [k.ps(f"ret_score{j}", [P, L], ctx) for j in range(4)]
        out = [k.ps(f"ret_out{j}", [P, L], ctx) for j in range(4)]
        scored, weighted = k.sem("ret_scored"), k.sem("ret_weighted")
        used, summed, taken = k.sem("ret_used"), k.sem("ret_summed"), k.sem("ret_taken")
        block = ctx.enter_context(nc.Block(no_gpsimd_drain=True))
        units = [(h, s) for h in range(RET_HEADS) for s in range(n)]
        strip, cstrip = tables.strip, tables.cstrip

        @block.tensor
        def _(pe):
            def weigh(u):
                h, s = units[u]
                pe.wait_ge(weighted, u + 1)
                if s == 0 and h >= 2:
                    pe.wait_ge(taken, 2 * (h - 1))
                for e in range(2):
                    val = v[:, s, (2 * h + e) * P:(2 * h + e + 1) * P] if s < NS else \
                        vc[:, s - NS, (2 * h + e) * P:(2 * h + e + 1) * P]
                    mm = nc.tensor.matmul(out[2 * (h % 2) + e][:], val, w[:, u % 4, :], start=(s == 0),
                                          stop=(s == n - 1), skip_group_check=True)
                mm.then_inc(used, 1)

            for u, (h, s) in enumerate(units):
                if u >= 4:
                    pe.wait_ge(weighted, u - 3)
                key = kk[:, h, s * P:(s + 1) * P] if s < NS else kc[:, h, (s - NS) * P:(s - NS + 1) * P]
                nc.tensor.matmul(score[u % 4][:], key, q[:, h, :], start=True, stop=True).then_inc(scored, 1)
                if u >= 2:
                    weigh(u - 2)
            weigh(len(units) - 2)
            weigh(len(units) - 1)

        @block.vector
        def _(dve):
            tables.vector_begin(dve)
            tables.exponents(dve, 0)
            tables.join(dve, 0)
            for u, (h, s) in enumerate(units):
                if h + 1 < RET_HEADS and s == 1:
                    tables.exponents(dve, h + 1)
                if h + 1 < RET_HEADS and s == n - 1:
                    tables.join(dve, h + 1)
                dve.wait_ge(scored, u + 1)
                if u >= 4:
                    dve.wait_ge(used, u - 3)
                at = (NS - 1 - s) * P if s < NS else (NC - 1 - (s - NS)) * P
                table = strip[:, h, at:at + L] if s < NS else cstrip[:, h, at:at + L]
                nc.vector.tensor_tensor(w[:, u % 4, :], score[u % 4][:], table, ALU.mult).then_inc(weighted, 1)

        @block.scalar
        def _(act):
            tables.scalar_begin(act)
            tables.scalar(act, 0)
            for h in range(RET_HEADS):
                if h + 1 < RET_HEADS:
                    tables.scalar(act, h + 1)
                act.wait_ge(used, n * (h + 1))
                for e in range(2):
                    nc.scalar.copy(y[:, 2 * h + e, :], out[2 * (h % 2) + e][:]).then_inc(taken, 1)


def pooling(k, p, inv_count, weights, gain, hi, lo, ring):
    nc = k.nc
    G = len(POOL_WINDOWS)
    PAD = max(POOL_WINDOWS)
    W = L + 2 * PAD
    with ExitStack() as ctx:
        s = [k.sb(f"pool_s{j}", [P, G, W], F32, ctx) for j in range(2)]
        d = k.sb("pool_d", [P, G, L], F32, ctx)
        mixed = k.sb("pool_mixed", [P, G, L], F32, ctx)
        prod = [k.ps(f"pool_prod{j}", [P, L], ctx) for j in range(G)]
        step, d_ready = k.sem("pool_step"), k.sem("pool_d_ready")
        product, mix_done, hi_ready = k.sem("pool_product"), k.sem("pool_mix"), k.sem("pool_hi")
        block = ctx.enter_context(nc.Block(no_gpsimd_drain=True))

        @block.sync
        def _(sp):
            ring.start(sp)

        @block.vector
        def _(dve):
            steps = 0

            def after(ins):
                nonlocal steps
                steps += 1
                ins.then_inc(step, 1)
                dve.wait_ge(step, steps)

            nc.vector.memset(s[0][:], 0.0).then_inc(step, 1)
            nc.vector.memset(s[1][:], 0.0).then_inc(step, 1)
            steps = 2
            dve.wait_ge(step, steps)
            after(nc.vector.tensor_copy(s[0][:, :, PAD:PAD + L], p[:]))
            for j in range(G):
                a, b, lag = s[j % 2], s[(j + 1) % 2], 2 ** j
                after(nc.vector.tensor_tensor(b[:, j:G, lag:W], a[:, j:G, lag:W], a[:, j:G, 0:W - lag], ALU.add))
                w = 2 ** (j + 1)
                at = PAD + w - w // 2 - 1
                after(nc.vector.tensor_tensor(d[:, j, :], b[:, j, at:at + L], inv_count[:, j, :], ALU.mult))
                nc.vector.tensor_tensor(d[:, j, :], d[:, j, :], p[:, j, :], ALU.subtract).then_inc(d_ready, 1)
            for g in range(G):
                dve.wait_ge(product, g + 1)
                nc.vector.tensor_scalar(mixed[:, g, :], prod[g][:], gain[:, g:g + 1], None, ALU.mult).then_inc(mix_done, 1)
            for g in range(G):
                dve.wait_ge(hi_ready, g + 1)
                nc.vector.tensor_tensor(lo[:, g, :], mixed[:, g, :], f32(hi[:, g, :]), ALU.subtract)

        @block.tensor
        def _(pe):
            for g in range(G):
                pe.wait_ge(d_ready, g + 1)
                nc.tensor.matmul(prod[g][:], weights[:, g, :], d[:, g, :], start=True, stop=True).then_inc(product, 1)

        @block.scalar
        def _(act):
            for g in range(G):
                act.wait_ge(mix_done, g + 1)
                nc.scalar.copy(hi[:, g, :], mixed[:, g, :]).then_inc(hi_ready, 1)



HEADS = 8
NKEYS = 128
TOPK = 16
PAIRS = HEADS * TOPK
LOWEST = -3.4028234663852886e38
TB = L // P
HALF = P // 2
PAD = 8
PIECE = NKEYS // 16


class Chooser:

    SCORES, PAIRED, BEST, PLACED = 1 + 2 + 4, 2 + 2 + 1 + 1, 1 + 2 + 1 + 1, 2 + 2 + 2 + 2 + 2

    def __init__(self, k, name, ctx):
        sb = lambda n, shape, dt=F32: k.sb(f"{name}_{n}", shape, dt, ctx)
        self.k, self.nc = k, k.nc
        self.step = k.sem(f"{name}_step")
        self.s = sb("s", [P, 2, NKEYS])
        self.top, self.index = sb("top", [P, 2, TOPK]), sb("index", [P, 2, TOPK], U32)
        self.index_f = sb("index_f", [P, 2, TOPK])
        self.cand = sb("cand", [P, TOPK, TOPK])
        self.best, self.pos = sb("best", [P, TOPK]), sb("pos", [P, TOPK], U32)
        self.place, self.place_f = sb("place", [P, 2, TOPK], U32), sb("place_f", [P, 2, TOPK])
        self.pick = [self.cand[:], self.s[:].rearrange("p r (a b) -> p (r a) b", b=TOPK)]
        self.n = 0

    def after(self, *inss):
        for ins in inss:
            ins.then_inc(self.step, 1)
        self.n += len(inss)
        self.nc.vector.wait_ge(self.step, self.n)

    def scores(self, s_all, tb, h):
        V, s, top, index = self.nc.vector, self.s, self.top, self.index
        self.n = 0
        self.after(V.tensor_copy(s[:], s_all[:, bass.ds(tb * (2 * HEADS) + h * 2, 2), :]))
        self.after(*[V.max(top[:, r, 0:8], s[:, r, :]) for r in range(2)])
        self.after(*[V.max_index(index[:, r, 0:8], top[:, r, 0:8], s[:, r, :]) for r in range(2)])
        self.after(*[V.match_replace(s[:, r, :], top[:, r, 0:8], s[:, r, :], LOWEST) for r in range(2)])
        assert self.n == self.SCORES

    def paired(self):
        V, rest, top, index = self.nc.vector, self.s, self.top, self.index
        grid = [P, TOPK, TOPK]
        self.after(*[V.max(top[:, r, 8:16], rest[:, r, :]) for r in range(2)])
        self.after(*[V.max_index(index[:, r, 8:16], top[:, r, 8:16], rest[:, r, :]) for r in range(2)],
                   V.tensor_tensor(self.cand[:], top[:, 0, :].unsqueeze(2).broadcast_to(grid),
                                   top[:, 1, :].unsqueeze(1).broadcast_to(grid), ALU.add))
        self.after(V.tensor_copy(self.index_f[:], index[:]))

    def sixteen(self):
        V = self.nc.vector
        cand = self.cand[:].rearrange("p a b -> p (a b)")
        best, pos = self.best, self.pos
        self.after(V.max(best[:, 0:8], cand))
        self.after(V.max_index(pos[:, 0:8], best[:, 0:8], cand))
        self.after(V.match_replace(cand, best[:, 0:8], cand, LOWEST))
        self.after(V.max(best[:, 8:16], cand))
        self.after(V.max_index(pos[:, 8:16], best[:, 8:16], cand))

    def placed(self, h, iota, found, shifted):
        V = self.nc.vector
        grid = [P, TOPK, TOPK]
        self.after(V.tensor_scalar(self.place[:, 0, :], self.pos[:], 4, None, ALU.logical_shift_right),
                   V.tensor_scalar(self.place[:, 1, :], self.pos[:], 15, None, ALU.bitwise_and))
        self.after(V.tensor_copy(self.place_f[:], self.place[:]),
                   V.tensor_scalar(shifted[:, bass.ds(h, 1), :], self.best[:].unsqueeze(1), self.best[:, 0:1], None, ALU.subtract))
        self.after(*[V.tensor_tensor(self.pick[r], self.place_f[:, r, :].unsqueeze(2).broadcast_to(grid),
                                     iota[:, 0:TOPK].unsqueeze(1).broadcast_to(grid), ALU.is_equal) for r in range(2)])
        self.after(*[V.tensor_tensor(self.pick[r], self.pick[r],
                                     self.index_f[:, r, :].unsqueeze(1).broadcast_to(grid), ALU.mult) for r in range(2)])
        self.after(*[V.tensor_reduce(found[:, r, bass.ds(h * TOPK, TOPK)], self.pick[r], AX.X, ALU.add) for r in range(2)])
        V.sem_clear(self.step)


def queries(k, name, wq, h_hi, h_lo, keys, iota, s_all, found, shifted, u, u_raw, u_landed, raw, landed, keys_loaded):
    nc = k.nc
    with ExitStack() as ctx:
        hi = [k.sb(f"{name}_hi{j}", [P, DC, P], F32R, ctx) for j in range(2)]
        lo = [k.sb(f"{name}_lo{j}", [P, DC, P], F32R, ctx) for j in range(2)]
        q = [k.sb(f"{name}_q{j}", [P, L], F32, ctx) for j in range(2)]
        acc = [k.ps(f"{name}_acc{j}", [P, L], ctx) for j in range(2)]
        score = [k.ps(f"{name}_score{j}", [P, TB, NKEYS], ctx) for j in range(2)]
        sem = lambda n: k.sem(f"{name}_{n}")
        hi_ready, lo_ready, product = sem("hi_ready"), sem("lo_ready"), sem("product")
        q_ready, scored, s_ready = sem("q_ready"), sem("scored"), sem("s_ready")
        chooser = Chooser(k, f"{name}_choose", ctx)
        FREE = 2
        block = ctx.enter_context(nc.Block(no_gpsimd_drain=True))

        @block.sync
        def _(sp):
            with sp.Fori(1, HEADS) as i:
                for j in range(2):
                    sp.wait_ge(lo_ready, 2 * i + j + 1)
                    sp.dma_start(raw[j][:], wq[2 * i + j]).then_inc(landed[j], 16)
            for j in range(4):
                sp.dma_start(u_raw[j][:], u[j]).then_inc(u_landed[j], 16)

        @block.tensor
        def _(pe):
            pe.sem_inc(product, FREE)

            def products(i, j):
                pe.wait_ge(lo_ready, FREE + 2 * i + j + 1)
                pe.wait_ge(q_ready, 2 * i + j + 1)
                for c in range(DC):
                    for m, (a, b) in enumerate(((hi, h_hi), (hi, h_lo), (lo, h_hi))):
                        mm = nc.tensor.matmul(acc[j][:], a[j][:, c, :], b[:, c, :],
                                              start=(c == 0 and m == 0), stop=(c == DC - 1 and m == 2))
                mm.then_inc(product, 1)

            def scores(h):
                pe.wait_ge(q_ready, FREE + 2 * h + 2)
                pe.wait_ge(s_ready, 2 * h + 2)
                for r in range(2):
                    for tb in range(TB):
                        mm = nc.tensor.matmul(score[r][:, tb, :], q[r][:, tb * P:(tb + 1) * P],
                                              keys[:, bass.ds(2 * h + r, 1), :].rearrange("p o k -> p (o k)"),
                                              start=True, stop=True)
                mm.then_inc(scored, 1)

            products(0, 0)
            products(0, 1)
            pe.wait_ge(keys_loaded, 16)
            with pe.Fori(1, HEADS) as i:
                products(i, 0)
                scores(i - 1)
                products(i, 1)
            scores(HEADS - 1)

        @block.scalar
        def _(act):
            act.sem_inc(q_ready, FREE)
            act.sem_inc(s_ready, 2)

            def split_hi(i, j):
                act.wait_ge(landed[j], 16 * (i + 1))
                act.wait_ge(product, 2 * i + j + 1)
                nc.scalar.copy(hi[j][:], raw[j][:]).then_inc(hi_ready, 1)

            def query(i, j):
                act.wait_ge(product, FREE + 2 * i + j + 1)
                nc.scalar.copy(q[j][:], acc[j][:]).then_inc(q_ready, 1)

            def take_scores(h):
                act.wait_ge(scored, h + 1)
                for r in range(2):
                    nc.scalar.copy(s_all[:].rearrange("p (tb hp) k -> p tb hp k", tb=TB)[:, :, bass.ds(2 * h + r, 1), :],
                                   score[r][:].unsqueeze(2)).then_inc(s_ready, 1)

            split_hi(0, 0)
            split_hi(0, 1)
            query(0, 0)
            with act.Fori(1, HEADS) as i:
                split_hi(i, 0)
                query(i - 1, 1)
                split_hi(i, 1)
                take_scores(i - 1)
                query(i, 0)
            query(HEADS - 1, 1)
            take_scores(HEADS - 1)

        @block.vector
        def _(dve):
            dve.sem_inc(lo_ready, FREE)

            def split_lo(i, j):
                dve.wait_ge(hi_ready, 2 * i + j + 1)
                nc.vector.tensor_tensor(lo[j][:], raw[j][:], f32(hi[j][:]), ALU.subtract).then_inc(lo_ready, 1)

            for i in range(2):
                split_lo(i, 0)
                split_lo(i, 1)
            with dve.Fori(2, HEADS) as i:
                dve.wait_ge(s_ready, 2 * i)
                split_lo(i, 0)
                chooser.scores(s_all, 0, i - 2)
                chooser.paired()
                split_lo(i, 1)
                chooser.sixteen()
                chooser.placed(i - 2, iota, found, shifted)


def expert_inputs(k, name, u, h_hi, h_lo, iota, s_all, found, shifted, acts, table, held,
                  raw, landed):
    nc = k.nc
    with ExitStack() as ctx:
        sb = lambda n, shape, dt=F32: k.sb(f"{name}_{n}", shape, dt, ctx)
        hi = [sb(f"hi{j}", [P, DC, P], F32R) for j in range(2)]
        lo = [sb(f"lo{j}", [P, DC, P], F32R) for j in range(2)]
        out = [sb(f"out{j}", [P, L]) for j in range(2)]
        one2 = [sb(f"one2_{j}", [P, 4, P], F32R) for j in range(2)]
        one1 = [sb(f"one1_{j}", [P, 4, P], BF16) for j in range(2)]
        gates = [sb(f"gates{j}", [P, 4, 2, P], F32R) for j in range(2)]
        low = [sb(f"low{j}", [P, 4, P]) for j in range(2)]
        warm = sb("warm", [P, 1])
        e, den, inv = sb("e", [P, HEADS, TOPK]), sb("den", [P, HEADS]), sb("inv", [P, HEADS])
        pairs = sb("pairs", [P, 2, P])
        gate_hi, gate_lo = sb("gate_hi", [P, P], F32R), sb("gate_lo", [P, P])
        acc = [k.ps(f"{name}_acc{j}", [P, L], ctx) for j in range(2)]
        bank = [k.ps(f"{name}_bank{j}", [P, 4, 2, P], ctx) for j in range(2)]
        turn = k.ps(f"{name}_turn", [P, 3, P], ctx)
        sem = lambda n: k.sem(f"{name}_{n}")
        stored = [sem("stored0"), sem("stored1")]
        sent = [sem("sent0"), sem("sent1")]
        hi_ready, lo_ready, product, taken = sem("hi_ready"), sem("lo_ready"), sem("product"), sem("taken")
        exp_done, summed, gate_ready, turned, pairs_ready = (sem(n) for n in ("exp_done", "summed", "gate_ready",
                                                                             "turned", "pairs_ready"))
        gate_split, equal, hot, spread, emptied = (sem(n) for n in ("gate_split", "equal", "hot", "spread", "emptied"))
        chosen, cleared, low_ready = sem("chosen"), sem("cleared"), sem("low_ready")
        chooser = Chooser(k, f"{name}_choose", ctx)
        FREE = 2
        block = ctx.enter_context(nc.Block(no_gpsimd_drain=True))

        def all_slabs(eng, start_block, slab):
            class State:
                pass

            def a_block(p, first, more):
                s = State()
                s.p, s.more = p, more
                start_block(p)
                for s.half in range(2):
                    s.before = not first or s.half == 1

                    def four(i, end):
                        for j in range(4):
                            s.block_end = end and j == 3
                            s.last = end and j >= 2 and not more
                            t = 16 * s.half + 4 * i + j
                            slab(32 * p + t, t, j, 4 * s.half + i, s)

                    with eng.Fori(0, 4 - s.half) as i:
                        four(i, False)
                    if s.half == 1:
                        four(3, True)

            a_block(0, True, True)
            with eng.Fori(1, TB - 1) as p:
                a_block(p, False, True)
            a_block(TB - 1, False, False)

        def nothing(p):
            pass

        @block.sync
        def _(sp):
            with sp.Fori(1, NKEYS // 4) as i:
                for j in range(4):
                    sp.wait_ge(lo_ready, FREE + 4 * i + j - 3)
                    sp.dma_start(raw[j][:], u[4 * i + j]).then_inc(landed[j], 16)

        @block.tensor
        def _(pe):
            pe.sem_inc(product, FREE)
            pe.sem_inc(spread, FREE)

            def turn_pairs(p):
                pe.wait_ge(gate_ready, p + 1)
                for j in range(3):
                    mm = nc.tensor.transpose(turn[:, j, :], found[:, j, :], k.ident[:])
                mm.then_inc(turned, 1)

            def products(n, j):
                pe.wait_ge(lo_ready, FREE + n + 1)
                pe.wait_ge(taken, n + 1)
                for c in range(DC):
                    for m, (a, b) in enumerate(((hi, h_hi), (hi, h_lo), (lo, h_hi))):
                        mm = nc.tensor.matmul(acc[j][:], a[j][:, c, :], b[:, c, :],
                                              start=(c == 0 and m == 0), stop=(c == DC - 1 and m == 2))
                mm.then_inc(product, 1)

            def slab(n, t, j, h, s):
                if s.block_end and s.more:
                    turn_pairs(s.p + 1)
                pe.wait_ge(hot, n + 1)
                pe.wait_ge(emptied, n + 2)
                for m in range(4):
                    mm = nc.tensor.matmul(bank[j % 2][:, m, :, :].rearrange("p r i -> p (r i)"), one2[j % 2][:, m, :],
                                          gates[j % 2][:, m, :, :].rearrange("p r i -> p (r i)"),
                                          start=True, stop=True)
                mm.then_inc(spread, 1)
                if not s.last:
                    products(n + 2, j % 2)

            products(0, 0)
            products(1, 1)
            turn_pairs(0)
            all_slabs(pe, nothing, slab)

        @block.scalar
        def _(act):
            act.sem_inc(taken, FREE)
            for j in range(2):
                act.sem_inc(stored[j], 16)
                act.sem_inc(sent[j], 16)

            def exp_scores(p):
                act.wait_ge(chosen, p + 1)
                nc.scalar.activation(e[:], shifted[:], ACT.Exp).then_inc(exp_done, 1)
                act.wait_ge(exp_done, 2 * p + 1)
                nc.scalar.activation(warm[:], e[:, 0, 0:1], ACT.Gelu).then_inc(exp_done, 1)

            def take_pairs(p):
                act.wait_ge(turned, p + 1)
                nc.scalar.copy(pairs[:], turn[:, 0:2, :]).then_inc(pairs_ready, 1)
                nc.scalar.copy(gate_hi[:], turn[:, 2, :]).then_inc(pairs_ready, 1)

            def split_hi(n, slot):
                act.wait_ge(landed[slot], 4 * (n - slot) + 16)
                act.wait_ge(product, n + 1)
                nc.scalar.copy(hi[slot % 2][:], raw[slot][:]).then_inc(hi_ready, 1)

            def take_low(n, j):
                act.wait_ge(spread, FREE + n)
                act.wait_ge(emptied, n + 1)
                nc.scalar.copy(low[j][:], bank[j][:, :, 1, :]).then_inc(low_ready, 1)

            def slab(n, t, j, h, s):
                if s.block_end and s.more:
                    exp_scores(s.p + 1)
                act.wait_ge(product, FREE + n + 1)
                act.wait_ge(stored[j % 2], 8 * (n - j % 2) + 16)
                nc.scalar.activation(out[j % 2][:], acc[j % 2][:], ACT.Gelu).then_inc(taken, 1)
                if not s.last:
                    split_hi(n + 2, (j + 2) % 4)
                if s.block_end and s.more:
                    act.wait_ge(hot, n + 1)
                    take_pairs(s.p + 1)
                act.wait_ge(taken, FREE + n + 1)
                act.dma_start(acts[bass.ds(n, 1)].rearrange("o p t -> p (o t)"), out[j % 2][:]).then_inc(stored[j % 2], 16)
                take_low(n, (j + 1) % 2)
                if s.before:
                    for m in ((0,), (1,), (2, 3), ())[j]:
                        at = t - 16 * s.half - j + m
                        act.wait_ge(emptied, 32 * s.p + 16 * s.half + 1)
                        act.wait_ge(sent[m % 2], 8 * (n - j + m - m % 2 - 16) + 16)
                        act.dma_start(table[bass.ds(at * PIECE, PIECE), :, bass.ds((2 * s.p + s.half - 1) * HALF, HALF)]
                                      .rearrange("i j t -> j i t"),
                                      held[:, bass.ds(at * PIECE, PIECE), (1 - s.half) * HALF:(2 - s.half) * HALF]
                                      ).then_inc(sent[m % 2], 16)

            for j in range(2):
                split_hi(j, j)
            exp_scores(0)
            take_pairs(0)
            all_slabs(act, nothing, slab)
            take_low(NKEYS, 1)
            for j in range(2):
                act.wait_ge(stored[j], 16 * (NKEYS // 2 + 1))
                act.wait_ge(sent[j], 128 * (2 * TB - 1) + 16)

        @block.vector
        def _(dve):
            for j in range(2):
                nc.vector.memset(bank[j][:], 0.0).then_inc(cleared, 1)
            nc.vector.memset(low[0][:], 0.0).then_inc(cleared, 1)
            dve.wait_ge(cleared, 3)
            dve.sem_inc(low_ready, 1)
            dve.sem_inc(emptied, 1)
            for h in (HEADS - 2, HEADS - 1):
                chooser.scores(s_all, 0, h)
                chooser.paired()
                chooser.sixteen()
                chooser.placed(h, iota, found, shifted)
            dve.sem_inc(chosen, 1)

            def gates_of(p):
                dve.wait_ge(exp_done, 2 * p + 2)
                nc.vector.tensor_reduce(den[:], e[:], AX.X, ALU.add).then_inc(summed, 1)
                dve.wait_ge(summed, 2 * p + 1)
                nc.vector.reciprocal(inv[:], den[:]).then_inc(summed, 1)
                dve.wait_ge(summed, 2 * p + 2)
                nc.vector.tensor_tensor(found[:, 2, :].rearrange("p (h c) -> p h c", h=HEADS), e[:],
                                        inv[:].unsqueeze(2).broadcast_to([P, HEADS, TOPK]), ALU.mult).then_inc(gate_ready, 1)

            def start_block(p):
                dve.wait_ge(pairs_ready, 2 * p + 2)
                nc.vector.tensor_tensor(gate_lo[:], turn[:, 2, :], f32(gate_hi[:]), ALU.subtract).then_inc(gate_split, 1)

            def add_parts(n, j, slot):
                nc.vector.tensor_tensor(held[:, :, bass.ds(slot * 4, 4)].rearrange("p i t -> p t i"),
                                        bank[j][:, :, 0, :], low[j][:], ALU.add).then_inc(emptied, 1)

            def slab(n, t, j, h, s):
                dve.wait_ge(spread, n + 1)
                if j == 0:
                    dve.wait_ge(gate_split, s.p + 1)
                grid = [P, 4, P]
                row = iota[:].unsqueeze(1).broadcast_to(grid)
                cols = lambda what: pairs[:, what, bass.ds(4 * t, 4)].unsqueeze(2).broadcast_to(grid)
                nc.vector.tensor_tensor(one2[j % 2][:], row, cols(1), ALU.is_equal)
                nc.vector.tensor_tensor(one1[j % 2][:], row, cols(0), ALU.is_equal).then_inc(equal, 1)
                if s.before and j == 0:
                    for r in range(2):
                        dve.wait_ge(sent[r], 128 * (2 * s.p + s.half - 1) + 16)
                dve.wait_ge(low_ready, n + 1)
                add_parts(n, j % 2, t)
                if s.more:
                    if j == 0:
                        chooser.scores(s_all, s.p + 1, h)
                    elif j == 1:
                        chooser.paired()
                    elif j == 2:
                        chooser.sixteen()
                    else:
                        chooser.placed(h, iota, found, shifted)
                if s.block_end and s.more:
                    dve.sem_inc(chosen, 1)
                    gates_of(s.p + 1)

            gates_of(0)
            all_slabs(dve, start_block, slab)
            for j in range(2):
                dve.wait_ge(low_ready, NKEYS + j + 1)
                if j == 0:
                    for r in range(2):
                        dve.wait_ge(sent[r], 128 * (2 * TB - 1) + 16)
                add_parts(NKEYS + j, j, j)

        @block.gpsimd
        def _(pool):
            pool.sem_inc(lo_ready, FREE)

            def split_lo(n, slot):
                pool.wait_ge(hi_ready, n + 1)
                nc.gpsimd.tensor_tensor(lo[slot % 2][:], raw[slot][:], f32(hi[slot % 2][:]), ALU.subtract).then_inc(lo_ready, 1)

            def slab(n, t, j, h, s):
                pool.wait_ge(equal, n + 1)
                for r, part in enumerate((f32(gate_hi[:]), gate_lo[:])):
                    ins = nc.gpsimd.tensor_tensor(gates[j % 2][:, :, r, :], one1[j % 2][:],
                                                  part[:, bass.ds(4 * t, 4)].unsqueeze(2).broadcast_to([P, 4, P]), ALU.mult)
                ins.then_inc(hot, 1)
                if not s.last:
                    split_lo(n + 2, (j + 2) % 4)

            for j in range(2):
                split_lo(j, j)
            all_slabs(pool, nothing, slab)


def expert_outputs(k, name, v, acts, table, held, x, gate, beside=None):
    nc = k.nc
    NT = NKEYS
    with ExitStack() as ctx:
        raw = [k.sb(f"{name}_raw{j}", [P, D], F32, ctx) for j in range(2)]
        hi = [k.sb(f"{name}_hi{j}", [P, D], F32R, ctx) for j in range(2)]
        lo = [k.sb(f"{name}_lo{j}", [P, D], F32R, ctx) for j in range(2)]
        a = [k.sb(f"{name}_a{j}", [P, L], F32, ctx) for j in range(2)]
        g = [k.sb(f"{name}_g{j}", [P, L], F32, ctx) for j in range(2)]
        w = [k.sb(f"{name}_w{j}", [P, L], F32, ctx) for j in range(2)]
        w_hi = [k.sb(f"{name}_w_hi{j}", [P, L], F32R, ctx) for j in range(2)]
        w_lo = [k.sb(f"{name}_w_lo{j}", [P, L], F32R, ctx) for j in range(2)]
        acc = [k.ps(f"{name}_acc{c}", [P, L], ctx) for c in range(DC)]
        sem = lambda n: k.sem(f"{name}_{n}")
        landed = [sem("landed0"), sem("landed1")]
        sent = sem("sent")
        w_ready, hi_ready, lo_ready, product = sem("w_ready"), sem("hi_ready"), sem("lo_ready"), sem("product")
        FREE = 2
        block = ctx.enter_context(nc.Block(no_gpsimd_drain=True))

        @block.sync
        def _(sp):
            def send(piece):
                rows = bass.ds(piece * PIECE, PIECE)
                sp.dma_start(table[rows, :, L - HALF:L].rearrange("i j t -> j i t"),
                             held[:, rows, HALF:P]).then_inc(sent, 16)
                sp.dma_start(table[rows, :, L:L + PAD].rearrange("i j t -> j i t"),
                             held[:, rows, 0:PAD]).then_inc(sent, 16)

            def load_piece(piece, first=False):
                if not first:
                    sp.wait_ge(sent, 32 * piece + 32)
                    if not isinstance(piece, int):
                        send(piece + 1)
                for s in range(PIECE):
                    j, n = s % 2, piece * PIECE + s
                    sp.wait_ge(lo_ready, n + 1)
                    sp.dma_start(a[j][:], acts[bass.ds(n, 1)].rearrange("o p t -> p (o t)")).then_inc(landed[j], 16)
                    sp.dma_start(raw[j][:], v[bass.ds(n, 1)].rearrange("o p t -> p (o t)")).then_inc(landed[j], 16)
                    if first and s == 0:
                        sp.wait_ge(sent, 32)
                        send(1)
                    sp.dma_start(g[j][:], table[bass.ds(n, 1), :, PAD:PAD + L].rearrange("o p t -> p (o t)")).then_inc(landed[j], 16)
                    if beside:
                        beside.load(sp, piece, s)

            send(0)
            load_piece(0, first=True)
            with sp.Fori(1, NT // PIECE - 1) as piece:
                load_piece(piece)
            load_piece(NT // PIECE - 1)

        @block.tensor
        def _(pe):
            pe.sem_inc(product, FREE)

            def products(i, j, first=False, last=False):
                pe.wait_ge(lo_ready, FREE + 2 * i + j + 1)
                for c in range(DC):
                    for m, (p, q) in enumerate(((hi, w_hi), (hi, w_lo), (lo, w_hi))):
                        mm = nc.tensor.matmul(acc[c][:], p[j][:, c * P:(c + 1) * P], q[j][:],
                                              start=(first and m == 0), stop=(last and m == 2), skip_group_check=True)
                mm.then_inc(product, 1)

            products(0, 0, first=True)
            products(0, 1)
            with pe.Fori(1, NT // 2 - 1) as i:
                products(i, 0)
                products(i, 1)
            products(NT // 2 - 1, 0)
            products(NT // 2 - 1, 1, last=True)

        @block.scalar
        def _(act):
            def split_piece(piece):
                for s in range(PIECE):
                    j, n = s % 2, piece * PIECE + s
                    act.wait_ge(product, n + 1)
                    act.wait_ge(landed[j], 24 * (n - j) + 48)
                    nc.scalar.copy(hi[j][:], raw[j][:])
                    act.wait_ge(w_ready, n + 1)
                    nc.scalar.copy(w_hi[j][:], w[j][:]).then_inc(hi_ready, 1)
                    if beside:
                        beside.scalar(act, piece, s)

            if beside:
                beside.begin(act)
            split_piece(0)
            with act.Fori(1, NT // PIECE) as piece:
                split_piece(piece)
            if beside:
                beside.scalar_end(act)

        @block.vector
        def _(dve):
            dve.sem_inc(lo_ready, FREE)
            if beside:
                beside.vector_begin(dve)
            with dve.Fori(0, NT // PIECE) as piece:
                for s in range(PIECE):
                    j, n = s % 2, piece * PIECE + s
                    dve.wait_ge(landed[j], 24 * (n - j) + 48)
                    nc.vector.tensor_tensor(w[j][:], a[j][:], g[j][:], ALU.mult).then_inc(w_ready, 1)
                    dve.wait_ge(hi_ready, n + 1)
                    nc.vector.tensor_tensor(lo[j][:], raw[j][:], f32(hi[j][:]), ALU.subtract)
                    nc.vector.tensor_tensor(w_lo[j][:], w[j][:], f32(w_hi[j][:]), ALU.subtract).then_inc(lo_ready, 1)
                    if beside:
                        beside.vector(dve, piece, s)
            if beside:
                beside.vector_end(dve)
            dve.wait_ge(product, FREE + NT)
            for c in range(DC):
                nc.vector.scalar_tensor_tensor(x[:, c, :], acc[c][:], gate[:, c:c + 1], x[:, c, :], ALU.mult, ALU.add)


def peer(k, name, x, gain, shift, scale, gate, wq, keys_in, u, v, beside=None):
    nc = k.nc
    k.recycle()
    with ExitStack() as whole:
        held = k.sb(f"{name}_held", [P, NKEYS, P], F32, whole)
        with ExitStack() as outer:
            h_hi = k.sb(f"{name}_h_hi", [P, DC, L], F32R, outer)
            h_lo = k.sb(f"{name}_h_lo", [P, DC, L], F32R, outer)
            s_all = k.sb(f"{name}_s_all", [P, TB * 2 * HEADS, NKEYS], F32, outer)
            found = k.sb(f"{name}_found", [P, 3, PAIRS], F32, outer)
            shifted = k.sb(f"{name}_shifted", [P, HEADS, TOPK], F32, outer)
            u_raw = [k.sb(f"{name}_u_raw{j}", [P, DC, P], F32, outer) for j in range(4)]
            u_landed = [k.sem(f"{name}_u_landed{j}") for j in range(4)]
            with ExitStack() as ctx:
                keys = k.sb(f"{name}_keys", [P, 2 * HEADS, NKEYS], F32, ctx)
                keys_loaded = k.sem(f"{name}_keys_loaded")
                ring = WeightRing(k, f"{name}_wq", wq, 0, DC, ctx)
                norm_modulate(k, f"{name}_norm", x, L, gain, shift, h_hi, h_lo, scale=scale, ring=ring,
                              later=((keys, keys_in), keys_loaded))
                queries(k, f"{name}_q", wq, h_hi, h_lo, keys, k.iota, s_all, found, shifted, u, u_raw, u_landed,
                        ring.raw, ring.landed, keys_loaded)
            expert_inputs(k, f"{name}_u", u, h_hi, h_lo, k.iota, s_all, found, shifted, k.acts, k.table, held,
                          u_raw, u_landed)
            k.recycle()
        expert_outputs(k, f"{name}_v", v, k.acts, k.table, held, x, gate,
                       beside(k, whole) if beside else None)



HG_HEADS = 4
HG_SCALE = 128 ** -0.5
TINY = 2.0 ** -60
S5_TILES = 16
TWO_PI = 6.283185307179586
MAGIC = 12582912.0


def lower_bound(k, logits, lb, one_minus):
    nc = k.nc
    with ExitStack() as ctx:
        t = k.sb("lb_t", [P, 4, HG_HEADS], F32, ctx)
        step, exp_done = k.sem("lb_step"), k.sem("lb_exp")
        block = ctx.enter_context(nc.Block(no_gpsimd_drain=True))

        @block.vector
        def _(dve):
            nc.vector.tensor_tensor(t[:, 0, :], logits[:, 0, :], logits[:, 1, :], ALU.max).then_inc(step, 1)
            dve.wait_ge(step, 1)
            for r in range(2):
                nc.vector.tensor_tensor(t[:, 1 + r, :], logits[:, r, :], t[:, 0, :], ALU.subtract).then_inc(step, 1)
            dve.wait_ge(exp_done, 1)
            nc.vector.tensor_tensor(t[:, 3, :], t[:, 1, :], t[:, 2, :], ALU.add).then_inc(step, 1)
            dve.wait_ge(step, 4)
            nc.vector.reciprocal(t[:, 0, :], t[:, 3, :]).then_inc(step, 1)
            dve.wait_ge(step, 5)
            nc.vector.tensor_tensor(lb[:], t[:, 1, :], t[:, 0, :], ALU.mult)
            nc.vector.tensor_tensor(one_minus[:], t[:, 2, :], t[:, 0, :], ALU.mult)

        @block.scalar
        def _(act):
            act.wait_ge(step, 3)
            nc.scalar.activation(t[:, 1:3, :], t[:, 1:3, :], ACT.Exp).then_inc(exp_done, 1)


def forget_gates(k, q, sig, lb, one_minus, resets, b, key):
    nc = k.nc
    H = HG_HEADS
    with ExitStack() as ctx:
        f = k.sb("fg_f", [P, H, L], F32, ctx)
        t = [k.sb(f"fg_t{j}", [P, H, L], F32, ctx) for j in range(2)]
        pool_done = k.sem("fg_pool_done")
        ready, logged, log_f, f_ready = k.sem("fg_ready"), k.sem("fg_logged"), k.sem("fg_log_f"), k.sem("fg_f_ready")
        block = ctx.enter_context(nc.Block(no_gpsimd_drain=True))

        @block.vector
        def _(dve):
            for h in range(H):
                nc.vector.tensor_scalar(f[:, h, :], sig[:, h, :], one_minus[:, h:h + 1], lb[:, h:h + 1],
                                        ALU.mult, ALU.add).then_inc(f_ready, 1)
            dve.wait_ge(f_ready, H)
            nc.vector.tensor_scalar(t[0][:], f[:], TINY, None, ALU.max).then_inc(ready, 1)
            nc.vector.tensor_scalar(t[1][:], f[:], 1.0 / TINY, 1.0, ALU.mult, ALU.min).then_inc(ready, 1)
            dve.wait_ge(logged, 2)
            for h in range(H):
                nc.vector.tensor_tensor(t[0][:, h, :], t[0][:, h, :], t[1][:, h, :], ALU.add).then_inc(log_f, 1)
            for h in range(H):
                dve.wait_ge(log_f, h + 1)
                nc.vector.tensor_tensor_scan(b[:, h, :], resets[:], t[0][:, h, :], 0.0, ALU.mult, ALU.add)
            dve.wait_ge(pool_done, 2)

        @block.gpsimd
        def _(pool):
            nc.gpsimd.tensor_scalar(q[:], q[:], HG_SCALE, None, ALU.mult).then_inc(pool_done, 1)
            pool.wait_ge(f_ready, H)
            nc.gpsimd.tensor_scalar(key[:], f[:], -1.0, 1.0, ALU.mult, ALU.add).then_inc(pool_done, 1)

        @block.scalar
        def _(act):
            for j in range(2):
                act.wait_ge(ready, j + 1)
                nc.scalar.activation(t[j][:], t[j][:], ACT.Ln).then_inc(logged, 1)


def chunk_scores(k, q, key, b, masks, scores):
    nc = k.nc
    U = HG_HEADS * L // P
    W = U * P
    halves = [64, 32, 16, 8, 4, 2, 1]
    with ExitStack() as ctx:
        ql = [k.sb(f"cs_q{j}", [P, W], F32, ctx) for j in range(2)]
        kl = [k.sb(f"cs_k{j}", [P, W], F32, ctx) for j in range(2)]
        e = [k.sb(f"cs_e{j}", [P, W], F32, ctx) for j in range(2)]
        out = [k.ps(f"cs_out{j}", [P, 4, P], ctx) for j in range(8)]
        cleared, diff, exp_done = k.sem("cs_cleared"), k.sem("cs_diff"), k.sem("cs_exp")
        factors, product, merged = k.sem("cs_factors"), k.sem("cs_product"), k.sem("cs_merged")
        block = ctx.enter_context(nc.Block(no_gpsimd_drain=True))
        flat = lambda t: t[:].rearrange("p h t -> p (h t)")
        levels = len(halves) + 1

        def parts(ap, m):
            v = ap.rearrange("p (n two m) -> p n two m", two=2, m=m)
            return v[:, :, 0, :], v[:, :, 1, :]

        @block.tensor
        def _(pe):
            for i in range(levels):
                if i < len(halves):
                    pe.wait_ge(factors, 2 * (i + 1))
                for g in range(U // 4):
                    if i >= 2:
                        pe.wait_ge(merged, (i - 2) * (U // 4) + g + 1)
                    for j in range(4):
                        u = slice((4 * g + j) * P, (4 * g + j + 1) * P)
                        a, c = (kl[i % 2][:, u], ql[i % 2][:, u]) if i < len(halves) else (flat(key)[:, u], flat(q)[:, u])
                        mm = nc.tensor.matmul(out[4 * (i % 2) + g][:, j, :], a, c, start=True, stop=True)
                    mm.then_inc(product, 1)

        @block.scalar
        def _(act):
            for i in range(len(halves)):
                act.wait_ge(diff, 2 * (i + 1))
                nc.scalar.activation(e[i % 2][:], e[i % 2][:], ACT.Exp).then_inc(exp_done, 1)

        @block.vector
        def _(dve):
            for j in range(2):
                nc.vector.memset(ql[j][:], 0.0).then_inc(cleared, 1)
                nc.vector.memset(kl[j][:], 0.0).then_inc(cleared, 1)
            nc.vector.memset(scores[:], 0.0).then_inc(cleared, 1)
            dve.wait_ge(cleared, 5)

            def level(i):
                m = halves[i]
                dve.wait_ge(exp_done, i + 1)
                if i >= 2:
                    dve.wait_ge(product, (i - 1) * (U // 4))
                e1, e2 = parts(e[i % 2][:], m)
                k1, _ = parts(flat(key), m)
                _, q2 = parts(flat(q), m)
                nc.vector.tensor_tensor(parts(kl[i % 2][:], m)[0], k1, e1, ALU.mult).then_inc(factors, 1)
                nc.vector.tensor_tensor(parts(ql[i % 2][:], m)[1], q2, e2, ALU.mult).then_inc(factors, 1)

            def merge(i):
                for g in range(U // 4):
                    dve.wait_ge(product, i * (U // 4) + g + 1)
                    if i >= 1:
                        dve.wait_ge(merged, (i - 1) * (U // 4) + g + 1)
                    nc.vector.copy_predicated(scores[:, 4 * g:4 * g + 4, :],
                                              masks[:, i, :].unsqueeze(1).broadcast_to([P, 4, P]),
                                              out[4 * (i % 2) + g][:]).then_inc(merged, 1)

            for i in range(len(halves)):
                level(i)
                if i >= 1:
                    merge(i - 1)
            merge(levels - 2)
            merge(levels - 1)

        @block.gpsimd
        def _(pool):
            for i, m in enumerate(halves):
                first, second = parts(flat(b), m)
                mid = first[:, :, m - 1:m].broadcast_to([P, W // (2 * m), m])
                if i >= 2:
                    pool.wait_ge(factors, 2 * (i - 1))
                e1, e2 = parts(e[i % 2][:], m)
                nc.gpsimd.tensor_tensor(e1, mid, first, ALU.subtract).then_inc(diff, 1)
                nc.gpsimd.tensor_tensor(e2, second, mid, ALU.subtract).then_inc(diff, 1)


def chunk_outputs(k, q, key, b, v, scores, y):
    nc = k.nc
    H, C = HG_HEADS, L // P
    U = H * C
    with ExitStack() as ctx:
        e = k.sb("co_e", [P, H, L], F32, ctx)
        qe = k.sb("co_qe", [P, H, L], F32, ctx)
        ke = k.sb("co_ke", [P, H, L], F32, ctx)
        kt = k.sb("co_kt", [P, U, P], F32, ctx)
        last = k.sb("co_last", [P, U], F32, ctx)
        state = k.sb("co_state", [P, U, P], F32, ctx)
        turn = [k.ps(f"co_turn{j}", [P, 4, P], ctx) for j in range(2)]
        out = [k.ps(f"co_out{j}", [P, L], ctx) for j in range(H)]
        add = [k.ps(f"co_add{j}", [P, 4, P], ctx) for j in range(2)]
        diff, exp_done, mult_done = k.sem("co_diff"), k.sem("co_exp"), k.sem("co_mult")
        turned, rows_ready, added, new_state = k.sem("co_turned"), k.sem("co_rows"), k.sem("co_added"), k.sem("co_state")
        out_done = k.sem("co_out_done")
        block = ctx.enter_context(nc.Block(no_gpsimd_drain=True))
        ends = b[:].rearrange("p h (c t) -> p (h c) t", t=P)[:, :, P - 1:P]

        @block.vector
        def _(dve):
            bu = b[:].rearrange("p h (c t) -> p (h c) t", t=P)
            nc.vector.tensor_tensor(ke[:].rearrange("p h (c t) -> p (h c) t", t=P),
                                    ends.broadcast_to([P, U, P]), bu, ALU.subtract).then_inc(diff, 1)
            dve.wait_ge(exp_done, 3)
            nc.vector.tensor_tensor(ke[:], ke[:], key[:], ALU.mult).then_inc(mult_done, 1)
            nc.vector.tensor_tensor(qe[:], q[:], e[:], ALU.mult).then_inc(mult_done, 1)
            for c in range(C - 1):
                dve.wait_ge(added, c + 1)
                if c >= 1:
                    dve.wait_ge(new_state, H * c)
                for h in range(H):
                    u = h * C + c
                    if c == 0:
                        ins = nc.vector.tensor_copy(state[:, u + 1, :], add[c % 2][:, h, :])
                    else:
                        ins = nc.vector.scalar_tensor_tensor(state[:, u + 1, :], state[:, u, :], last[:, u:u + 1],
                                                             add[c % 2][:, h, :], ALU.mult, ALU.add)
                    ins.then_inc(new_state, 1)

        @block.scalar
        def _(act):
            nc.scalar.activation(e[:], b[:], ACT.Exp).then_inc(exp_done, 1)
            nc.scalar.activation(last[:].unsqueeze(2), ends, ACT.Exp).then_inc(exp_done, 1)
            act.wait_ge(diff, 1)
            nc.scalar.activation(ke[:], ke[:], ACT.Exp).then_inc(exp_done, 1)
            for h in range(H):
                act.wait_ge(turned, h + 1)
                nc.scalar.copy(kt[:, 4 * h:4 * h + 4, :], turn[h % 2][:]).then_inc(rows_ready, 1)
            for h in range(H):
                act.wait_ge(out_done, H)
                nc.scalar.copy(y[:, h, :], out[h][:])

        @block.tensor
        def _(pe):
            pe.wait_ge(mult_done, 1)
            for h in range(H):
                if h >= 2:
                    pe.wait_ge(rows_ready, h - 1)
                for c in range(C):
                    mm = nc.tensor.transpose(turn[h % 2][:, c, :], ke[:, h, c * P:(c + 1) * P], k.ident[:])
                mm.then_inc(turned, 1)
            pe.wait_ge(rows_ready, H)
            for c in range(C - 1):
                if c >= 2:
                    pe.wait_ge(new_state, H * (c - 1))
                for h in range(H):
                    mm = nc.tensor.matmul(add[c % 2][:, h, :], kt[:, h * C + c, :], v[:, c, h * P:(h + 1) * P],
                                          start=True, stop=True)
                mm.then_inc(added, 1)
            pe.wait_ge(mult_done, 2)
            for c in range(C):
                if c >= 1:
                    pe.wait_ge(new_state, H * c)
                for h in range(H):
                    u, at = h * C + c, slice(c * P, (c + 1) * P)
                    mm = nc.tensor.matmul(out[h][:, at], v[:, c, h * P:(h + 1) * P], scores[:, u, :],
                                          start=True, stop=(c == 0))
                    if c >= 1:
                        mm = nc.tensor.matmul(out[h][:, at], state[:, u, :], qe[:, h, at], start=False, stop=True)
                    if c == C - 1:
                        mm.then_inc(out_done, 1)


def s5_parameters(k, a_re, a_im, log_dt, mag, turn_hi, turn_lo, coef_re, minus_coef_im):
    nc = k.nc
    T = S5_TILES
    with ExitStack() as ctx:
        t = k.sb("s5p", [P, 20, T], F32, ctx)
        r12 = k.sb("s5p_r12", [P, T], F32R, ctx)
        step, act_done = k.sem("s5p_step"), k.sem("s5p_act")
        block = ctx.enter_context(nc.Block(no_gpsimd_drain=True))
        (dt, ard, th, n, r, r2, sin, cos, are, aim, den, inv, nr, p1, p2, cr, ci, ab, q1, q2) = (t[:, j, :] for j in range(20))

        @block.scalar
        def _(act):
            nc.scalar.activation(dt, log_dt[:], ACT.Exp).then_inc(act_done, 1)
            act.wait_ge(step, 2)
            nc.scalar.activation(mag[:], ard, ACT.Exp).then_inc(act_done, 1)
            act.wait_ge(step, 9)
            nc.scalar.activation(sin, r2, ACT.Sin, scale=6.28318500).then_inc(act_done, 1)
            nc.scalar.activation(cos, ab, ACT.Sin, scale=6.28318500).then_inc(act_done, 1)

        @block.vector
        def _(dve):
            steps = 0

            def after(ins):
                nonlocal steps
                steps += 1
                ins.then_inc(step, 1)
                dve.wait_ge(step, steps)

            V = nc.vector
            dve.wait_ge(act_done, 1)
            after(V.tensor_tensor(th, a_im[:], dt, ALU.mult))
            after(V.tensor_tensor(ard, a_re[:], dt, ALU.mult))
            after(V.tensor_scalar(n, th, 1.0 / TWO_PI, MAGIC, ALU.mult, ALU.add))
            after(V.tensor_scalar(n, n, MAGIC, None, ALU.subtract))
            after(V.scalar_tensor_tensor(r, n, -6.28125, th, ALU.mult, ALU.add))
            after(V.scalar_tensor_tensor(r, n, -(TWO_PI - 6.28125), r, ALU.mult, ALU.add))
            after(V.tensor_scalar(r2, r, 1.0 / TWO_PI, None, ALU.mult))
            after(V.scalar_tensor_tensor(ab, r2, -1.0, r2, ALU.mult, ALU.max))
            after(V.tensor_scalar(ab, ab, -1.0, 0.25, ALU.mult, ALU.add))
            after(V.tensor_copy(r12[:], r2))
            after(V.tensor_copy(turn_hi[:], f32(r12[:])))
            after(V.tensor_tensor(turn_lo[:], r2, turn_hi[:], ALU.subtract))
            dve.wait_ge(act_done, 4)
            after(V.tensor_tensor(are, mag[:], cos, ALU.mult))
            after(V.tensor_tensor(aim, mag[:], sin, ALU.mult))
            after(V.tensor_scalar(nr, are, 1.0, None, ALU.subtract))
            after(V.tensor_tensor(p1, a_re[:], a_re[:], ALU.mult))
            after(V.tensor_tensor(p2, a_im[:], a_im[:], ALU.mult))
            after(V.tensor_tensor(den, p1, p2, ALU.add))
            after(V.reciprocal(inv, den))
            for x1, y1, x2, y2, op, dst in ((nr, a_re[:], aim, a_im[:], ALU.add, coef_re[:]), (nr, a_im[:], aim, a_re[:], ALU.subtract, minus_coef_im[:])):
                after(V.tensor_tensor(p1, x1, y1, ALU.mult))
                after(V.tensor_tensor(p2, x2, y2, ALU.mult))
                after(V.tensor_tensor(p1, p1, p2, op))
                after(V.tensor_tensor(dst, p1, inv, ALU.mult))

class BesideOutputs:

    def __init__(self, k, ctx):
        self.k, self.nc = k, k.nc
        self.rows = [k.sb(f"beside_rows{j}", [P, D], F32, ctx) for j in range(3)]
        self.turns, self.whole = k.sb("beside_turns", [P, L], F32, ctx), k.sb("beside_whole", [P, L], F32, ctx)
        self.arg = k.sb("beside_arg", [P, 2, L], F32, ctx)
        self.table = k.sb("beside_table", [P, 2, L], F32, ctx)
        self.c = k.sb("beside_c", [P, 2, P], F32, ctx)
        self.part = k.sb("beside_part", [P, 2, P], F32, ctx)
        self.cc = k.sb("beside_cc", [P, 2, P], F32, ctx)
        self.time = k.sb("beside_time", [P, L], F32, ctx)
        self.cond = k.sb("beside_cond", [P, D], F32, ctx)
        self.bias = k.sb("beside_bias", [P, 6 * DC], F32, ctx)
        sem = lambda n: k.sem(f"beside_{n}")
        self.rows_landed = [sem(f"rows_landed{j}") for j in range(3)]
        self.modulated, self.loaded, self.cond_ready = sem("modulated"), sem("loaded"), sem("cond_ready")
        self.step, self.arg_ready = sem("step"), sem("arg_ready")
        self.c_landed, self.c_step, self.cc_sent = sem("c_landed"), sem("c_step"), sem("cc_sent")
        self.table_ready, self.table_sent = sem("table_ready"), sem("table_sent")

    def load(self, sp, piece, s):
        if s in (0, 2, 4):
            m = s // 2
            if s == 0:
                sp.wait_ge(self.modulated, 3 * piece + 1)
            else:
                sp.wait_ge(self.modulated, 3 * piece + m + 1)
            sp.dma_start(self.rows[m][:], self.k.dram["ada_w_2"][3 * piece + m]).then_inc(self.rows_landed[m], 16)

        if s == 2:
            sp.wait_ge(self.c_step, 4 * piece + 1)
            sp.dma_start(self.c[:], self.k.dram["s5_c"][bass.ds(piece, 1)].rearrange("o p r c -> p (o r) c")).then_inc(self.c_landed, 16)

    def begin(self, act):
        act.dma_start(self.time[:], self.k.dram["time"]).then_inc(self.loaded, 16)
        act.dma_start(self.bias[:], self.k.dram["ada_b_2"]).then_inc(self.loaded, 16)
        act.dma_start(self.cond[:], self.k.dram["cond_2"]).then_inc(self.loaded, 16)
        act.wait_ge(self.loaded, 48)
        self.nc.scalar.activation(self.cond[:], self.cond[:], ACT.Silu).then_inc(self.cond_ready, 1)

    def scalar(self, act, piece, s):
        if isinstance(piece, int) and piece == 0:
            return
        self.tables(act, piece - 1, s)

    def tables(self, act, tile, s):
        if s in (0, 1):
            if s == 0:
                act.wait_ge(self.arg_ready, tile + 1)
                act.wait_ge(self.table_sent, 16 * tile + 16)
            self.nc.scalar.activation(self.table[:, s, :], self.arg[:, s, :], ACT.Sin,
                                      scale=6.28318500).then_inc(self.table_ready, 1)
        if s == 1:
            act.wait_ge(self.table_ready, 2 * tile + 4)
            act.dma_start(self.k.s5_table[bass.ds(tile, 1)].rearrange("o p r t -> p (o r) t"),
                          self.table[:]).then_inc(self.table_sent, 16)

        if s == 3:
            act.wait_ge(self.c_step, 4 * tile + 5)
            act.dma_start(self.k.s5_out[bass.ds(tile, 1)].rearrange("o p r c -> p (o r) c"),
                          self.cc[:]).then_inc(self.cc_sent, 16)

    def scalar_end(self, act):
        for s in (0, 1, 3):
            self.tables(act, S5_TILES - 1, s)
        act.wait_ge(self.table_sent, 16 * (S5_TILES + 1))
        act.wait_ge(self.cc_sent, 16 * (S5_TILES + 1))

    def vector_begin(self, dve):
        dve.sem_inc(self.modulated, 3)
        dve.sem_inc(self.step, 1)
        dve.sem_inc(self.table_ready, 2)
        dve.sem_inc(self.table_sent, 16)
        dve.sem_inc(self.c_step, 1)
        dve.sem_inc(self.cc_sent, 16)
        dve.wait_ge(self.cond_ready, 1)

    def vector(self, dve, piece, s):
        V, k = self.nc.vector, self.k
        turns, whole, arg_sin, arg_cos = self.turns[:], self.whole[:], self.arg[:, 0, :], self.arg[:, 1, :]
        theta_hi, theta_lo = (t[:, bass.ds(piece, 1)] for t in (k.turn_hi, k.turn_lo))
        if s == 5:
            dve.wait_ge(self.table_ready, 2 * piece + 2)
        dve.wait_ge(self.step, 8 * piece + s + 1)
        if s == 0:
            ins = V.tensor_scalar(turns, self.time[:], theta_hi, None, ALU.mult)
        elif s in (1, 4):
            ins = V.tensor_scalar(whole, turns, MAGIC, MAGIC, ALU.add, ALU.subtract)
        elif s == 2:
            ins = V.tensor_tensor(turns, turns, whole, ALU.subtract)
        elif s == 3:
            ins = V.scalar_tensor_tensor(turns, self.time[:], theta_lo, turns, ALU.mult, ALU.add)
        elif s == 5:
            ins = V.tensor_tensor(arg_sin, turns, whole, ALU.subtract)
        elif s == 6:
            ins = V.scalar_tensor_tensor(arg_cos, arg_sin, -1.0, arg_sin, ALU.mult, ALU.max)
        else:
            ins = V.tensor_scalar(arg_cos, arg_cos, -1.0, 0.25, ALU.mult, ALU.add)
        ins.then_inc(self.step, 1)
        if s == 7:
            dve.wait_ge(self.step, 8 * piece + 9)
            dve.sem_inc(self.arg_ready, 1)
        if s >= 4:
            self.outputs(dve, piece, s - 4)
        if s in (1, 3, 5):
            m = s // 2
            dve.wait_ge(self.rows_landed[m], 16 * piece + 16)
            rows = self.rows[m][:]
            V.scalar_tensor_tensor(rows, rows, 1.0, self.cond[:], ALU.mult, ALU.mult,
                                   accum_out=k.mods2[:, bass.ds(3 * piece + m, 1), 0]).then_inc(self.modulated, 1)

    def outputs(self, dve, piece, i):
        V, k = self.nc.vector, self.k
        c_re, c_im = self.c[:, 0, :], self.c[:, 1, :]
        re, minus_im = (t[:, bass.ds(piece, 1)] for t in (k.coef_re, k.minus_coef_im))
        if i == 0:
            dve.wait_ge(self.c_landed, 16 * piece + 16)
        if i == 1:
            dve.wait_ge(self.cc_sent, 16 * piece + 16)
        dve.wait_ge(self.c_step, 4 * piece + i + 1)
        if i == 0:
            ins = V.tensor_scalar(self.part[:, 0, :], c_im, minus_im, None, ALU.mult)
        elif i == 1:
            ins = V.scalar_tensor_tensor(self.cc[:, 0, :], c_re, re, self.part[:, 0, :], ALU.mult, ALU.add)
        elif i == 2:
            ins = V.tensor_scalar(self.part[:, 1, :], c_im, re, None, ALU.mult)
        else:
            ins = V.scalar_tensor_tensor(self.cc[:, 1, :], c_re, minus_im, self.part[:, 1, :], ALU.mult, ALU.subtract)
        ins.then_inc(self.c_step, 1)

    def vector_end(self, dve):
        dve.wait_ge(self.modulated, 3 + 6 * DC)
        mods = self.k.mods2[:, :, 0]
        self.nc.vector.tensor_tensor(mods, mods, self.bias[:], ALU.add)


def s5_scan(k, u, mag, skip_in, y):
    nc = k.nc
    T = S5_TILES
    NT, NW, NB = 5, 6, 3
    with ExitStack() as ctx:
        sb = lambda n, c: [k.sb(f"s5_{n}{j}", [P, L], F32, ctx) for j in range(c)]
        b = [k.sb(f"s5_b{j}", [P, 2, P], F32, ctx) for j in range(NW)]
        cc = [k.sb(f"s5_cc{j}", [P, 2, P], F32, ctx) for j in range(NW)]
        skip = k.sb("s5_skip", [P, 4], F32, ctx)
        w_landed = [k.sem(f"s5_w_landed{j}") for j in range(NW)]
        skip_loaded = k.sem("s5_skip_loaded")
        table = [k.sb(f"s5_table{j}", [P, 2, L], F32, ctx) for j in range(NT)]
        m, zin, z, parts, x = sb("m", 8), sb("zin", 4), sb("z", 4), sb("parts", 4), sb("x", 4)
        ypre = k.sb("s5_ypre", [P, 4, L], F32, ctx)
        bu = [k.ps(f"s5_bu{j}", [P, L], ctx) for j in range(2 * NB)]
        out = [k.ps(f"s5_out{j}", [P, L], ctx) for j in range(2)]
        landed = [k.sem(f"s5_landed{j}") for j in range(NT)]
        driven, turned, zin_ready, scanned = k.sem("s5_driven"), k.sem("s5_turned"), k.sem("s5_zin"), k.sem("s5_scanned")
        parts_vector, parts_pool = k.sem("s5_parts_vector"), k.sem("s5_parts_pool")
        x_vector, x_pool = k.sem("s5_x_vector"), k.sem("s5_x_pool")
        summed, y_ready = k.sem("s5_summed"), k.sem("s5_y")
        block = ctx.enter_context(nc.Block(no_gpsimd_drain=True))
        sin, cos = (lambda j: table[j % NT][:, 0, :]), (lambda j: table[j % NT][:, 1, :])


        @block.sync
        def _(sp):
            def weights(j):
                if j >= NW:
                    sp.wait_ge(summed, j - NW + 1)
                sp.dma_start(b[j % NW][:], k.dram["s5_b"][j]).then_inc(w_landed[j % NW], 16)
                sp.dma_start(cc[j % NW][:], k.s5_out[j]).then_inc(w_landed[j % NW], 16)

            weights(0)
            weights(1)
            for j in range(T):
                if j + 2 < T:
                    weights(j + 2)
                if j == 0:
                    sp.dma_start(skip[:], skip_in).then_inc(skip_loaded, 16)
                if j >= NT:
                    sp.wait_ge(parts_vector, 2 * (j - NT + 1))
                    sp.wait_ge(parts_pool, 2 * (j - NT + 1))
                sp.dma_start(table[j % NT][:], k.s5_table[j]).then_inc(landed[j % NT], 16)

        @block.tensor
        def _(pe):
            def drive(j):
                if j >= NB:
                    pe.wait_ge(turned, 4 * (j - NB + 1))
                pe.wait_ge(w_landed[j % NW], 32 * (j // NW + 1))
                for part in range(2):
                    mm = nc.tensor.matmul(bu[2 * (j % NB) + part][:], b[j % NW][:, part, :], u[:, j // 4, :],
                                          start=True, stop=True)
                mm.then_inc(driven, 1)

            for j in range(NB):
                drive(j)
            for j in range(T):
                if j + NB < T:
                    drive(j + NB)
                if j % 4 == 0 and j >= 8:
                    pe.wait_ge(y_ready, j // 4 - 1)
                pe.wait_ge(x_pool, j + 1)
                pe.wait_ge(x_vector, j + 1)
                for part in range(2):
                    mm = nc.tensor.matmul(out[j // 4 % 2][:], cc[j % NW][:, part, :], x[2 * (j % 2) + part][:],
                                          start=(j % 4 == 0 and part == 0), stop=(j % 4 == 3 and part == 1),
                                          skip_group_check=True)
                mm.then_inc(summed, 1)

        @block.scalar
        def _(act):
            for c in range(4):
                act.wait_ge(y_ready, c + 1)
                nc.scalar.activation(y[:, c, :], ypre[:, c, :], ACT.Gelu)

        @block.vector
        def _(dve):
            V = nc.vector

            def turn_back(j):
                s, c, a = sin(j), cos(j), 4 * (j % 2)
                br, bi = bu[2 * (j % NB)][:], bu[2 * (j % NB) + 1][:]
                dve.wait_ge(landed[j % NT], 16 * (j // NT + 1))
                dve.wait_ge(driven, j + 1)
                if j >= 2:
                    dve.wait_ge(zin_ready, 2 * (j - 1))
                for r, (p, q) in enumerate(((c, br), (s, bi), (c, bi), (s, br))):
                    V.tensor_tensor(m[a + r][:], p, q, ALU.mult).then_inc(turned, 1)

            def scan(j):
                a = 2 * (j % 2)
                dve.wait_ge(zin_ready, 2 * (j + 1))
                if j >= 2:
                    dve.wait_ge(parts_pool, 2 * (j - 1))
                    dve.wait_ge(parts_vector, 2 * (j - 1))
                decay = mag[:, j:j + 1].broadcast_to([P, L])
                for r in range(2):
                    V.tensor_tensor_scan(z[a + r][:], decay, zin[a + r][:], 0.0, ALU.mult, ALU.add).then_inc(scanned, 1)

            def turn_forth(j):
                dve.wait_ge(scanned, 2 * (j + 1))
                if j >= 1:
                    dve.wait_ge(x_vector, j)
                for r, p in enumerate((sin(j), cos(j))):
                    V.tensor_tensor(parts[2 + r][:], p, z[2 * (j % 2) + r][:], ALU.mult).then_inc(parts_vector, 1)
                if j >= 2:
                    dve.wait_ge(summed, j - 1)
                dve.wait_ge(parts_vector, 2 * (j + 1))
                V.tensor_tensor(x[2 * (j % 2) + 1][:], parts[2][:], parts[3][:], ALU.add).then_inc(x_vector, 1)

            def take(c):
                dve.wait_ge(summed, 4 * (c + 1))
                V.scalar_tensor_tensor(ypre[:, c, :], u[:, c, :], skip[:, c:c + 1], out[c % 2][:],
                                       ALU.mult, ALU.add).then_inc(y_ready, 1)

            turn_back(0)
            dve.wait_ge(skip_loaded, 16)
            for j in range(T):
                if j + 1 < T:
                    turn_back(j + 1)
                scan(j)
                turn_forth(j)
                if j % 4 == 1 and j > 4:
                    take(j // 4 - 1)
            take(3)

        @block.gpsimd
        def _(pool):
            G = nc.gpsimd

            def add(j):
                a = 4 * (j % 2)
                pool.wait_ge(turned, 4 * (j + 1))
                if j >= 2:
                    pool.wait_ge(scanned, 2 * (j - 1))
                for r, op in enumerate((ALU.add, ALU.subtract)):
                    G.tensor_tensor(zin[2 * (j % 2) + r][:], m[a + 2 * r][:], m[a + 2 * r + 1][:], op).then_inc(zin_ready, 1)

            def turn_forth(j):
                pool.wait_ge(landed[j % NT], 16 * (j // NT + 1))
                pool.wait_ge(scanned, 2 * (j + 1))
                if j >= 1:
                    pool.wait_ge(x_pool, j)
                for r, p in enumerate((cos(j), sin(j))):
                    G.tensor_tensor(parts[r][:], p, z[2 * (j % 2) + r][:], ALU.mult).then_inc(parts_pool, 1)
                if j >= 2:
                    pool.wait_ge(summed, j - 1)
                pool.wait_ge(parts_pool, 2 * (j + 1))
                G.tensor_tensor(x[2 * (j % 2)][:], parts[0][:], parts[1][:], ALU.subtract).then_inc(x_pool, 1)

            add(0)
            for j in range(T):
                if j + 1 < T:
                    add(j + 1)
                turn_forth(j)


def second_mixer(k, x):
    nc, d = k.nc, k.dram
    mods = k.mods2
    with ExitStack() as outer:
        out_ring = WeightRing(k, "mix2_out", d["w_out_2"], 0, DC, outer)
        both_hi = k.sb("both_hi", [P, DC, L], F32R, outer)
        both_lo = k.sb("both_lo", [P, DC, L], F32R, outer)
        with ExitStack() as top:
            u = k.sb("s5_u", [P, 4, L], F32, top)
            with ExitStack() as mid:
                q, sig, gate = (k.sb(n, [P, HG_HEADS, L], F32, mid) for n in ("hg_q", "hg_sig", "hg_gate"))
                v = k.sb("hg_v", [P, L // P, HG_HEADS * P], F32, mid)
                with ExitStack() as ctx:
                    vf = k.sb("hg_vf", [P, HG_HEADS, L], F32, ctx)
                    h_hi = k.sb("h2_hi", [P, DC, L], F32R, ctx)
                    h_lo = k.sb("h2_lo", [P, DC, L], F32R, ctx)
                    ring = WeightRing(k, "in2", d["w_in_2"], 0, DC, ctx)
                    norm_modulate(k, "mix2_norm", x, L, d["norm_mix_w_2"], mods[:, 0:DC, 0], h_hi, h_lo,
                                  scale=mods[:, DC:2 * DC, 0], ring=ring)
                    gemm(k, "in2", ring, [
                        Section(0, 4, act_out=activate(nc, q, ACT.Silu)),
                        Section(4, 8, act_out=activate(nc, sig, ACT.Sigmoid)),
                        Section(8, 12, act_out=activate(nc, vf, ACT.Copy)),
                        Section(12, 16, act_out=activate(nc, gate, ACT.Silu)),
                        Section(16, 20, act_out=activate(nc, u, ACT.Copy))], DC, h_hi, h_lo, L)
                    to_rows(k, "hg_v_rows", vf, v, HG_HEADS, L // P)
                k.recycle()
                key, b, y = (k.sb(n, [P, HG_HEADS, L], F32, mid) for n in ("hg_key", "hg_b", "hg_y"))
                scores = k.sb("hg_scores", [P, 16, P], F32, mid)
                masks = k.sb("hg_masks", [P, 8, P], U32, mid)
                logits = k.sb("hg_logits", [P, 2, HG_HEADS], F32, mid)
                lb, one_minus = (k.sb(n, [P, HG_HEADS], F32, mid) for n in ("hg_lb", "hg_1lb"))
                resets = k.sb("hg_resets", [P, L], F32, mid)
                gn = k.sb("hg_gn", [P, 1], F32, mid)
                ones = k.sb("ones_head2", [P, P], F32, mid)
                load_all(k, "hg", [(masks, d["hg_masks"]), (logits, d["hg_lower_bounds"]), (resets, d["resets"]),
                                   (gn, d["hg_gnorm_w"])])
                fill_constants(k, [(ones, 1.0 / P)])
                lower_bound(k, logits, lb, one_minus)
                forget_gates(k, q, sig, lb, one_minus, resets, b, key)
                chunk_scores(k, q, key, b, masks, scores)
                chunk_outputs(k, q, key, b, v, scores, y)
                head_norm(k, "hg_norm", y, HG_HEADS, 1, ones, False, lambda c: gn[:, 0:1], gate, both_hi, both_lo, 0)
            k.recycle()
            y = k.sb("s5_y", [P, 4, L], F32, top)
            s5_scan(k, u, k.mag, d["s5_d"], y)
            with ExitStack() as mid:
                y_hi = k.sb("s5_y_hi", [P, 4, L], F32R, mid)
                y_lo = k.sb("s5_y_lo", [P, 4, L], F32R, mid)
                glu = k.sb("s5_glu", [P, 4, L], F32, mid)
                bias = k.sb("s5_glu_b", [P, 4], F32, mid)
                ring = WeightRing(k, "s5_glu", d["s5_glu_w"], 0, 4, mid)
                split(k, "s5_y_split", y, y_hi, y_lo, 4, ring, (bias, d["s5_glu_b"]))
                gemm(k, "s5_glu", ring, [Section(0, 4, act_out=lambda e, n, ps: nc.scalar.activation(
                    glu[:, bass.ds(n, 1), :], ps, ACT.Sigmoid, bias=bias[:, bass.ds(n, 1)]))], 4, y_hi, y_lo, L)
                gate_and_split(k, "s5_gated", y, glu, both_hi, both_lo, 4, 4, out_ring)
        residual_gemm(k, "mix2_out", out_ring, both_hi, both_lo, x, mods[:, 2 * DC:3 * DC, 0])


def gate_and_split(k, name, y, g, hi, lo, chunks, first, ring):
    nc = k.nc
    gated, hi_ready = k.sem(f"{name}_gated"), k.sem(f"{name}_hi_ready")
    with nc.Block(no_gpsimd_drain=True) as block:

        @block.sync
        def _(sp):
            ring.start(sp)

        @block.vector
        def _(dve):
            for c in range(chunks):
                nc.vector.tensor_tensor(y[:, c, :], y[:, c, :], g[:, c, :], ALU.mult).then_inc(gated, 1)
            for c in range(chunks):
                dve.wait_ge(hi_ready, c + 1)
                nc.vector.tensor_tensor(lo[:, first + c, :], y[:, c, :], f32(hi[:, first + c, :]), ALU.subtract)

        @block.scalar
        def _(act):
            for c in range(chunks):
                act.wait_ge(gated, c + 1)
                nc.scalar.copy(hi[:, first + c, :], y[:, c, :]).then_inc(hi_ready, 1)




def first_mixer(k, x):
    nc, d = k.nc, k.dram
    mods, ada_w = k.mods1, d["ada_w"]

    def modulation_tiles(first, vector, cond):
        return ada_w[first:6 * DC], cond[:], lambda n: mods[:, bass.ds(first + n, 1), vector]

    def add_bias(first, last, vector):
        m = mods[:, first:last, vector]
        return nc.vector.tensor_tensor(m, m, k.ada_b[:, first:last], ALU.add)

    with ExitStack() as outer:
        g_pool = k.sb("g_pool", [P, DC, L], F32, outer)
        g_ret = k.sb("g_ret", [P, DC, L], F32, outer)
        with ExitStack() as mid:
            gate = k.sb("gate", [P, DC, L], F32, mid)
            pool_in = k.sb("pool_in", [P, 4, L], F32, mid)
            with ExitStack() as inner:
                q = k.sb("q", [P, RET_HEADS, L], F32, inner)
                kk = k.sb("kk", [P, RET_HEADS, L], F32, inner)
                v = k.sb("v", [P, L // P, D], F32, inner)
                with ExitStack() as ctx:
                    vf = k.sb("vf", [P, DC, L], F32, ctx)
                    with ExitStack() as act_ctx:
                        h_hi = k.sb("h_hi", [P, DC, L], F32R, act_ctx)
                        h_lo = k.sb("h_lo", [P, DC, L], F32R, act_ctx)
                        ring = WeightRing(k, "in", d["w_in"], 0, DC, act_ctx)
                        norm_modulate(k, "mix_norm", x, L, d["norm_mix_g"], mods[:, 0:DC, 0], h_hi, h_lo,
                                      scale=mods[:, DC:2 * DC, 0], ring=ring)

                        def rest(first):
                            return modulation_tiles(first, 0, k.cond)

                        def context(first):
                            return modulation_tiles(first, 1, k.cond_ctx)

                        gemm(k, "in", ring, [
                            Section(0, 4, act_out=activate(nc, pool_in, ACT.Copy), modulate=context(0)),
                            Section(4, 8, act_out=activate(nc, q, ACT.Copy), modulate=context(4)),
                            Section(8, 12, act_out=activate(nc, kk, ACT.Copy), modulate=context(8)),
                            Section(12, 16, act_out=activate(nc, vf[:, 0:4, :], ACT.Copy), modulate=context(12)),
                            Section(16, 20, act_out=activate(nc, vf[:, 4:8, :], ACT.Copy), modulate=rest(16)),
                            Section(20, 28, act_out=activate(nc, gate, ACT.Silu), modulate=rest(20)),
                            Section(28, 36, act_out=activate(nc, g_pool, ACT.Sigmoid), modulate=rest(28)),
                            Section(36, 44, act_out=activate(nc, g_ret, ACT.Sigmoid), modulate=rest(36))],
                            DC, h_hi, h_lo, L, at_end=lambda: (add_bias(0, 16, 1), add_bias(16, 44, 0)))
                    to_rows(k, "v_rows", vf, v, DC, L // P)
                k.recycle()
                kc = k.sb("kc", [P, RET_HEADS, LC], F32, inner)
                vc = k.sb("vc", [P, LC // P, D], F32, inner)
                with ExitStack() as ctx:
                    ctx_in = k.sb("ctx_in", [P, DC, LC], F32, ctx)
                    ctx_hi = k.sb("ctx_hi", [P, DC, LC], F32R, ctx)
                    ctx_lo = k.sb("ctx_lo", [P, DC, LC], F32R, ctx)
                    vcf = k.sb("vcf", [P, DC, LC], F32, ctx)
                    ring = WeightRing(k, "ctx", d["w_ctx"], 0, DC, ctx)
                    load_all(k, "ctx_in", [(ctx_in, d["ctx"])])
                    norm_modulate(k, "ctx_norm", ctx_in, LC, d["norm_mix_g"], mods[:, 0:DC, 1], ctx_hi, ctx_lo,
                                  scale=mods[:, DC:2 * DC, 1], ring=ring)
                    gemm(k, "ctx_kv", ring, [
                        Section(0, 4, act_out=lambda e, n, ps: nc.scalar.mul(kc[:, bass.ds(n, 1), :], ps, K_SCALE),
                                modulate=modulation_tiles(44, 0, k.cond)),
                        Section(4, 12, act_out=activate(nc, vcf, ACT.Copy))],
                        DC, ctx_hi, ctx_lo, LC, at_end=lambda: add_bias(44, 48, 0))
                    to_rows(k, "ctx_v_rows", vcf, vc, DC, LC // P)
                y = k.sb("ret_y", [P, DC, L], F32, inner)
                with ExitStack() as ctx:
                    decay = k.sb("decay", [P, 2 * RET_HEADS], F32, ctx)
                    rel = k.sb("rel", [P, STRIP], F32, ctx)
                    crel = k.sb("crel", [P, CSTRIP], F32, ctx)
                    loaded = k.sem("decay_loaded")
                    with ExitStack() as c2:
                        table = {n: k.sb(f"rope_{n}", [P, L], F32, c2) for n in ("cos", "sin", "kcos", "ksin")}
                        load_all(k, "rope", [(t, d[f"rope_{n}"]) for n, t in table.items()],
                                 [(decay, d["ret_decay"]), (rel, d["rel"]), (crel, d["crel"])], loaded)
                        rope(k, "rope_q", q, table["cos"][:], table["sin"][:], RET_HEADS)
                        rope(k, "rope_k", kk, table["kcos"][:], table["ksin"][:], RET_HEADS)
                    strip = k.sb("strip", [P, RET_HEADS, STRIP], F32, ctx)
                    cstrip = k.sb("cstrip", [P, RET_HEADS, CSTRIP], F32, ctx)
                    tables = DecayTables(k, decay, rel, crel, strip, cstrip, loaded, ctx)
                    retention(k, q, kk, kc, v, vc, tables, y)
                k.recycle()
                with ExitStack() as ctx:
                    ng = k.sb("ret_ng", [P, DC], F32, ctx)
                    ones = k.sb("ones_head", [P, P], F32, ctx)
                    r_hi = k.sb("r_hi", [P, DC, L], F32R, ctx)
                    r_lo = k.sb("r_lo", [P, DC, L], F32R, ctx)
                    ring = WeightRing(k, "ret_out", d["ret_out"], 0, DC, ctx)
                    fill_constants(k, [(ones, 1.0 / (2 * P))])
                    load_all(k, "ret_ng", [(ng, d["ret_norm_g"])])
                    with ExitStack() as c2:
                        head_norm(k, "ret_norm", y, RET_HEADS, 2, ones, True, lambda c: ng[:, c:c + 1], gate,
                                  r_hi, r_lo, 0, ring, v[:].rearrange("p a (b t) -> p (a b) t", t=L))
                    gemm(k, "ret_out", ring, [Section(0, DC, dve_out=lambda e, n, ps: nc.vector.tensor_tensor(
                        g_ret[:, bass.ds(n, 1), :], ps, g_ret[:, bass.ds(n, 1), :], ALU.mult))], DC, r_hi, r_lo, L)
            with ExitStack() as ctx:
                inv = k.sb("inv_count", [P, 4, L], F32, ctx)
                pw = k.sb("pool_w", [P, 4, P], F32, ctx)
                pg = k.sb("pool_gain", [P, 4], F32, ctx)
                p_hi = k.sb("p_hi", [P, 4, L], F32R, ctx)
                p_lo = k.sb("p_lo", [P, 4, L], F32R, ctx)
                ring = WeightRing(k, "pool_out", d["pool_out"], 0, 4, ctx)
                load_all(k, "pool", [(inv, d["inv_count"]), (pw, d["pool_w"]), (pg, d["pool_scale"])])
                pooling(k, pool_in, inv, pw, pg, p_hi, p_lo, ring)
                gemm(k, "pool_out", ring, [Section(0, DC, dve_out=lambda e, n, ps: nc.vector.tensor_tensor(
                    g_pool[:, bass.ds(n, 1), :], ps, g_pool[:, bass.ds(n, 1), :], ALU.mult))], 4, p_hi, p_lo, L)
        with ExitStack() as ctx:
            m_hi = k.sb("m_hi", [P, DC, L], F32R, ctx)
            m_lo = k.sb("m_lo", [P, DC, L], F32R, ctx)
            ring = WeightRing(k, "mix_out", d["w_out"], 0, DC, ctx)
            add_into(k, "merge", g_pool, g_ret, DC)
            split(k, "merged", g_pool, m_hi, m_lo, DC, ring)
            residual_gemm(k, "mix_out", ring, m_hi, m_lo, x, mods[:, 2 * DC:3 * DC, 0])


def add_into(k, name, a, b, chunks):
    nc = k.nc
    with nc.Block(no_gpsimd_drain=True) as block:

        @block.vector
        def _(dve):
            for c in range(chunks):
                nc.vector.tensor_tensor(a[:, c, :], a[:, c, :], b[:, c, :], ALU.add)


def residual_gemm(k, name, ring, hi, lo, x, gate):
    nc = k.nc
    gemm(k, name, ring, [Section(0, DC, dve_out=lambda e, n, ps: nc.vector.scalar_tensor_tensor(
        x[:, bass.ds(n, 1), :], ps, gate[:, bass.ds(n, 1)], x[:, bass.ds(n, 1), :], ALU.mult, ALU.add))], DC, hi, lo, L)


def program(nc, dram, out):
    with ExitStack() as ctx:
        k = Core(nc, dram, ctx)
        d = dram
        x = k.sb("x", [P, DC, L])
        k.mods1 = k.sb("mods1", [P, 6 * DC, 2])
        k.mods2 = k.sb("mods2", [P, 6 * DC, 1])
        k.ident = k.sb("ident", [P, P])
        k.ones_model = k.sb("ones_model", [P, P])
        k.iota = k.sb("iota", [P, NKEYS])
        k.mag, k.turn_hi, k.turn_lo, k.coef_re, k.minus_coef_im = (
            k.sb(f"s5_{n}", [P, S5_TILES]) for n in ("mag", "turn_hi", "turn_lo", "coef_re", "minus_coef_im"))
        k.table = nc.dram_tensor("gate_table", [NKEYS, NKEYS, PAD + L], F32).ap()
        k.acts = nc.dram_tensor("expert_acts", [NKEYS, NKEYS, L], F32).ap()
        k.s5_out = nc.dram_tensor("s5_outputs", [S5_TILES, P, 2, P], F32).ap()
        k.s5_table = nc.dram_tensor("s5_rotations", [S5_TILES, P, 2, L], F32).ap()

        def third(m, j):
            return m[:, j * DC:(j + 1) * DC, 0]

        with ExitStack() as mixer:
            k.cond, k.cond_ctx = (k.sb(n, [P, D], F32, mixer) for n in ("cond", "cond_ctx"))
            k.ada_b = k.sb("ada_b", [P, 6 * DC], F32, mixer)
            k.swap = k.sb("swap", [P, P], F32, mixer)
            with ExitStack() as begin:
                a_re, a_im, log_dt = (k.sb(f"s5_{n}", [P, S5_TILES], F32, begin) for n in ("a_re", "a_im", "log_dt"))
                start(k, [(x, d["x"]), (k.ident, d["ident"]), (k.swap, d["swap"]), (k.iota, d["iota"]),
                          (k.ada_b, d["ada_b"]), (a_re, d["s5_a_re"]), (a_im, d["s5_a_im"]), (log_dt, d["s5_log_dt"])],
                      [(k.cond, d["cond"]), (k.cond_ctx, d["cond_ctx"])],
                      d["ada_w"], k.ada_b, k.mods1, 2 * DC)
                s5_parameters(k, a_re, a_im, log_dt, k.mag, k.turn_hi, k.turn_lo, k.coef_re, k.minus_coef_im)
            first_mixer(k, x)
        peer(k, "peer1", x, d["norm_ffn_g"], third(k.mods1, 3), third(k.mods1, 4), third(k.mods1, 5),
             d["peer_wq"], d["peer_keys"], d["peer_u"], d["peer_v"], BesideOutputs)
        final_norm(k, "norm1", x, d["final_g"])
        k.recycle()
        second_mixer(k, x)
        peer(k, "peer2", x, d["norm_ffn_w_2"], third(k.mods2, 3), third(k.mods2, 4), third(k.mods2, 5),
             d["peer_wq_2"], d["peer_keys_2"], d["peer_u_2"], d["peer_v_2"])
        final_norm(k, "norm2", x, d["final_norm_w_2"])
        store(k, x, out)


def final_norm(k, name, x, gain):
    norm_modulate(k, name, x, L, gain, None, None, None, None, plain=x)


def store(k, x, out):
    nc = k.nc
    stored = k.sem("stored")
    with nc.Block(no_gpsimd_drain=True) as block:

        @block.sync
        def _(sp):
            sp.dma_start(out, x[:]).then_inc(stored, 16)
            sp.wait_ge(stored, 16)




def by_feature(a):
    t, f = a.shape
    return a.reshape(t, f // P, P).transpose(2, 1, 0)


def columns(a):
    return a.reshape(-1, P).T


def slabs(w):
    kk, n = w.shape
    return w.reshape(kk // P, P, n // P, P).transpose(2, 1, 0, 3)


def rows(w):
    return w.T.reshape(w.shape[1] // P, P, w.shape[0])


def shape_constants():
    f = np.float32
    c = {"ident": np.eye(P, dtype=f)}
    swap = np.zeros((P, P), f)
    swap[(np.arange(P) + P // 2) % P, np.arange(P)] = 1
    c["swap"] = swap
    grid = 64
    quarter = RET_DK // 4
    inv = (np.float32(10000.0) ** (-np.arange(quarter, dtype=f) / f(quarter))).astype(f)
    t = np.arange(L)
    row, col = (t // grid).astype(f), (t % grid).astype(f)
    ang = np.concatenate([row[:, None] * inv, col[:, None] * inv], axis=-1).astype(f)
    cos, sin = np.cos(ang).T.astype(f), np.sin(ang).T.astype(f)
    c["rope_cos"], c["rope_sin"] = np.concatenate([cos, cos]), np.concatenate([-sin, sin])
    c["rope_kcos"], c["rope_ksin"] = c["rope_cos"] * f(K_SCALE), c["rope_sin"] * f(K_SCALE)
    s = np.arange(P)
    c["rel"] = (np.arange(STRIP)[None] - 3 * P - s[:, None]).astype(f)
    c["crel"] = (np.arange(CSTRIP)[None] + P - s[:, None]).astype(f)
    counts = [np.clip(t + w - w // 2, 0, L) - np.clip(t - w // 2, 0, L) for w in POOL_WINDOWS]
    c["inv_count"] = np.broadcast_to(np.stack([f(1) / n.astype(f) for n in counts]), (P, 4, L))
    c["resets"] = np.broadcast_to((t % P != 0).astype(f), (P, L))
    c["time"] = np.broadcast_to(t.astype(f), (P, L))
    masks = []
    for m in (64, 32, 16, 8, 4, 2, 1):
        half, blk = (s // m) % 2, s // (2 * m)
        masks.append((blk[:, None] == blk[None]) & (half[:, None] == 0) & (half[None] == 1))
    masks.append(s[:, None] == s[None])
    c["hg_masks"] = np.stack(masks).transpose(1, 0, 2).astype(np.uint32)
    c["iota"] = np.broadcast_to(np.arange(NKEYS, dtype=f), (P, NKEYS))
    return c


def layout(v):
    w_in = slabs(v["w_in"][0])
    a = {
        "x": by_feature(v["x"][0]),
        "ctx": by_feature(v["ctx"][0]),
        "cond": np.broadcast_to(v["c"][0], (P, D)), "cond_ctx": np.broadcast_to(v["c_ctx"], (P, D)),
        "ada_w": rows(v["ada_w"][0]), "ada_b": columns(v["ada_b"][0]),
        "norm_mix_g": columns(v["norm_mix_g"][0]), "norm_ffn_g": columns(v["norm_ffn_g"][0]),
        "w_in": w_in, "w_ctx": w_in[8:20],
        "pool_w": v["pool_w"][0].transpose(1, 0, 2), "pool_scale": columns(v["pool_scale"][0]),
        "pool_out": slabs(v["pool_out"][0]),
        "ret_decay": np.broadcast_to(v["ret_decay"][0].reshape(1, -1), (P, 2 * RET_HEADS)),
        "ret_norm_g": columns(v["ret_norm_g"][0]),
        "ret_out": slabs(v["ret_out"][0]), "w_out": slabs(v["w_out"][0]),
    }
    def states(a):
        return a.reshape(S5_TILES, P).T

    def s5_blocks(w):
        out = np.zeros((S5_TILES, P, P), w.dtype)
        for g in range(w.shape[0]):
            r, c = (g % 2) * 64, (g % 8) * 16
            out[g // 2, r:r + 64, c:c + 16] = w[g]
        return out

    def experts(u):
        return u.reshape(NKEYS, NKEYS, DC, P).transpose(0, 3, 2, 1)

    a.update({
        "cond_2": np.broadcast_to(v["c_2"][0], (P, D)),
        "ada_w_2": rows(v["ada_w_2"][0]), "ada_b_2": columns(v["ada_b_2"][0]),
        "norm_mix_w_2": columns(v["norm_mix_w_2"][0]), "norm_ffn_w_2": columns(v["norm_ffn_w_2"][0]),
        "w_in_2": slabs(v["w_in_2"][0]), "w_out_2": slabs(v["w_out_2"][0]),
        "hg_lower_bounds": v["hg_lower_bounds_2"].reshape(2, HG_HEADS, P).transpose(2, 0, 1),
        "hg_gnorm_w": columns(v["hg_gnorm_w_2"][0]),
        "s5_a_re": states(v["s5_a_re_2"][0]), "s5_a_im": states(v["s5_a_im_2"][0]),
        "s5_log_dt": states(np.repeat(v["s5_log_dt_2"][0][:, None], 64, axis=1)),
        "s5_b": np.stack([s5_blocks(v["s5_b_re_2"][0]), s5_blocks(v["s5_b_im_2"][0])]).transpose(1, 3, 0, 2),
        "s5_c": np.stack([s5_blocks(v["s5_c_re_2"][0].transpose(0, 2, 1)),
                          s5_blocks(v["s5_c_im_2"][0].transpose(0, 2, 1))]).transpose(1, 2, 0, 3),
        "s5_d": columns(v["s5_d_2"][0]), "s5_glu_w": slabs(v["s5_glu_w_2"][0]), "s5_glu_b": columns(v["s5_glu_b_2"][0]),
        "peer_wq_2": slabs(v["peer_wq_2"][0]),
        "peer_keys_2": np.stack([v["peer_keys1_2"][0], v["peer_keys2_2"][0]] * HEADS).transpose(2, 0, 1),
        "peer_u_2": experts(v["peer_u_2"][0]), "peer_v_2": v["peer_v_2"][0].reshape(NKEYS, NKEYS, D),
        "final_g": columns(v["final_g"]), "final_norm_w_2": columns(v["final_norm_w_2"]),
        "peer_wq": slabs(v["peer_wq"][0]),
        "peer_keys": v["peer_keys"][0].reshape(2 * HEADS, NKEYS, P).transpose(2, 0, 1),
        "peer_u": experts(v["peer_u"][0]), "peer_v": v["peer_v"][0].reshape(NKEYS, NKEYS, D),
    })
    a.update(shape_constants())
    return a


def kernel(**inputs):
    import concourse.bacc as bacc
    from concourse.bass_utils import run_bass_kernel_spmd

    nc = bacc.Bacc("TRN2", target_bir_lowering=False, num_devices=1)
    arrays = {f"in_{n}": np.ascontiguousarray(a) for n, a in layout({n: np.asarray(a) for n, a in inputs.items()}).items()}
    dram = {n[3:]: nc.dram_tensor(n, a.shape, mybir.dt.from_np(a.dtype), kind="ExternalInput").ap()
            for n, a in arrays.items()}
    out = nc.dram_tensor("out", (P, DC, L), F32, kind="ExternalOutput").ap()
    program(nc, dram, out)
    got = run_bass_kernel_spmd(nc, [arrays], core_ids=[0]).results[0]["out"]
    return np.ascontiguousarray(np.asarray(got).transpose(2, 1, 0).reshape(1, L, D))
```
